# Optimizing a Trainium2 kernel written in Bass

```python
import math
import jax, jax.numpy as jnp
from jax import lax
import numpy as np

D_MODEL = 1024
BATCH = 1
SEQ = 2048
DEPTH = 1
DEC_BATCH = 8
DEC_SEQ = 1
PAST_LEN = 512
PAGE_SIZE = 128

PLE_DIM = 256
LRU_WIDTH = 512
LRU_BLOCKS = 8
LRU_BLOCK = LRU_WIDTH // LRU_BLOCKS
CONV_WIDTH = 4
ATT_HEADS = 4
ATT_HD = 64
ATT_WIDTH = ATT_HEADS * 2 * ATT_HD
MIX_WIDTH = LRU_WIDTH + ATT_WIDTH
IN_WIDTH = 2 * LRU_WIDTH + 3 * ATT_WIDTH
SPLITS = (LRU_WIDTH, 2 * LRU_WIDTH, 2 * LRU_WIDTH + ATT_WIDTH, 2 * LRU_WIDTH + 2 * ATT_WIDTH)
ROT_DIM = ATT_HD // 4
ROPE_THETA = 500000.0
Q_BLOCK = 128
D_FF = -(-8 * D_MODEL // (3 * 256)) * 256
NEG_INF = -1e30

kernel_name = 'hymba_rglru_diffattn_decode_step'

def _rmsnorm(x, g, eps=1e-6):
    xf = x.astype(jnp.float32)
    y = xf * lax.rsqrt(jnp.mean(xf * xf, axis=-1, keepdims=True) + eps)
    return (y * g.astype(jnp.float32)).astype(x.dtype)

def _rope(t, pos):
    half = ROT_DIM // 2
    inv = ROPE_THETA ** (-jnp.arange(0, ROT_DIM, 2, dtype=jnp.float32) / ROT_DIM)
    ang = pos.astype(jnp.float32)[:, None] * inv[None, :]
    cos = jnp.cos(ang)[None, :, None, :]
    sin = jnp.sin(ang)[None, :, None, :]
    tf = t.astype(jnp.float32)
    t1 = tf[..., :half]
    t2 = tf[..., half:ROT_DIM]
    out = jnp.concatenate([t1 * cos - t2 * sin, t2 * cos + t1 * sin, tf[..., ROT_DIM:]], axis=-1)
    return out.astype(t.dtype)

def _lin_combine(c1, c2):
    a1, b1 = c1
    a2, b2 = c2
    return a1 * a2, a2 * b1 + b2

def _diff_attend(q1, q2, k1, k2, v, q_pos, k_pos, lam):
    scale = ATT_HD ** -0.5
    mask = k_pos[None, :] <= q_pos[:, None]

    def probs(q, k):
        s = jnp.einsum('bqhd,bkhd->bhqk', q.astype(jnp.float32), k.astype(jnp.float32)) * scale
        return jax.nn.softmax(jnp.where(mask, s, NEG_INF), axis=-1)

    w = probs(q1, k1) - lam * probs(q2, k2)
    return jnp.einsum('bhqk,bkhe->bqhe', w, v.astype(jnp.float32))

def _attend(q1, q2, k1, k2, v, q_pos, k_pos, lam):
    b, sq = q1.shape[0], q1.shape[1]
    if sq <= Q_BLOCK or sq % Q_BLOCK != 0:
        return _diff_attend(q1, q2, k1, k2, v, q_pos, k_pos, lam)
    nb = sq // Q_BLOCK

    def split(t):
        return jnp.moveaxis(t.reshape((b, nb, Q_BLOCK) + t.shape[2:]), 1, 0)

    def one(args):
        qa, qb, qp = args
        return _diff_attend(qa, qb, k1, k2, v, qp, k_pos, lam)

    out = lax.map(one, (split(q1), split(q2), q_pos.reshape(nb, Q_BLOCK)))
    return jnp.moveaxis(out, 0, 1).reshape((b, sq) + out.shape[3:])

def _layer(x, p, conv_prev, h_prev, k_past, v_past, lw, lam_init):
    b, s, _ = x.shape
    past = 0 if k_past is None else k_past.shape[1]
    q_pos = past + jnp.arange(s, dtype=jnp.int32)

    h = _rmsnorm(x, lw['norm_pre_mix'])
    u = h @ lw['w_in']
    xl, gl, q, k, v = jnp.split(u, SPLITS, axis=-1)

    xpad = jnp.concatenate([conv_prev.astype(xl.dtype), xl], axis=1)
    xc = lw['conv_b'] + xpad[:, 0:s] * lw['conv_w'][0]
    for j in range(1, CONV_WIDTH):
        xc = xc + xpad[:, j:j + s] * lw['conv_w'][j]
    new_conv = xpad[:, -(CONV_WIDTH - 1):]
    xb = xc.reshape(b, s, LRU_BLOCKS, LRU_BLOCK)
    r = jax.nn.sigmoid(jnp.einsum('bsni,nij->bsnj', xb, lw['lru_w_a']) + lw['lru_b_a']).reshape(b, s, LRU_WIDTH)
    ig = jax.nn.sigmoid(jnp.einsum('bsni,nij->bsnj', xb, lw['lru_w_x']) + lw['lru_b_x']).reshape(b, s, LRU_WIDTH)
    log_a = -8.0 * r.astype(jnp.float32) * jax.nn.softplus(-lw['lru_L'].astype(jnp.float32))
    a = jnp.exp(log_a)
    bt = jnp.sqrt(-jnp.expm1(2.0 * log_a)) * (ig * xc).astype(jnp.float32)
    bt = bt.at[:, 0].add(a[:, 0] * h_prev.astype(jnp.float32))
    _, hs = lax.associative_scan(_lin_combine, (a, bt), axis=1)
    lru_out = hs.astype(x.dtype) * jax.nn.gelu(gl)
    new_h = hs[:, -1].astype(x.dtype)

    q = q.reshape(b, s, ATT_HEADS, 2, ATT_HD)
    k = k.reshape(b, s, ATT_HEADS, 2, ATT_HD)
    q1 = _rope(q[..., 0, :], q_pos)
    q2 = _rope(q[..., 1, :], q_pos)
    k_new = jnp.concatenate([_rope(k[..., 0, :], q_pos), _rope(k[..., 1, :], q_pos)], axis=-1)
    v_new = v.reshape(b, s, ATT_HEADS, 2 * ATT_HD)
    if k_past is None:
        k_all, v_all, k_pos = k_new, v_new, q_pos
    else:
        k_all = jnp.concatenate([k_past.astype(k_new.dtype), k_new], axis=1)
        v_all = jnp.concatenate([v_past.astype(v_new.dtype), v_new], axis=1)
        k_pos = jnp.arange(past + s, dtype=jnp.int32)
    f32 = jnp.float32
    lam = (jnp.exp(jnp.sum(lw['lambda_q1'].astype(f32) * lw['lambda_k1'].astype(f32)))
           - jnp.exp(jnp.sum(lw['lambda_q2'].astype(f32) * lw['lambda_k2'].astype(f32))) + lam_init)
    o = _attend(q1, q2, k_all[..., :ATT_HD], k_all[..., ATT_HD:], v_all, q_pos, k_pos, lam)
    o = _rmsnorm(o, lw['subln_g'], eps=1e-5) * (1.0 - lam_init)
    att_out = o.reshape(b, s, ATT_WIDTH).astype(x.dtype)

    mix = jnp.concatenate([lru_out, att_out], axis=-1) @ lw['w_out']
    x = x + _rmsnorm(mix, lw['norm_post_mix'])

    h = _rmsnorm(x, lw['norm_pre_ffn'])
    f = (jax.nn.silu(h @ lw['ffn_w_gate']) * (h @ lw['ffn_w_up'])) @ lw['ffn_w_down']
    x = x + _rmsnorm(f, lw['norm_post_ffn'])

    gate = jax.nn.sigmoid(x @ lw['ple_w_gate'])
    x = x + _rmsnorm(gate * (p @ lw['ple_w_proj']), lw['ple_norm'])
    return x, k_new, v_new, new_conv, new_h

def setup_inputs(seed: int = 0) -> dict:
    key = jax.random.key(seed)
    ks = jax.random.split(key, 40)
    f32 = jnp.float32
    n_pages = PAST_LEN // PAGE_SIZE
    n_used = DEC_BATCH * n_pages
    n_phys = n_used + max(1, n_used // 4)

    def nrm(k, shape, scale):
        return jax.random.normal(k, shape, f32) * scale

    def gain(k, shape):
        return 1.0 + 0.05 * jax.random.normal(k, shape, f32)

    page_table = jax.random.permutation(ks[0], n_phys)[:n_used].reshape(DEC_BATCH, n_pages).astype(jnp.int32)
    a0 = jax.random.uniform(ks[1], (DEPTH, LRU_WIDTH), f32, 0.9, 0.999)
    lru_L = jnp.log(a0) - jnp.log1p(-a0)
    return {
        'x_prompt': nrm(ks[2], (BATCH, SEQ, D_MODEL), 1.0),
        'x_sample': nrm(ks[3], (DEC_BATCH, DEC_SEQ, D_MODEL), 1.0),
        'cache_k': nrm(ks[4], (DEPTH, n_phys, PAGE_SIZE, ATT_HEADS, 2 * ATT_HD), 1.0),
        'cache_v': nrm(ks[5], (DEPTH, n_phys, PAGE_SIZE, ATT_HEADS, 2 * ATT_HD), 1.0),
        'state_conv': nrm(ks[6], (DEPTH, DEC_BATCH, CONV_WIDTH - 1, LRU_WIDTH), 1.0),
        'state_h': nrm(ks[7], (DEPTH, DEC_BATCH, LRU_WIDTH), 0.5),
        'page_table': page_table,
        'p_prompt': nrm(ks[8], (DEPTH, BATCH, SEQ, PLE_DIM), 1.0),
        'p_sample': nrm(ks[9], (DEPTH, DEC_BATCH, DEC_SEQ, PLE_DIM), 1.0),
        'norm_pre_mix': gain(ks[10], (DEPTH, D_MODEL)),
        'w_in': nrm(ks[11], (DEPTH, D_MODEL, IN_WIDTH), D_MODEL ** -0.5),
        'conv_w': nrm(ks[12], (DEPTH, CONV_WIDTH, LRU_WIDTH), CONV_WIDTH ** -0.5),
        'conv_b': nrm(ks[13], (DEPTH, LRU_WIDTH), 0.02),
        'lru_w_a': nrm(ks[14], (DEPTH, LRU_BLOCKS, LRU_BLOCK, LRU_BLOCK), LRU_BLOCK ** -0.5),
        'lru_b_a': nrm(ks[15], (DEPTH, LRU_BLOCKS, LRU_BLOCK), 0.02),
        'lru_w_x': nrm(ks[16], (DEPTH, LRU_BLOCKS, LRU_BLOCK, LRU_BLOCK), LRU_BLOCK ** -0.5),
        'lru_b_x': nrm(ks[17], (DEPTH, LRU_BLOCKS, LRU_BLOCK), 0.02),
        'lru_L': lru_L,
        'lambda_q1': nrm(ks[18], (DEPTH, ATT_HD), 0.1),
        'lambda_k1': nrm(ks[19], (DEPTH, ATT_HD), 0.1),
        'lambda_q2': nrm(ks[20], (DEPTH, ATT_HD), 0.1),
        'lambda_k2': nrm(ks[21], (DEPTH, ATT_HD), 0.1),
        'subln_g': gain(ks[22], (DEPTH, 2 * ATT_HD)),
        'w_out': nrm(ks[23], (DEPTH, MIX_WIDTH, D_MODEL), MIX_WIDTH ** -0.5),
        'norm_post_mix': gain(ks[24], (DEPTH, D_MODEL)),
        'norm_pre_ffn': gain(ks[25], (DEPTH, D_MODEL)),
        'ffn_w_gate': nrm(ks[26], (DEPTH, D_MODEL, D_FF), D_MODEL ** -0.5),
        'ffn_w_up': nrm(ks[27], (DEPTH, D_MODEL, D_FF), D_MODEL ** -0.5),
        'ffn_w_down': nrm(ks[28], (DEPTH, D_FF, D_MODEL), D_FF ** -0.5),
        'norm_post_ffn': gain(ks[29], (DEPTH, D_MODEL)),
        'ple_w_gate': nrm(ks[30], (DEPTH, D_MODEL, D_MODEL), D_MODEL ** -0.5),
        'ple_w_proj': nrm(ks[31], (DEPTH, PLE_DIM, D_MODEL), PLE_DIM ** -0.5),
        'ple_norm': gain(ks[32], (DEPTH, D_MODEL)),
    }

def reference(x_prompt, x_sample, cache_k, cache_v, state_conv, state_h, page_table, p_prompt, p_sample,
              norm_pre_mix, w_in, conv_w, conv_b, lru_w_a, lru_b_a, lru_w_x, lru_b_x, lru_L,
              lambda_q1, lambda_k1, lambda_q2, lambda_k2, subln_g, w_out, norm_post_mix,
              norm_pre_ffn, ffn_w_gate, ffn_w_up, ffn_w_down, norm_post_ffn,
              ple_w_gate, ple_w_proj, ple_norm):
    n_pages = page_table.shape[1]
    xp, xs = x_prompt, x_sample
    kps, vps, cps, hps, kss, vss, css, hss = [], [], [], [], [], [], [], []
    for i in range(DEPTH):
        lw = {
            'norm_pre_mix': norm_pre_mix[i], 'w_in': w_in[i], 'conv_w': conv_w[i], 'conv_b': conv_b[i],
            'lru_w_a': lru_w_a[i], 'lru_b_a': lru_b_a[i], 'lru_w_x': lru_w_x[i], 'lru_b_x': lru_b_x[i],
            'lru_L': lru_L[i], 'lambda_q1': lambda_q1[i], 'lambda_k1': lambda_k1[i],
            'lambda_q2': lambda_q2[i], 'lambda_k2': lambda_k2[i], 'subln_g': subln_g[i],
            'w_out': w_out[i], 'norm_post_mix': norm_post_mix[i], 'norm_pre_ffn': norm_pre_ffn[i],
            'ffn_w_gate': ffn_w_gate[i], 'ffn_w_up': ffn_w_up[i], 'ffn_w_down': ffn_w_down[i],
            'norm_post_ffn': norm_post_ffn[i], 'ple_w_gate': ple_w_gate[i], 'ple_w_proj': ple_w_proj[i],
            'ple_norm': ple_norm[i],
        }
        lam_init = 0.8 - 0.6 * math.exp(-0.3 * i)
        conv0 = jnp.zeros((xp.shape[0], CONV_WIDTH - 1, LRU_WIDTH), xp.dtype)
        h0 = jnp.zeros((xp.shape[0], LRU_WIDTH), jnp.float32)
        xp, kp, vp, cp, hp = _layer(xp, p_prompt[i], conv0, h0, None, None, lw, lam_init)
        db = xs.shape[0]
        k_past = cache_k[i][page_table].reshape(db, n_pages * PAGE_SIZE, ATT_HEADS, 2 * ATT_HD)
        v_past = cache_v[i][page_table].reshape(db, n_pages * PAGE_SIZE, ATT_HEADS, 2 * ATT_HD)
        xs, ksm, vsm, csm, hsm = _layer(xs, p_sample[i], state_conv[i], state_h[i], k_past, v_past, lw, lam_init)
        kps.append(kp); vps.append(vp); cps.append(cp); hps.append(hp)
        kss.append(ksm); vss.append(vsm); css.append(csm); hss.append(hsm)
    return (xp, xs, jnp.stack(kps), jnp.stack(vps), jnp.stack(cps), jnp.stack(hps),
            jnp.stack(kss), jnp.stack(vss), jnp.stack(css), jnp.stack(hss))


_drawn_inputs = setup_inputs


def setup_inputs(seed=0):
    import zlib

    import numpy as np

    out = dict(_drawn_inputs(seed))
    spreads = {}
    factors = {'lru_b_a': 8.0, 'lru_b_x': 8.0}
    for name, (base, spread) in spreads.items():
        noise = np.random.default_rng([zlib.crc32(name.encode()), seed]).standard_normal(out[name].shape)
        drawn = base * np.exp(spread * noise) if base else spread * noise
        out[name] = __import__('jax').numpy.asarray(drawn.astype(out[name].dtype))
    for name, factor in factors.items():
        out[name] = (out[name] * factor).astype(out[name].dtype)
    return out
```

```python
from contextlib import ExitStack

import numpy as np

import concourse.bass as bass
from concourse import mybir

F32 = mybir.dt.float32
F32R = mybir.dt.float32r
I32 = mybir.dt.int32
ALU = mybir.AluOpType
ACT = mybir.ActivationFunctionType
AX = mybir.AxisListType.X

P = 128
D = 1024
SEQ = 2048
GROUP = 512
GROUPS = SEQ // GROUP
TILES = GROUP // P
NS = 8
WIDE = GROUP + NS
KD = D // P
LRU = 512
LC = LRU // P
TAPS = 4
HEADS = 4
HD = 64
COMP = 2 * HEADS
ROT = HD // 4
HALF = ROT // 2
PAGE = 128
PAGES = 4
FF = 2816
FB = FF // P
PLE = 256
EPS = 1e-6
EPS_SUBLN = 1e-5
LAM_INIT = 0.2
QSCALE = HD ** -0.5

PRODUCTS = ((0, 0), (0, 1), (1, 0))


class Chain:

    def __init__(self, eng, sem, base=0):
        self.eng, self.sem, self.base, self.n = eng, sem, base, 0

    def __call__(self, instruction):
        self.n += 1
        instruction.then_inc(self.sem, 1)
        self.eng.wait_ge(self.sem, self.base + self.n)


def group_tiles(last):
    return [(t, t * P, P) for t in range(TILES)] + ([(TILES, GROUP, NS)] if last else [])


def project(nc, io, sems):
    ctx = ExitStack()
    sb = lambda name, shape, dt=F32: ctx.enter_context(nc.sbuf_tensor(name, shape, dt))
    sem = lambda name: sems.enter_context(nc.semaphore(name))
    CH = 10
    SLOT = (0, 1, 2, 3, 0, 1, 2, 3, 1, 2)
    FREED = [max([b + 1 - (CH if b >= c else 0) for b in range(CH) if SLOT[b] == SLOT[c] and b != c and b < c] or
                 [max(b for b in range(CH) if SLOT[b] == SLOT[c]) + 1 - CH]) for c in range(CH)]
    RAW = 2
    AHEAD = 2
    JOBS = 20
    with ctx:
        ident = sb("a_ident", [P, P])
        gain = sb("a_gain", [P, D])
        convw = sb("a_convw", [P, LC, TAPS])
        convb = sb("a_convb", [P, LC])
        gate_b = sb("a_gate_b", [P, 2, LC])
        gate_w = sb("a_gate_w", [P, 2, LC, P])
        lru_l = sb("a_lru_l", [P, LC])
        sp_t = sb("a_sp_t", [P, 6, LC])
        sp8 = sb("a_sp8", [P, LC])
        nsp8 = sb("a_nsp8", [P, LC])
        eps = sb("a_eps", [P, 1])
        rope = sb("a_rope", [P, SEQ // P, 2, HALF])
        rope_s = sb("a_rope_s", [NS, 2, HALF])
        x = sb("a_x", [P, 2, D])
        junk = sb("a_junk", [P, D], mybir.dt.bfloat16)
        ssq = sb("a_ssq", [P, TILES + 1])
        rstd = sb("a_rstd", [P, TILES + 1])
        hn = sb("a_hn", [P, 2, D])
        hT = sb("a_hT", [P, 2, KD, WIDE], F32R)
        raw = sb("a_raw", [P, RAW, 2048])
        w = sb("a_w", [P, max(SLOT) + 1, 2, 2048], F32R)
        xpad = sb("a_xpad", [P, LC, TAPS - 1 + GROUP])
        xc = sb("a_xc", [P, LC, GROUP])
        gg = sb("a_gg", [P, LC, GROUP])
        ri = sb("a_ri", [P, 2, GROUP])
        u = sb("a_u", [P, GROUP])
        aa = sb("a_aa", [P, 2, GROUP])
        rec = sb("a_rec", [P, GROUP])
        qq = sb("a_qq", [P, GROUP])
        igx = sb("a_igx", [P, 2, GROUP])
        sq = sb("a_sq", [P, GROUP])
        hs = sb("a_hs", [P, 2, GROUP])
        hlast = sb("a_hlast", [P, LC])
        lo_out = sb("a_lo_out", [P, 2, GROUP])
        rows = sb("a_rows", [P, 3, 512])
        rt = sb("a_rt", [P, 4, COMP, HALF])
        s_xl = sb("a_s_xl", [P, LC, NS])
        s_gg = sb("a_s_gg", [P, LC, NS])
        s_conv = sb("a_s_conv", [P, LC, TAPS - 1, NS])
        s_h = sb("a_s_h", [P, LC, NS])
        s_w = sb("a_s_w", [P, 12, LC, NS])
        s_ri = sb("a_s_ri", [P, 2, LC, NS])
        banks = [ctx.enter_context(nc.psum_tensor(f"a_bank{n}", [P, 512], F32)) for n in range(8)]
        TB = banks[0:2]
        ACC = banks[2:6]
        SB_, GB = banks[6], (banks[7], banks[0])
        consts_in = sem("a_consts_in")
        ready0 = sem("a_memsets")
        eps_ready = sem("a_eps_ready")
        sp_chain_a = sem("a_softplus_act")
        sp_ready = sem("a_softplus_ready")
        x_in = [sem(f"a_x_in{n}") for n in range(2)]
        act_chain = sem("a_act_chain")
        dve_chain = sem("a_dve_chain")
        std_ready = sem("a_std_ready")
        hn_ready = sem("a_hn_ready")
        tp_done = sem("a_transposed")
        hi_ready = sem("a_hT_hi")
        lo_ready = sem("a_hT_ready")
        raw_in = [sem(f"a_raw_in{n}") for n in range(RAW)]
        w_hi = sem("a_w_hi")
        w_ready = sem("a_w_ready")
        half_used = sem("a_half_used")
        job_done = sem("a_job_done")
        job_free = sem("a_job_free")
        sjob_done = sem("a_sample_job_done")
        sjob_free = sem("a_sample_job_free")
        xc_ready = sem("a_xc_ready")
        gate_done = sem("a_gate_done")
        gate_free = sem("a_gate_free")
        tanh_ready = sem("a_tanh_ready")
        quot_ready = sem("a_quotient_ready")
        root_ready = sem("a_root_ready")
        lru_done = sem("a_lru_done")
        rows_ready = sem("a_rows_ready")
        rows_out = [sem(f"a_rows_out{n}") for n in range(3)]
        lru_out = [sem(f"a_lru_out{n}") for n in range(2)]
        small_in = sem("a_small_in")
        small_ready = sem("a_small_ready")
        small_out = sem("a_small_out")
        pool_turn = sem("a_pool_turn")
        s_chain = sem("a_s_act_chain")
        s_xc_ready = sem("a_s_xc_ready")
        s_gate_done = sem("a_s_gate_done")
        s_r_ready = sem("a_s_r_ready")
        s_u_ready = sem("a_s_u_ready")
        s_t_ready = sem("a_s_t_ready")
        s_q_ready = sem("a_s_q_ready")
        s_root = sem("a_s_root")

        x_v = io["x_prompt"].rearrange("b (g t p) d -> (b g) t p d", g=GROUPS, p=P)
        w_v = io["w_in"][0].rearrange("(k p) n -> p k n", p=P)

        def chunk(c):
            return w_v[:, :, c * 256:c * 256 + 256] if c < 4 else (
                w_v[:, (c % 2) * 4:(c % 2) * 4 + 4, 1024 + (c - 4) // 2 * 512:1536 + (c - 4) // 2 * 512])

        def width(c):
            return 256 if c < 4 else 512

        def job_bank(j):
            return ACC[j % 4]

        q_v = io["q"][0:SEQ].rearrange("(g t p) n -> g t p n", g=GROUPS, p=P)
        k_v = io["k_prompt"].rearrange("l b (g t p) h e -> (l b g) t p (h e)", g=GROUPS, p=P)
        v_v = io["v_prompt"].rearrange("l b (g t p) h e -> (l b g) t p (h e)", g=GROUPS, p=P)
        s_rows = [io["q"][SEQ:SEQ + NS], io["k_sample"].rearrange("l b s h e -> (l b s) (h e)"),
                  io["v_sample"].rearrange("l b s h e -> (l b s) (h e)")]
        mix_v = io["mixT"][0:LRU].rearrange("(c p) t -> c p t", p=P)

        block = ctx.enter_context(nc.Block())

        @block.sync
        def _(sp):
            sp.dma_start(x[:, 0], x_v[0, 0]).then_inc(x_in[0], 16)
            sp.dma_start(gain[:], io["norm_pre_mix"].broadcast_to([P, D])).then_inc(consts_in, 16)
            sp.dma_start(ident[:], io["ident"]).then_inc(consts_in, 16)
            sp.dma_start(x[:, 1], x_v[0, 1]).then_inc(x_in[1], 16)
            for c in range(AHEAD):
                sp.dma_start(raw[:, c].rearrange("p (k n) -> p k n", n=width(c)), chunk(c)).then_inc(raw_in[c], 16)
            sp.dma_start(rope[:], io["rope"][0:SEQ].rearrange("(t p) a f -> p t a f", p=P)).then_inc(consts_in, 16)
            sp.dma_start(rope_s[:], io["rope"][SEQ:SEQ + NS]).then_inc(consts_in, 16)
            with nc.allow_non_contiguous_dma("a few vectors, channels onto partitions"):
                for c in range(LC):
                    sp.dma_start(convw[:, c], io["conv_w"][0, :, c * P:(c + 1) * P].rearrange("j p -> p j")).then_inc(consts_in, 16)
                sp.dma_start(convb[:], io["conv_b"][0].rearrange("(c p) -> p c", p=P)).then_inc(consts_in, 16)
                sp.dma_start(lru_l[:], io["lru_L"][0].rearrange("(c p) -> p c", p=P)).then_inc(consts_in, 16)
                for n, name in enumerate(("lru_b_a", "lru_b_x")):
                    sp.dma_start(gate_b[:, n], io[name][0].rearrange("(c h) j -> (h j) c", h=2)).then_inc(consts_in, 16)
                sp.wait_ge(ready0, 1)
                for n, name in enumerate(("lru_w_a", "lru_w_x")):
                    for h in range(2):
                        sp.dma_start(gate_w[h * 64:h * 64 + 64, n, :, h * 64:h * 64 + 64],
                                     io[name][0].rearrange("(c h) i j -> h i c j", h=2)[h]).then_inc(consts_in, 16)
                for c in range(LC):
                    for j in range(TAPS - 1):
                        sp.dma_start(s_conv[:, c, j], io["state_conv"][0, :, j, c * P:(c + 1) * P].rearrange("b p -> p b")).then_inc(small_in, 16)
                    sp.dma_start(s_h[:, c], io["state_h"][0, :, c * P:(c + 1) * P].rearrange("b p -> p b")).then_inc(small_in, 16)

            def group(i, last):
                for t, _, n in group_tiles(last):
                    if last or t >= 2:
                        sp.wait_ge(hn_ready, 4 * i + t - 1)
                    if last and t == TILES:
                        sp.dma_start(x[0:n, 0], io["x_sample"].rearrange("b s d -> (b s) d")).then_inc(x_in[0], 16)
                    elif t >= 2:
                        sp.dma_start(x[:, t % 2], x_v[i, t]).then_inc(x_in[t % 2], 16)
                for c in range(AHEAD, CH):
                    sp.wait_ge(w_ready, CH * i + c - RAW + 1)
                    sp.dma_start(raw[:, c % RAW].rearrange("p (k n) -> p k n", n=width(c)), chunk(c)).then_inc(raw_in[c % RAW], 16)
                if not last:
                    for t in range(2):
                        sp.wait_ge(hn_ready, 4 * i + t + 3)
                        sp.dma_start(x[:, t], x_v[i + 1, t]).then_inc(x_in[t], 16)
                    for c in range(AHEAD):
                        sp.wait_ge(w_ready, CH * i + CH + c - RAW + 1)
                        sp.dma_start(raw[:, c].rearrange("p (k n) -> p k n", n=width(c)), chunk(c)).then_inc(raw_in[c], 16)

            with sp.Fori(0, GROUPS - 1) as i:
                group(i, False)
            group(GROUPS - 1, True)

        @block.gpsimd
        def _(pool):
            pool.memset(gate_w[:], 0.0).then_inc(ready0, 1)

            def group(i, last):
                for which in range(3):
                    for t, _, n in group_tiles(last):
                        r = 4 * which + t
                        if t < TILES:
                            pool.wait_ge(rows_ready, 12 * i + r + 1 + (which if last else 0))
                            slot = (12 * 3 + r + which) % 3 if last else r % 3
                            dst = (q_v, k_v, v_v)[which][i, t]
                        else:
                            pool.wait_ge(rows_ready, 12 * i + 4 * which + which + TILES + 1)
                            slot = (12 * 3 + 4 * which + which + TILES) % 3
                            dst = s_rows[which]
                        pool.sem_inc(pool_turn, 1)
                        pool.dma_start(dst, rows[0:n, slot]).then_inc(rows_out[slot], 16)
                    if which >= 1:
                        for g in ((0, 1), (2, 3))[which - 1]:
                            pool.wait_ge(lru_done, LC * i + g + 1)
                            pool.sem_inc(pool_turn, 1)
                            pool.dma_start(mix_v[g, :, bass.ts(i, GROUP)], lo_out[:, g % 2]).then_inc(lru_out[g % 2], 16)

            with pool.Fori(0, GROUPS - 1) as i:
                group(i, False)
            group(GROUPS - 1, True)
            with nc.allow_non_contiguous_dma("states, a few thousand values"):
                pool.wait_ge(small_ready, 2)
                for c in range(LC):
                    ch = slice(c * P, (c + 1) * P)
                    pool.dma_start(io["conv_prompt"][0, 0, :, ch].rearrange("j p -> p j"), xpad[:, c, GROUP:GROUP + 3]).then_inc(small_out, 16)
                    pool.dma_start(io["conv_sample"][0, :, 0, ch].rearrange("b p -> p b"), s_conv[:, c, 1]).then_inc(small_out, 16)
                    pool.dma_start(io["conv_sample"][0, :, 1, ch].rearrange("b p -> p b"), s_conv[:, c, 2]).then_inc(small_out, 16)
                    pool.dma_start(io["conv_sample"][0, :, 2, ch].rearrange("b p -> p b"), s_xl[:, c]).then_inc(small_out, 16)
                    pool.dma_start(io["h_sample"][0, :, ch].rearrange("b p -> p b"), s_w[:, 10, c]).then_inc(small_out, 16)
                    pool.dma_start(io["mixT"][ch, SEQ:SEQ + NS], s_w[:, 11, c]).then_inc(small_out, 16)
                pool.dma_start(io["h_prompt"][0, 0].rearrange("(c p) -> p c", p=P), hlast[:]).then_inc(small_out, 16)
            pool.wait_ge(small_out, 16 * (6 * LC + 1))
            for n in range(3):
                pool.wait_ge(rows_out[n], 16 * 17)
            for n in range(2):
                pool.wait_ge(lru_out[n], 16 * 2 * GROUPS)

        def chunk_used(eng, i, n, last):
            before, c = ((i - 1), n - 1 + CH) if n <= 0 else (i, n - 1)
            which = (c - 4) // 2
            if c >= 4 and c % 2 == 0:
                eng.wait_ge(half_used, 3 * before + which + 1)
            else:
                eng.wait_ge(job_done, JOBS * before + (2 * c + 2 if c < 4 else 8 + 4 * which + 4))
                if last and n > 0:
                    eng.wait_ge(sjob_done, 2 * c + 2 if c < 4 else 8 + which + 1)

        def row_slot(i, last, which, t):
            if last:
                r = 36 + 5 * which + t
                return r % 3, r, r // 3
            r = 4 * which + t
            return r % 3, 12 * i + r, 4 * i + r // 3

        @block.scalar
        def _(act):
            def split_first(c):
                act.wait_ge(raw_in[c], 16)
                nc.scalar.activation(w[:, c, 0], raw[:, c], ACT.Copy).then_inc(w_hi, 1)

            def root(i, g):
                act.wait_ge(quot_ready, LC * i + g + 1)
                act.wait_ge(lru_done, LC * i + g)
                nc.scalar.activation(sq[:], qq[:], ACT.Sqrt, scale=2.0).then_inc(root_ready, 1)

            act.wait_ge(sp_chain_a, 1)
            nc.scalar.activation(sp_t[:, 1], sp_t[:, 0], ACT.Exp, scale=-1.0).then_inc(eps_ready, 1)
            act.wait_ge(sp_chain_a, 2)
            nc.scalar.activation(sp_t[:, 3], sp_t[:, 2], ACT.Ln).then_inc(eps_ready, 1)
            for c in range(AHEAD):
                split_first(c)

            def group(i, last):
                for t, col, n in group_tiles(last):
                    act.wait_ge(x_in[t % 2], 16 * (2 * i + t // 2 + 1))
                    nc.scalar.activation(junk[0:n], x[0:n, t % 2], ACT.Square, accum_out=ssq[0:n, t:t + 1]).then_inc(act_chain, 1)
                    act.wait_ge(act_chain, 4 * i + t + 1)
                    nc.scalar.activation(ssq[0:n, t:t + 1], ssq[0:n, t:t + 1], ACT.Sqrt, bias=eps[0:n], scale=1.0 / D).then_inc(std_ready, 1)
                    if t >= 1:
                        hi_halves(i, t - 1, col - P, P)
                hi_halves(i, t, col, n)
                for c in range(CH):
                    if c + AHEAD < CH:
                        split_in(i, c + AHEAD, last)
                    elif not last:
                        split_in(i + 1, c + AHEAD - CH, False)
                    if c < 4:
                        for f in range(2):
                            j, fc = 2 * c + f, (2 * c + f) % 4
                            act.wait_ge(job_done, JOBS * i + j + 1)
                            if c < 2:
                                act.wait_ge(xc_ready, LC * i)
                                nc.scalar.activation(xpad[:, fc, 3:], job_bank(j)[:], ACT.Copy).then_inc(job_free, 1)
                            else:
                                act.wait_ge(lru_done, LC * i)
                                nc.scalar.activation(gg[:, fc], job_bank(j)[:], ACT.Gelu_apprx_tanh).then_inc(job_free, 1)
                            if last:
                                act.wait_ge(sjob_done, j + 1)
                                if c < 2:
                                    nc.scalar.activation(s_xl[:, fc], SB_[:, 0:NS], ACT.Copy).then_inc(sjob_free, 1)
                                else:
                                    nc.scalar.activation(s_gg[:, fc], SB_[:, 0:NS], ACT.Gelu_apprx_tanh).then_inc(sjob_free, 1)
                    if c >= 6 and c < 10:
                        root(i, c - 6)
                    if c >= 5 and c % 2 == 1:
                        which = (c - 5) // 2
                        for t, _, n in group_tiles(last):
                            slot, before, uses = row_slot(i, last, which, t)
                            act.wait_ge(rows_out[slot], 16 * uses)
                            if t < TILES:
                                act.wait_ge(job_done, JOBS * i + 8 + 4 * which + t + 1)
                                nc.scalar.activation(rows[:, slot], ACC[t][:], ACT.Copy).then_inc(job_free, 1)
                            else:
                                act.wait_ge(sjob_done, 8 + which + 1)
                                nc.scalar.activation(rows[0:n, slot], SB_[0:n], ACT.Copy).then_inc(sjob_free, 1)
                    if c >= 5 and c < 9:
                        gates(i, c - 5)
                if last:
                    sample_gates()

            def hi_halves(i, t, col, n):
                for half in range(2):
                    if t == 0 and half == 0:
                        act.wait_ge(job_done, JOBS * i)
                    act.wait_ge(tp_done, 8 * i + 2 * t + half + 1)
                    nc.scalar.activation(hT[:, 0, 4 * half:4 * half + 4, col:col + n],
                                         TB[half][:, 0:4 * n].rearrange("p (k t) -> p k t", k=4), ACT.Copy).then_inc(hi_ready, 1)

            def split_in(i, c, last):
                act.wait_ge(raw_in[c % RAW], 16 * (CH // RAW * i + c // RAW + 1))
                chunk_used(act, i, FREED[c] if c < AHEAD else max(FREED[c], 0), last)
                nc.scalar.activation(w[:, SLOT[c], 0], raw[:, c % RAW], ACT.Copy).then_inc(w_hi, 1)

            def gates(i, g):
                act.wait_ge(gate_done, LC * i + g + 1)
                act.wait_ge(quot_ready, LC * i + g)
                nc.scalar.activation(ri[:, 0], GB[0][:], ACT.Sigmoid, bias=gate_b[:, 0, g:g + 1]).then_inc(gate_free, 1)
                nc.scalar.activation(ri[:, 1], GB[1][:], ACT.Sigmoid, bias=gate_b[:, 1, g:g + 1]).then_inc(gate_free, 1)
                act.wait_ge(gate_free, 2 * (LC * i + g + 1))
                nc.scalar.activation(u[:], ri[:, 0], ACT.Tanh, scale=sp8[:, g:g + 1])
                act.wait_ge(lru_done, LC * i + max(g - 1, 0))
                nc.scalar.activation(aa[:, g % 2], ri[:, 0], ACT.Exp, scale=nsp8[:, g:g + 1]).then_inc(tanh_ready, 1)

            def sample_gates():
                act.wait_ge(s_r_ready, 1)
                nc.scalar.activation(s_ri[:], s_ri[:], ACT.Sigmoid).then_inc(s_chain, 1)
                act.wait_ge(s_t_ready, 1)
                nc.scalar.activation(s_w[:, 1], s_w[:, 0], ACT.Tanh)
                nc.scalar.activation(s_w[:, 2], s_w[:, 0], ACT.Exp, scale=-1.0).then_inc(s_chain, 1)
                act.wait_ge(s_q_ready, 1)
                nc.scalar.activation(s_w[:, 6], s_w[:, 5], ACT.Sqrt, scale=2.0).then_inc(s_chain, 1)

            act.wait_ge(sp_ready, 1)
            with act.Fori(0, GROUPS - 1) as i:
                group(i, False)
            group(GROUPS - 1, True)

        @block.vector
        def _(dve):
            N_CONST = 4 + LC + 4 + 4
            V = nc.vector
            V.memset(eps[:], EPS)
            V.memset(hlast[:], 0.0)
            V.memset(xpad[:], 0.0)
            link = Chain(dve, dve_chain)
            dve.wait_ge(consts_in, 16 * N_CONST)
            link(V.tensor_scalar(sp_t[:, 4], lru_l[:], -1.0, None, ALU.mult))
            V.tensor_tensor(sp_t[:, 0], sp_t[:, 4], lru_l[:], ALU.max).then_inc(sp_chain_a, 1)
            dve.wait_ge(eps_ready, 1)
            link(V.tensor_scalar(sp_t[:, 2], sp_t[:, 1], 1.0, None, ALU.add))
            V.tensor_scalar(sp_t[:, 5], sp_t[:, 2], -1.0, 1e-30, ALU.add, ALU.max).then_inc(sp_chain_a, 1)
            dve.wait_ge(eps_ready, 2)
            dve.wait_ge(sp_chain_a, 2)
            link(V.reciprocal(sp8[:], sp_t[:, 5]))
            link(V.tensor_tensor(sp8[:], sp8[:], sp_t[:, 3], ALU.mult))
            link(V.tensor_scalar(sp_t[:, 5], sp_t[:, 2], 1.0, None, ALU.is_equal))
            link(V.tensor_tensor(sp8[:], sp8[:], sp_t[:, 5], ALU.add))
            link(V.tensor_tensor(sp8[:], sp8[:], sp_t[:, 1], ALU.mult))
            link(V.tensor_scalar(sp_t[:, 4], sp_t[:, 4], 0.0, None, ALU.max))
            link(V.tensor_tensor(sp8[:], sp8[:], sp_t[:, 4], ALU.add))
            link(V.tensor_scalar(sp8[:], sp8[:], 8.0, None, ALU.mult))
            V.tensor_scalar(nsp8[:], sp8[:], -1.0, None, ALU.mult).then_inc(sp_ready, 1)
            links0 = link.n
            LINKS = 64

            def split_lo(n, c):
                dve.wait_ge(w_hi, n)
                V.tensor_tensor(w[:, SLOT[c], 1], raw[:, c % RAW], w[:, SLOT[c], 0].bitcast(F32), ALU.subtract).then_inc(w_ready, 1)

            for c in range(AHEAD):
                split_lo(c + 1, c)

            def lru_head(i, g):
                dve.wait_ge(tanh_ready, LC * i + g + 1)
                link(V.tensor_scalar(rec[:], u[:], 1.0, None, ALU.add))
                link(V.reciprocal(rec[:], rec[:]))
                V.tensor_tensor(igx[:, g % 2], ri[:, 1], xc[:, g], ALU.mult)
                link(V.tensor_tensor(qq[:], u[:], rec[:], ALU.mult))
                V.nop().then_inc(quot_ready, 1)

            def lru_tail(i, g):
                dve.wait_ge(root_ready, LC * i + g + 1)
                link(V.tensor_tensor(igx[:, g % 2], sq[:], igx[:, g % 2], ALU.mult))
                link(V.tensor_tensor_scan(hs[:, g % 2], aa[:, g % 2], igx[:, g % 2], hlast[:, g:g + 1], ALU.mult, ALU.add))
                V.tensor_copy(hlast[:, g:g + 1], hs[:, g % 2, GROUP - 1:GROUP])
                dve.wait_ge(lru_out[g % 2], 16 * (2 * i + g // 2))
                link(V.tensor_tensor(lo_out[:, g % 2], hs[:, g % 2], gg[:, g], ALU.mult))
                V.nop().then_inc(lru_done, 1)

            def group(i, last):
                for t, col, n in group_tiles(last):
                    dve.wait_ge(std_ready, 4 * i + t + 1)
                    link(V.reciprocal(rstd[0:n, t:t + 1], ssq[0:n, t:t + 1]))
                    if t >= 2:
                        dve.wait_ge(tp_done, 8 * i + 2 * (t - 1))
                    else:
                        dve.wait_ge(tp_done, 8 * i)
                    V.scalar_tensor_tensor(hn[0:n, t % 2], x[0:n, t % 2], rstd[0:n, t:t + 1], gain[0:n], ALU.mult, ALU.mult).then_inc(hn_ready, 1)
                    if t >= 1:
                        lo_halves(i, t - 1, col - P, P)
                lo_halves(i, t, col, n)
                for c in range(CH):
                    if c + AHEAD < CH:
                        split_lo(CH * i + c + AHEAD + 1, (c + AHEAD) % CH)
                    elif not last:
                        split_lo(CH * i + c + AHEAD + 1, (c + AHEAD) % CH)
                    if c < 2:
                        for f in range(2):
                            fc = 2 * c + f
                            dve.wait_ge(job_free, JOBS * i + fc + 1)
                            link(V.tensor_scalar(xc[:, fc], xpad[:, fc, 0:GROUP], convw[:, fc, 0:1], convb[:, fc:fc + 1], ALU.mult, ALU.add))
                            for j in range(1, TAPS):
                                link(V.scalar_tensor_tensor(xc[:, fc], xpad[:, fc, j:j + GROUP], convw[:, fc, j:j + 1], xc[:, fc], ALU.mult, ALU.add))
                            if not last:
                                link(V.tensor_copy(xpad[:, fc, 0:3], xpad[:, fc, GROUP:GROUP + 3]))
                            V.nop().then_inc(xc_ready, 1)
                    if c == 3 and last:
                        sample_conv()
                    if c >= 5 and c % 2 == 1:
                        which = (c - 5) // 2
                        for t, _, n in group_tiles(last):
                            slot, before, uses = row_slot(i, last, which, t)
                            if t < TILES:
                                dve.wait_ge(job_free, JOBS * i + 8 + 4 * which + t + 1)
                            else:
                                dve.wait_ge(sjob_free, 8 + which + 1)
                            if which < 2:
                                v = rows[0:n, slot].rearrange("p (c d) -> p c d", d=HD)
                                t1, t2 = v[:, :, 0:HALF], v[:, :, HALF:ROT]
                                table = rope[:, 4 * i + t] if t < TILES and isinstance(i, int) else (rope[:, bass.ds(4 * i + t, 1)].rearrange("p o a f -> p (o a) f") if t < TILES else rope_s[:])
                                cos = table[:, 0:1, :].broadcast_to([n, COMP, HALF])
                                sin = table[:, 1:2, :].broadcast_to([n, COMP, HALF])
                                V.tensor_tensor(rt[0:n, 0], t1, cos, ALU.mult)
                                V.tensor_tensor(rt[0:n, 1], t2, sin, ALU.mult)
                                V.tensor_tensor(rt[0:n, 2], t2, cos, ALU.mult)
                                link(V.tensor_tensor(rt[0:n, 3], t1, sin, ALU.mult))
                                V.tensor_tensor(t1, rt[0:n, 0], rt[0:n, 1], ALU.subtract)
                                link(V.tensor_tensor(t2, rt[0:n, 2], rt[0:n, 3], ALU.add))
                            V.nop().then_inc(rows_ready, 1)
                    if c >= 6:
                        lru_tail(i, c - 6)
                    if c >= 5 and c < 9:
                        lru_head(i, c - 5)
                if last:
                    sample_lru()
                    V.nop().then_inc(small_ready, 1)

            def lo_halves(i, t, col, n):
                for half in range(2):
                    dve.wait_ge(hi_ready, 8 * i + 2 * t + half + 1)
                    dst = hT[:, :, 4 * half:4 * half + 4, col:col + n]
                    V.tensor_tensor(dst[:, 1], TB[half][:, 0:4 * n].rearrange("p (k t) -> p k t", k=4),
                                    dst[:, 0].bitcast(F32), ALU.subtract).then_inc(lo_ready, 1)

            def over(v):
                return v.rearrange("p (c o) -> p c o", o=1).broadcast_to([P, LC, NS])

            def sample_conv():
                dve.wait_ge(small_in, 16 * 4 * LC)
                dve.wait_ge(sjob_free, 4)
                link(V.tensor_tensor(s_w[:, 0], s_conv[:, :, 0], over(convw[:, :, 0]), ALU.mult))
                link(V.tensor_tensor(s_w[:, 7], s_w[:, 0], over(convb[:]), ALU.add))
                for j in range(1, TAPS):
                    tap = s_conv[:, :, j] if j < 3 else s_xl[:]
                    link(V.tensor_tensor(s_w[:, 0], tap, over(convw[:, :, j]), ALU.mult))
                    link(V.tensor_tensor(s_w[:, 7], s_w[:, 7], s_w[:, 0], ALU.add))
                V.nop().then_inc(s_xc_ready, 1)

            def sample_lru():
                dve.wait_ge(s_gate_done, 1)
                V.tensor_tensor(s_ri[:, 0], GB[0][:, 0:LC * NS].rearrange("p (c b) -> p c b", b=NS), over(gate_b[:, 0]), ALU.add)
                link(V.tensor_tensor(s_ri[:, 1], GB[1][:, 0:LC * NS].rearrange("p (c b) -> p c b", b=NS), over(gate_b[:, 1]), ALU.add))
                V.nop().then_inc(s_r_ready, 1)
                dve.wait_ge(s_chain, 1)
                link(V.tensor_tensor(s_w[:, 0], s_ri[:, 0], over(sp8[:]), ALU.mult))
                V.nop().then_inc(s_t_ready, 1)
                link(V.tensor_tensor(s_w[:, 8], s_ri[:, 1], s_w[:, 7], ALU.mult))
                dve.wait_ge(s_chain, 2)
                link(V.tensor_scalar(s_w[:, 3], s_w[:, 1], 1.0, None, ALU.add))
                link(V.reciprocal(s_w[:, 4], s_w[:, 3]))
                link(V.tensor_tensor(s_w[:, 5], s_w[:, 1], s_w[:, 4], ALU.mult))
                V.nop().then_inc(s_q_ready, 1)
                link(V.tensor_tensor(s_w[:, 9], s_w[:, 2], s_h[:], ALU.mult))
                dve.wait_ge(s_chain, 3)
                link(V.tensor_tensor(s_w[:, 8], s_w[:, 8], s_w[:, 6], ALU.mult))
                link(V.tensor_tensor(s_w[:, 10], s_w[:, 8], s_w[:, 9], ALU.add))
                dve.wait_ge(sjob_free, 8)
                link(V.tensor_tensor(s_w[:, 11], s_w[:, 10], s_gg[:], ALU.mult))
                V.nop().then_inc(small_ready, 1)

            with dve.Fori(0, GROUPS - 1) as i:
                link = Chain(dve, dve_chain, LINKS * i + links0)
                group(i, False)
                assert link.n == LINKS, link.n
            link = Chain(dve, dve_chain, LINKS * (GROUPS - 1) + links0)
            group(GROUPS - 1, True)

        @block.tensor
        def _(pe):
            pe.wait_ge(consts_in, 16 * 16)

            def products(out, blocks, lhs, rhs, first=True, end=True):
                for k in range(blocks):
                    for n, (a, b) in enumerate(PRODUCTS):
                        ins = nc.tensor.matmul(out, lhs(k, a), rhs(k, b), start=first and k == 0 and n == 0,
                                               stop=end and k == blocks - 1 and n == 2)
                return ins

            def group(i, last):
                pe.wait_ge(gate_free, 2 * LC * i)
                for t, col, n in group_tiles(last):
                    pe.wait_ge(hn_ready, 4 * i + t + 1)
                    for half in range(2):
                        pe.wait_ge(lo_ready, 8 * i + 2 * t + half - 1 if t else 8 * i)
                        for k in range(4):
                            kk = 4 * half + k
                            ins = nc.tensor.transpose(TB[half][:, k * n:k * n + n], hn[0:n, t % 2, kk * P:kk * P + P], ident[0:n, 0:n])
                        ins.then_inc(tp_done, 1)
                pe.wait_ge(lo_ready, 8 * i + 2 * len(group_tiles(last)))
                for c in range(CH):
                    s = SLOT[c]
                    pe.wait_ge(w_ready, CH * i + c + 1)
                    wv = w[:, s].rearrange("p a (k n) -> p a k n", n=width(c))
                    if c < 4:
                        for f in range(2):
                            j = 2 * c + f
                            pe.wait_ge(job_free, JOBS * i + max(j - 3, 0))
                            ins = products(job_bank(j)[:], KD, lambda k, a: wv[:, a, k, f * P:f * P + P],
                                     lambda k, b: hT[:, b, k, 0:GROUP])
                            ins.then_inc(job_done, 1)
                            if last:
                                if j:
                                    pe.wait_ge(sjob_free, j)
                                ins = products(SB_[:, 0:NS], KD, lambda k, a: wv[:, a, k, f * P:f * P + P],
                                         lambda k, b: hT[:, b, k, GROUP:WIDE])
                                ins.then_inc(sjob_done, 1)
                    else:
                        which, kh = (c - 4) // 2, c % 2
                        for t, col, n in group_tiles(last):
                            if kh == 0:
                                if t < TILES:
                                    pe.wait_ge(job_free, JOBS * i + 8 + 4 * which + t - 3)
                                else:
                                    pe.wait_ge(sjob_free, 8 + which)
                            out = ACC[t][:] if t < TILES else SB_[0:n]
                            ins = products(out, 4, lambda k, a: hT[:, a, 4 * kh + k, col:col + n],
                                           lambda k, b: wv[:, b, k, :], kh == 0, kh == 1)
                            if kh == 1:
                                ins.then_inc(job_done if t < TILES else sjob_done, 1)
                    if c >= 4 and c % 2 == 0:
                        ins.then_inc(half_used, 1)
                    if 4 <= c < 8:
                        g = c - 4
                        pe.wait_ge(xc_ready, LC * i + g + 1)
                        pe.wait_ge(gate_free, 2 * (LC * i + g))
                        nc.tensor.matmul(GB[0][:], gate_w[:, 0, g], xc[:, g], start=True, stop=True)
                        nc.tensor.matmul(GB[1][:], gate_w[:, 1, g], xc[:, g], start=True, stop=True).then_inc(gate_done, 1)
                if last:
                    pe.wait_ge(s_xc_ready, 1)
                    pe.wait_ge(gate_free, 2 * LC * GROUPS)
                    for g in range(LC):
                        for n in range(2):
                            ins = nc.tensor.matmul(GB[n][:, g * NS:g * NS + NS], gate_w[:, n, g], s_w[:, 7, g], start=True, stop=True)
                    ins.then_inc(s_gate_done, 1)

            with pe.Fori(0, GROUPS - 1) as i:
                group(i, False)
            group(GROUPS - 1, True)


def attend_prompt(nc, io, sems):
    ctx = ExitStack()
    sb = lambda name, shape, dt=F32: ctx.enter_context(nc.sbuf_tensor(name, shape, dt))
    sem = lambda name: sems.enter_context(nc.semaphore(name))
    QT = SEQ // P
    NK = [i // 4 + 1 for i in range(QT)]
    size = lambda i, kc: 512 if kc < NK[i] - 1 else (i % 4 + 1) * P
    before = [sum(NK[:i]) for i in range(QT + 1)]
    CHUNKS = before[QT]
    SCORES = 2 * CHUNKS
    RESCALED = [sum(n > 1 for n in NK[:i]) for i in range(QT + 1)]
    WT_JOBS = CHUNKS + 4
    with ctx:
        ident = sb("b_ident", [P, P])
        ident_r = sb("b_ident_r", [P, P], F32R)
        mask_in = sb("b_mask_in", [P, P])
        mask = sb("b_mask", [P, P], F32R)
        lam_in = sb("b_lam_in", [P, 4, HD])
        lam_t = sb("b_lam_t", [P, 2, HD])
        lam_s = sb("b_lam_s", [P, 4])
        nlam = sb("b_nlam", [P, 1])
        gain = sb("b_gain", [P, 1])
        eps = sb("b_eps", [P, 1])
        raw = sb("b_raw", [P, 3, QT, P])
        kin = sb("b_kin", [P, 2, 2, HD], F32R)
        qin = sb("b_qin", [P, 2, 2, 2, HD], F32R)
        vv = sb("b_v", [P, QT, 2, P], F32R)
        kT = sb("b_kT", [P, 2, SEQ], F32R)
        qT = sb("b_qT", [P, 2, 4, P], F32R)
        p = sb("b_p", [P, 2, 2, SEQ])
        w = sb("b_w", [P, 2, SEQ])
        wT = sb("b_wT", [P, 2, 2, 512], F32R)
        m = sb("b_m", [P, 2, 2, 4])
        nm = sb("b_nm", [P, 2, 2, 4])
        ls = sb("b_l", [P, 2, 2, 4])
        top = sb("b_top", [P, 2])
        dm = sb("b_dm", [P, 2, 4])
        al = sb("b_al", [P, 2, 4])
        la = sb("b_la", [P, 2, 4])
        rl = sb("b_rl", [P, 2])
        coef = sb("b_coef", [P, 2, 2, 4])
        ob = sb("b_ob", [P, P])
        o = sb("b_o", [P, QT, P])
        osq = sb("b_osq", [P, QT, P])
        oss = sb("b_oss", [P, QT])
        ors = sb("b_ors", [P, QT])
        oT = sb("b_oT", [P, SEQ])
        S = [ctx.enter_context(nc.psum_tensor(f"b_S{n}", [P, 512], F32)) for n in range(4)]
        WT = [ctx.enter_context(nc.psum_tensor(f"b_WT{n}", [P, 512], F32)) for n in range(2)]
        O = ctx.enter_context(nc.psum_tensor("b_O", [P, 512], F32))
        M = ctx.enter_context(nc.psum_tensor("b_M", [P, 512], F32))
        consts_in = sem("b_consts_in")
        setup = sem("b_setup")
        lam_sum = sem("b_lam_sum")
        lam_exp = sem("b_lam_exp")
        rows_in = [sem(f"b_rows_in{n}") for n in range(4)]
        split_hi = sem("b_split_hi")
        split = sem("b_split")
        m_done = sem("b_m_done")
        k_free = sem("b_kT_ready")
        q_free = sem("b_qT_ready")
        s_done = sem("b_scores")
        nm_ready = sem("b_nm_ready")
        exp_done = sem("b_exp_done")
        dm_ready = sem("b_dm_ready")
        al_ready = sem("b_al_ready")
        coef_ready = sem("b_coef_ready")
        t2_ready = sem("b_t2_ready")
        w_ready = sem("b_w_ready")
        wt_done = sem("b_wT_in_psum")
        wt_hi = sem("b_wT_hi")
        wt_lo = sem("b_wT_lo")
        pv_done = sem("b_pv_done")
        ob_ready = sem("b_ob_ready")
        o_ready = sem("b_o_ready")
        osq_ready = sem("b_osq_ready")
        oss_ready = sem("b_oss_ready")
        std_ready = sem("b_std_ready")
        on_ready = sem("b_on_ready")
        dve_chain = sem("b_dve_chain")
        stored = sem("b_stored")
        stored_turn = sem("b_stored_turn")
        rows_v = [io["q"][0:SEQ].rearrange("(t p) (h e) -> h p t e", p=P, e=P),
                  io["k_prompt"].rearrange("l b (t p) h e -> (l b h) p t e", p=P),
                  io["v_prompt"].rearrange("l b (t p) h e -> (l b h) p t e", p=P)]
        out_v = io["mixT"][LRU:, 0:SEQ].rearrange("(h e) t -> h e t", e=P)
        block = ctx.enter_context(nc.Block())

        @block.sync
        def _(sp):
            sp.dma_start(ident[:], io["ident"]).then_inc(consts_in, 16)
            sp.dma_start(mask_in[:], io["mask"]).then_inc(consts_in, 16)
            for n, name in enumerate(("lambda_q1", "lambda_k1", "lambda_q2", "lambda_k2")):
                sp.dma_start(lam_in[:, n], io[name].broadcast_to([P, HD])).then_inc(consts_in, 16)
            sp.dma_start(gain[:], io["subln_g"].rearrange("l (e o) -> (l e) o", o=1)).then_inc(consts_in, 16)
            for g in range(4):
                for n in range(3):
                    sp.dma_start(raw[:, n, 4 * g:4 * g + 4], rows_v[n][0, :, 4 * g:4 * g + 4]).then_inc(rows_in[g], 16)
            with sp.Fori(0, HEADS - 1) as h:
                for g in range(4):
                    sp.wait_ge(split, QT * h + 4 * g + 4)
                    for n in range(3):
                        sp.dma_start(raw[:, n, 4 * g:4 * g + 4], rows_v[n][h + 1, :, 4 * g:4 * g + 4]).then_inc(rows_in[g], 16)

        @block.gpsimd
        def _(pool):
            with pool.Fori(0, HEADS) as h:
                pool.wait_ge(wt_lo, WT_JOBS * (h + 1))
                pool.sem_inc(stored_turn, 1)
                pool.dma_start(out_v[h], oT[:]).then_inc(stored, 16)
            pool.wait_ge(stored, 16 * HEADS)

        def steps():
            return range(-1, QT)

        def chunks_of(i):
            return NK[i] if 0 <= i < QT else 0

        @block.scalar
        def _(act):
            A = nc.scalar
            act.wait_ge(lam_sum, 1)
            A.activation(lam_s[:, 2:4], lam_s[:, 0:2], ACT.Exp).then_inc(lam_exp, 1)
            act.wait_ge(consts_in, 16 * 7)
            A.activation(ident_r[:], ident[:], ACT.Copy)
            A.activation(mask[:], mask_in[:], ACT.Copy).then_inc(setup, 1)

            def head(h):
                def prep(t):
                    if t % 4 == 0:
                        act.wait_ge(rows_in[t // 4], 48 * (h + 1))
                    act.wait_ge(m_done, 2 * (QT * h + t))
                    A.activation(kin[:, :, 0], raw[:, 1, t].rearrange("p (c d) -> p c d", d=HD), ACT.Copy)
                    A.activation(qin[:, :, 0], raw[:, 0, t].rearrange("p (c o d) -> p c o d", o=1, d=HD).broadcast_to([P, 2, 2, HD]), ACT.Copy)
                    if t == 0:
                        act.wait_ge(pv_done, CHUNKS * h)
                    A.activation(vv[:, t, 0], raw[:, 2, t], ACT.Copy).then_inc(split_hi, 1)

                def keys(t):
                    act.wait_ge(m_done, 2 * (QT * h + t) + 1)
                    A.activation(kT[:, :, t * P:t * P + P], M[:, 0:2 * P].rearrange("p (c t) -> p c t", c=2), ACT.Copy).then_inc(k_free, 1)

                def exps(i, kc):
                    for c in range(2):
                        j = 2 * (before[i] + kc) + c
                        act.wait_ge(nm_ready, SCORES * h + j + 1)
                        if kc == 0 and c == 0:
                            act.wait_ge(w_ready, CHUNKS * h + (before[i - 1] if i >= 1 else 0))
                        n = size(i, kc)
                        A.activation(p[:, i % 2, c, kc * 512:kc * 512 + n], S[j % 4][:, 0:n], ACT.Exp,
                                     bias=nm[:, i % 2, c, kc:kc + 1], scale=QSCALE,
                                     accum_out=ls[:, i % 2, c, kc:kc + 1]).then_inc(exp_done, 1)

                def hi(i, kc):
                    j = before[i] + kc
                    act.wait_ge(pv_done, CHUNKS * h + max(j - 1, 0))
                    act.wait_ge(wt_done, WT_JOBS * h + j + 1)
                    n = size(i, kc)
                    A.activation(wT[:, j % 2, 0, 0:n], WT[j % 2][:, 0:n], ACT.Copy).then_inc(wt_hi, 1)

                prep(0)
                keys(0)
                prep(1)
                for i in steps():
                    if i >= 0 and NK[i] > 1:
                        act.wait_ge(dm_ready, RESCALED[QT] * h + RESCALED[i] + 1)
                        A.activation(al[:, :, 0:NK[i]], dm[:, :, 0:NK[i]], ACT.Exp, scale=QSCALE).then_inc(al_ready, 1)
                    for kc in range(max(chunks_of(i), chunks_of(i + 1))):
                        if kc < chunks_of(i):
                            if kc == 0:
                                act.wait_ge(coef_ready, QT * h + i + 1)
                            n = size(i, kc)
                            A.activation(p[:, i % 2, 1, kc * 512:kc * 512 + n], p[:, i % 2, 1, kc * 512:kc * 512 + n], ACT.Copy,
                                         scale=coef[:, i % 2, 1, kc:kc + 1]).then_inc(t2_ready, 1)
                        if kc < chunks_of(i + 1):
                            exps(i + 1, kc)
                        if kc == 0 and i + 2 < QT:
                            keys(i + 2)
                            if i + 3 < QT:
                                prep(i + 3)
                        if 1 <= kc <= chunks_of(i):
                            hi(i, kc - 1)
                    if i >= 0:
                        if max(chunks_of(i), chunks_of(i + 1)) == chunks_of(i):
                            hi(i, NK[i] - 1)
                        act.wait_ge(pv_done, CHUNKS * h + before[i + 1])
                        act.wait_ge(o_ready, QT * h + i)
                        A.activation(ob[:], O[:, P:2 * P], ACT.Copy).then_inc(ob_ready, 1)
                act.wait_ge(o_ready, QT * (h + 1))
                A.activation(osq[:], o[:], ACT.Square).then_inc(osq_ready, 1)
                act.wait_ge(oss_ready, h + 1)
                A.activation(ors[:], oss[:], ACT.Sqrt, bias=eps[:], scale=1.0 / P).then_inc(std_ready, 1)

            with act.Fori(0, HEADS) as h:
                head(h)

        @block.vector
        def _(dve):
            V = nc.vector
            V.memset(eps[:], EPS_SUBLN)
            link = Chain(dve, dve_chain)
            dve.wait_ge(consts_in, 16 * 7)
            link(V.tensor_tensor(lam_t[:], lam_in[:, 0:4:2], lam_in[:, 1:4:2], ALU.mult))
            V.reduce_sum(lam_s[:, 0:2], lam_t[:], axis=AX).then_inc(lam_sum, 1)
            dve.wait_ge(lam_exp, 1)
            link(V.tensor_tensor(nlam[:], lam_s[:, 3:4], lam_s[:, 2:3], ALU.subtract))
            link(V.tensor_scalar(nlam[:], nlam[:], -LAM_INIT, None, ALU.add))
            link(V.tensor_scalar(gain[:], gain[:], 1.0 - LAM_INIT, None, ALU.mult))
            links0 = link.n
            LINKS = 0

            def head(h, link):
                def prep(t):
                    dve.wait_ge(split_hi, QT * h + t + 1)
                    V.tensor_tensor(kin[:, :, 1], raw[:, 1, t].rearrange("p (c d) -> p c d", d=HD), kin[:, :, 0].bitcast(F32), ALU.subtract)
                    V.tensor_tensor(qin[:, :, 1], raw[:, 0, t].rearrange("p (c o d) -> p c o d", o=1, d=HD).broadcast_to([P, 2, 2, HD]),
                                    qin[:, :, 0].bitcast(F32), ALU.subtract)
                    V.tensor_tensor(vv[:, t, 1], raw[:, 2, t], vv[:, t, 0].bitcast(F32), ALU.subtract).then_inc(split, 1)

                def queries(t):
                    dve.wait_ge(m_done, 2 * (QT * h + t) + 2)
                    V.tensor_copy(qT[:, t % 2].rearrange("p a t -> p (a t)"), M[:]).then_inc(q_free, 1)

                def maxes(i, kc):
                    for c in range(2):
                        j = 2 * (before[i] + kc) + c
                        n = size(i, kc)
                        dve.wait_ge(s_done, SCORES * h + j + 1)
                        link(V.reduce_max(m[:, i % 2, c, kc:kc + 1], S[j % 4][:, 0:n], axis=AX))
                        V.tensor_scalar(nm[:, i % 2, c, kc:kc + 1], m[:, i % 2, c, kc:kc + 1], -QSCALE, None, ALU.mult).then_inc(nm_ready, 1)

                def lo(i, kc):
                    j = before[i] + kc
                    n = size(i, kc)
                    dve.wait_ge(wt_hi, CHUNKS * h + j + 1)
                    V.tensor_tensor(wT[:, j % 2, 1, 0:n], WT[j % 2][:, 0:n], wT[:, j % 2, 0, 0:n].bitcast(F32), ALU.subtract).then_inc(wt_lo, 1)

                def stats(i):
                    b, n = i % 2, NK[i]
                    dve.wait_ge(exp_done, SCORES * h + 2 * before[i + 1])
                    if n > 1:
                        link(V.reduce_max(top[:], m[:, b, :, 0:n], axis=AX))
                        V.tensor_tensor(dm[:, :, 0:n], m[:, b, :, 0:n], top[:].rearrange("p (c o) -> p c o", o=1).broadcast_to([P, 2, n]),
                                        ALU.subtract).then_inc(dm_ready, 1)
                        dve.wait_ge(al_ready, RESCALED[QT] * h + RESCALED[i] + 1)
                        link(V.tensor_tensor(la[:, :, 0:n], ls[:, b, :, 0:n], al[:, :, 0:n], ALU.mult))
                        link(V.reduce_sum(rl[:], la[:, :, 0:n], axis=AX))
                        link(V.reciprocal(rl[:], rl[:]))
                        link(V.tensor_tensor(rl[:, 1:2], rl[:, 1:2], nlam[:], ALU.mult))
                        link(V.tensor_tensor(coef[:, b, :, 0:n], al[:, :, 0:n], rl[:].rearrange("p (c o) -> p c o", o=1).broadcast_to([P, 2, n]), ALU.mult))
                    else:
                        link(V.reciprocal(coef[:, b, :, 0:1], ls[:, b, :, 0:1]))
                        link(V.tensor_tensor(coef[:, b, 1, 0:1], coef[:, b, 1, 0:1], nlam[:], ALU.mult))
                    V.nop().then_inc(coef_ready, 1)

                prep(0)
                queries(0)
                prep(1)
                for i in steps():
                    if i >= 0:
                        stats(i)
                    for kc in range(max(chunks_of(i), chunks_of(i + 1))):
                        if kc < chunks_of(i + 1):
                            maxes(i + 1, kc)
                        if kc < chunks_of(i):
                            n = size(i, kc)
                            span = slice(kc * 512, kc * 512 + n)
                            dve.wait_ge(t2_ready, CHUNKS * h + before[i] + kc + 1)
                            V.scalar_tensor_tensor(w[:, i % 2, span], p[:, i % 2, 0, span], coef[:, i % 2, 0, kc:kc + 1],
                                                   p[:, i % 2, 1, span], ALU.mult, ALU.add).then_inc(w_ready, 1)
                        if kc == 0 and i + 2 < QT:
                            queries(i + 2)
                            if i + 3 < QT:
                                prep(i + 3)
                        if 1 <= kc <= chunks_of(i):
                            lo(i, kc - 1)
                    if i >= 0:
                        if max(chunks_of(i), chunks_of(i + 1)) == chunks_of(i):
                            lo(i, NK[i] - 1)
                        dve.wait_ge(ob_ready, QT * h + i + 1)
                        V.tensor_tensor(o[:, i], O[:, 0:P], ob[:], ALU.add).then_inc(o_ready, 1)
                dve.wait_ge(osq_ready, h + 1)
                V.reduce_sum(oss[:], osq[:], axis=AX).then_inc(oss_ready, 1)
                dve.wait_ge(std_ready, h + 1)
                link(V.reciprocal(ors[:], ors[:]))
                V.tensor_tensor(osq[:], o[:], ors[:].rearrange("p (t o) -> p t o", o=1).broadcast_to([P, QT, P]), ALU.mult).then_inc(on_ready, 1)
                dve.wait_ge(stored, 16 * h)
                for b in range(4):
                    j = CHUNKS + b
                    dve.wait_ge(wt_done, WT_JOBS * h + j + 1)
                    V.tensor_scalar(oT[:, b * 512:b * 512 + 512], WT[j % 2][:], gain[:], None, ALU.mult).then_inc(wt_lo, 1)

            LINKS = 2 * CHUNKS + 5 * 12 + 12 + 2 * 4 + 1
            with dve.Fori(0, HEADS) as h:
                link = Chain(dve, dve_chain, LINKS * h + links0)
                head(h, link)
                assert link.n == LINKS, (link.n, LINKS)

        @block.tensor
        def _(pe):
            pe.wait_ge(setup, 1)

            def head(h):
                def prep(t):
                    pe.wait_ge(split, QT * h + t + 1)
                    pe.wait_ge(q_free, QT * h + t)
                    for c in range(2):
                        ins = nc.tensor.transpose(M[:, c * P:c * P + P], kin[:, c].bitcast(F32).rearrange("p a d -> p (a d)"), ident[:])
                    ins.then_inc(m_done, 1)
                    pe.wait_ge(k_free, QT * h + t + 1)
                    for c in range(2):
                        for a in range(2):
                            ins = nc.tensor.transpose(M[:, (2 * c + a) * P:(2 * c + a + 1) * P],
                                                      qin[:, c, a].bitcast(F32).rearrange("p a d -> p (a d)"), ident[:])
                    ins.then_inc(m_done, 1)

                def scores(i, kc):
                    for c in range(2):
                        j = 2 * (before[i] + kc) + c
                        n = size(i, kc)
                        pe.wait_ge(q_free, QT * h + i + 1)
                        pe.wait_ge(exp_done, SCORES * h + max(j - 3, 0))
                        diagonal = kc == NK[i] - 1
                        for a in range(2):
                            ins = nc.tensor.matmul(S[j % 4][:, 0:n], qT[:, i % 2, 2 * c + a], kT[:, c, kc * 512:kc * 512 + n],
                                                   start=a == 0, stop=a == 1 and not diagonal)
                        if diagonal:
                            ins = nc.tensor.matmul(S[j % 4][:, n - P:n], ident_r[:], mask[:], start=False, stop=True)
                        ins.then_inc(s_done, 1)

                def weights(i, kc):
                    j = before[i] + kc
                    n = size(i, kc)
                    pe.wait_ge(w_ready, CHUNKS * h + j + 1)
                    pe.wait_ge(wt_lo, WT_JOBS * h + max(j - 1, 0))
                    for t in range(n // P):
                        ins = nc.tensor.transpose(WT[j % 2][:, t * P:t * P + P], w[:, i % 2, kc * 512 + t * P:kc * 512 + t * P + P], ident[:])
                    ins.then_inc(wt_done, 1)

                def values(i, kc):
                    j = before[i] + kc
                    n = size(i, kc)
                    pe.wait_ge(wt_lo, WT_JOBS * h + j + 1)
                    if kc == 0:
                        pe.wait_ge(o_ready, QT * h + i)
                    for t in range(n // P):
                        k = kc * 4 + t
                        nc.tensor.matmul(O[:, 0:2 * P], wT[:, j % 2, 0, t * P:t * P + P], vv[:, k].rearrange("p a e -> p (a e)"),
                                         start=k == 0, stop=False)
                        ins = nc.tensor.matmul(O[:, 0:P], wT[:, j % 2, 1, t * P:t * P + P], vv[:, k, 0], start=False, stop=k == i)
                    ins.then_inc(pv_done, 1)

                prep(0)
                for i in steps():
                    for kc in range(max(chunks_of(i), chunks_of(i + 1))):
                        if kc < chunks_of(i + 1):
                            scores(i + 1, kc)
                        if kc < chunks_of(i):
                            weights(i, kc)
                        if kc == 0 and i + 2 < QT:
                            prep(i + 2)
                        if 1 <= kc <= chunks_of(i):
                            values(i, kc - 1)
                    if i >= 0 and max(chunks_of(i), chunks_of(i + 1)) == chunks_of(i):
                        values(i, NK[i] - 1)
                pe.wait_ge(on_ready, h + 1)
                for b in range(4):
                    j = CHUNKS + b
                    pe.wait_ge(wt_lo, WT_JOBS * h + j - 1)
                    for t in range(4):
                        ins = nc.tensor.transpose(WT[j % 2][:, t * P:t * P + P], osq[:, 4 * b + t], ident[:])
                    ins.then_inc(wt_done, 1)

            with pe.Fori(0, HEADS) as h:
                head(h)


def attend_sample(nc, io, sems):
    ctx = ExitStack()
    sb = lambda name, shape, dt=F32: ctx.enter_context(nc.sbuf_tensor(name, shape, dt))
    sem = lambda name: sems.enter_context(nc.semaphore(name))
    W = HEADS * P
    R = NS * COMP
    RH = NS * HEADS
    N_PHYS = io["cache_k"].shape[1]
    with ctx:
        table = sb("d_table", [1, NS * PAGES], I32)
        kp = sb("d_k", [P, NS, PAGES, W])
        vp = sb("d_v", [P, NS, PAGES, W])
        qb = sb("d_q", [P, NS, W])
        prod = sb("d_prod", [P, 2, PAGES, W])
        sc = sb("d_scores", [P, PAGES, R])
        ident = sb("d_ident", [P, P])
        ones = sb("d_ones", [P, P])
        sel = sb("d_sel", [R, 2])
        lam_in = sb("d_lam_in", [P, 4, HD])
        lam_t = sb("d_lam_t", [P, 2, HD])
        lam_s = sb("d_lam_s", [P, 4])
        nlam = sb("d_nlam", [P, 1])
        gain = sb("d_gain", [P, 1])
        eps = sb("d_eps", [P, 1])
        q64 = sb("d_q64", [R, HD])
        k64 = sb("d_k64", [R, HD])
        v32 = sb("d_v32", [RH, P])
        own = sb("d_own", [R, 1])
        pp = sb("d_p", [R, PAGES * PAGE])
        st = sb("d_st", [R, 8])
        wn = sb("d_wn", [R, P])
        cp = sb("d_cp", [P, PAGES * R])
        ws = sb("d_ws", [P, PAGES, RH])
        wnb = sb("d_wnb", [P, R])
        wo = sb("d_wo", [P, RH])
        vT = sb("d_vT", [P, RH])
        o = sb("d_o", [P, RH])
        osq = sb("d_osq", [P, RH])
        ors = sb("d_ors", [P, RH])
        res = sb("d_res", [P, HEADS, NS])
        ST = ctx.enter_context(nc.psum_tensor("d_ST", [P, 512], F32))
        PT = ctx.enter_context(nc.psum_tensor("d_PT", [P, 512], F32))
        OT = ctx.enter_context(nc.psum_tensor("d_OT", [P, 512], F32))
        VT = ctx.enter_context(nc.psum_tensor("d_VT", [P, 512], F32))
        WB = ctx.enter_context(nc.psum_tensor("d_WB", [P, 512], F32))
        SS = ctx.enter_context(nc.psum_tensor("d_SS", [P, 512], F32))
        table_in = sem("d_table_in")
        consts_in = sem("d_consts_in")
        k_in = [sem(f"d_k_in{b}") for b in range(NS // 2)]
        v_in = [sem(f"d_v_in{b}") for b in range(NS // 2)]
        q_in = sem("d_q_in")
        chain = sem("d_dve_chain")
        to_act = sem("d_to_act")
        from_act = sem("d_from_act")
        to_pe = sem("d_to_pe")
        from_pe = sem("d_from_pe")
        res_ready = sem("d_res_ready")
        stored = sem("d_stored")
        rows = [io["q"][SEQ:SEQ + NS], io["k_sample"].rearrange("l b s h e -> (l b s) (h e)"),
                io["v_sample"].rearrange("l b s h e -> (l b s) (h e)")]
        ck = io["cache_k"].rearrange("l n t h e -> (l n) t (h e)")
        cv = io["cache_v"].rearrange("l n t h e -> (l n) t (h e)")
        block = ctx.enter_context(nc.Block())

        def pages(eng, cache, dst, arrived):
            eng.wait_ge(table_in, 16)
            for b in range(NS):
                for n in range(PAGES):
                    page = eng.value_load(table[0:1, b * PAGES + n:b * PAGES + n + 1], min_val=0, max_val=N_PHYS - 1)
                    eng.dma_start(dst[:, b, n], cache[page]).then_inc(arrived[b // 2], 16)

        @block.sync
        def _(sp):
            sp.dma_start(table[:], io["page_table"].rearrange("(o b) n -> o (b n)", o=1)).then_inc(table_in, 16)
            for b in range(NS):
                sp.dma_start(qb[:, b], rows[0][b:b + 1].broadcast_to([P, W])).then_inc(q_in, 16)
            pages(sp, ck, kp, k_in)
            sp.wait_ge(res_ready, 1)
            for h in range(HEADS):
                sp.dma_start(io["mixT"][LRU + h * P:LRU + h * P + P, SEQ:SEQ + NS], res[:, h]).then_inc(stored, 16)
            sp.wait_ge(stored, 16 * HEADS)

        @block.scalar
        def _(act):
            A = nc.scalar
            act.dma_start(ident[:], io["ident"]).then_inc(consts_in, 16)
            act.dma_start(sel[:], io["sel"]).then_inc(consts_in, 16)
            for n, name in enumerate(("lambda_q1", "lambda_k1", "lambda_q2", "lambda_k2")):
                act.dma_start(lam_in[:, n], io[name].broadcast_to([P, HD])).then_inc(consts_in, 16)
            act.dma_start(gain[:], io["subln_g"].rearrange("l (e o) -> (l e) o", o=1)).then_inc(consts_in, 16)
            act.dma_start(q64[:], rows[0].rearrange("b (c d) -> (b c) d", d=HD)).then_inc(consts_in, 16)
            act.dma_start(k64[:], rows[1].rearrange("b (c d) -> (b c) d", d=HD)).then_inc(consts_in, 16)
            act.dma_start(v32[:], rows[2].rearrange("b (h e) -> (b h) e", e=P)).then_inc(consts_in, 16)
            pages(act, cv, vp, v_in)
            act.wait_ge(to_act, 1)
            A.activation(lam_s[:, 2:4], lam_s[:, 0:2], ACT.Exp).then_inc(from_act, 1)
            act.wait_ge(to_act, 2)
            A.activation(pp[:], ST[0:R], ACT.Exp, bias=st[:, 1:2], scale=QSCALE, accum_out=st[:, 2:3])
            A.activation(st[:, 3:4], own[:], ACT.Exp, bias=st[:, 1:2], scale=QSCALE).then_inc(from_act, 1)
            act.wait_ge(from_pe, 2)
            A.activation(cp[:], PT[:, 0:PAGES * R], ACT.Copy)
            A.activation(wnb[:], WB[:, 0:R], ACT.Copy).then_inc(from_act, 1)
            act.wait_ge(from_pe, 4)
            A.activation(ors[:], SS[:, 0:RH], ACT.Sqrt, bias=eps[:], scale=1.0 / P).then_inc(from_act, 1)

        @block.vector
        def _(dve):
            V = nc.vector
            link = Chain(dve, chain)
            V.memset(ones[:], 1.0)
            link(V.memset(eps[:], EPS_SUBLN))
            dve.wait_ge(consts_in, 16 * 10)
            link(V.tensor_tensor(lam_t[:], lam_in[:, 0:4:2], lam_in[:, 1:4:2], ALU.mult))
            V.reduce_sum(lam_s[:, 0:2], lam_t[:], axis=AX).then_inc(to_act, 1)
            dve.wait_ge(from_act, 1)
            link(V.tensor_tensor(nlam[:], lam_s[:, 3:4], lam_s[:, 2:3], ALU.subtract))
            link(V.tensor_scalar(nlam[:], nlam[:], -LAM_INIT, None, ALU.add))
            link(V.tensor_scalar(gain[:], gain[:], 1.0 - LAM_INIT, None, ALU.mult))
            link(V.scalar_tensor_tensor(st[:, 5:6], sel[:, 1:2], nlam[0:R], sel[:, 0:1], ALU.mult, ALU.add))
            link(V.tensor_tensor(q64[:], q64[:], k64[:], ALU.mult))
            link(V.reduce_sum(own[:], q64[:], axis=AX))
            dve.wait_ge(q_in, 16 * NS)
            for b in range(NS):
                dve.wait_ge(k_in[b // 2], 2 * 16 * PAGES)
                link(V.tensor_tensor(prod[:, b % 2], kp[:, b], qb[:, b:b + 1].broadcast_to([P, PAGES, W]), ALU.mult))
                ins = V.reduce_sum(sc[:, :, b * COMP:(b + 1) * COMP], prod[:, b % 2].rearrange("p n (c d) -> p n c d", d=HD), axis=AX)
            ins.then_inc(to_pe, 1)
            dve.wait_ge(from_pe, 1)
            link(V.reduce_max(st[:, 0:1], ST[0:R], axis=AX))
            link(V.tensor_tensor(st[:, 0:1], st[:, 0:1], own[:], ALU.max))
            V.tensor_scalar(st[:, 1:2], st[:, 0:1], -QSCALE, None, ALU.mult).then_inc(to_act, 1)
            dve.wait_ge(from_act, 2)
            link(V.tensor_tensor(st[:, 4:5], st[:, 2:3], st[:, 3:4], ALU.add))
            link(V.reciprocal(st[:, 4:5], st[:, 4:5]))
            link(V.tensor_tensor(st[:, 4:5], st[:, 4:5], st[:, 5:6], ALU.mult))
            V.tensor_scalar(pp[:], pp[:], st[:, 4:5], None, ALU.mult)
            link(V.tensor_tensor(st[:, 6:7], st[:, 3:4], st[:, 4:5], ALU.mult))
            V.tensor_scalar(wn[:], ones[0:R], st[:, 6:7], None, ALU.mult).then_inc(to_pe, 1)
            dve.wait_ge(from_act, 3)
            c4 = cp[:].rearrange("p (n r c) -> p n r c", n=PAGES, c=2)
            V.tensor_tensor(ws[:], c4[:, :, :, 0], c4[:, :, :, 1], ALU.add).then_inc(to_pe, 1)
            w2 = wnb[:].rearrange("p (r c) -> p r c", c=2)
            link(V.tensor_tensor(wo[:], w2[:, :, 0], w2[:, :, 1], ALU.add))
            dve.wait_ge(from_pe, 2)
            link(V.tensor_copy(vT[:], VT[:, 0:RH]))
            link(V.tensor_tensor(wo[:], wo[:], vT[:], ALU.mult))
            dve.wait_ge(from_pe, 3)
            link(V.tensor_tensor(o[:], OT[:, 0:RH], wo[:], ALU.add))
            V.tensor_tensor(osq[:], o[:], o[:], ALU.mult).then_inc(to_pe, 1)
            dve.wait_ge(from_act, 4)
            link(V.reciprocal(ors[:], ors[:]))
            link(V.tensor_tensor(o[:], o[:], ors[:], ALU.mult))
            V.tensor_scalar(res[:].rearrange("p h b -> p b h"), o[:].rearrange("p (b h) -> p b h", h=HEADS), gain[:], None, ALU.mult).then_inc(res_ready, 1)

        @block.tensor
        def _(pe):
            T = nc.tensor
            pe.wait_ge(consts_in, 16 * 10)
            pe.wait_ge(to_pe, 1)
            for n in range(PAGES):
                ins = T.transpose(ST[0:R, n * PAGE:(n + 1) * PAGE], sc[:, n], ident[:])
            ins.then_inc(from_pe, 1)
            pe.wait_ge(to_pe, 2)
            T.transpose(VT[:, 0:RH], v32[:], ident[0:RH, 0:RH])
            for n in range(PAGES):
                T.transpose(PT[:, n * R:(n + 1) * R], pp[:, n * PAGE:(n + 1) * PAGE], ident[0:R, 0:R])
            T.matmul(WB[:, 0:R], wn[:], ident[0:R, 0:R], start=True, stop=True).then_inc(from_pe, 1)
            pe.wait_ge(to_pe, 3)
            for b in range(NS):
                pe.wait_ge(v_in[b // 2], 2 * 16 * PAGES)
                for h in range(HEADS):
                    for n in range(PAGES):
                        ins = T.matmul(OT[:, b * HEADS + h:b * HEADS + h + 1], vp[:, b, n, h * P:(h + 1) * P],
                                       ws[:, n, b * HEADS + h:b * HEADS + h + 1], start=n == 0, stop=n == PAGES - 1)
            ins.then_inc(from_pe, 1)
            pe.wait_ge(to_pe, 4)
            T.matmul(SS[:, 0:RH], ones[:], osq[:], start=True, stop=True).then_inc(from_pe, 1)


def mix_and_feed(nc, io, sems):
    ctx = ExitStack()
    sem = lambda name: sems.enter_context(nc.semaphore(name))
    CH, RING, RAW, AHEAD = 42, 3, 2, 2
    UP0, DOWN0, PROJ, GATE0 = 4, 26, 37, 38
    MIXED = DOWN0 + 5
    FJOBS = FB
    with ctx:
        base = nc.sbuf_base
        base += -base % 64
        top = [base]

        def sb(name, shape, dt=F32, at=None):
            n = int(np.prod(shape[1:])) * (2 if dt == mybir.dt.bfloat16 else 4)
            if at is None:
                at, top[0] = top[0], top[0] + n + -n % 32
            return nc.alloc_sbuf_tensor_at(name, shape, dt, offset=at)

        w = sb("c_w", [P, RING, 2, 2048], F32R)
        raw = sb("c_raw", [P, RAW, 2048])
        h_at = top[0]
        hT = sb("c_hT", [P, 2, KD, WIDE], F32R)
        f_at = top[0]
        fT = sb("c_fT", [P, FB, 2, WIDE], F32R)
        x2T = sb("c_x2T", [P, 2, KD, WIDE], F32R, at=f_at)
        hn = sb("c_hn", [P, 2, D], at=f_at)
        at = f_at + 2 * KD * WIDE * 4
        mix = sb("c_mix", [P, KD, WIDE], at=at)
        at += KD * WIDE * 4
        x1 = sb("c_x1", [P, TILES + 1, D], at=at)
        x2 = sb("c_x2", [P, TILES + 1, D], at=at)
        at += (TILES + 1) * D * 4
        mo = sb("c_mo", [P, TILES + 1, D], at=at)
        pr = sb("c_pr", [P, TILES + 1, D], at=at)
        assert at + (TILES + 1) * D * 4 <= top[0]
        fo = sb("c_fo", [P, TILES + 1, D], at=h_at)
        pT = sb("c_pT", [P, 2, 2, WIDE], F32R)
        xr = sb("c_xr", [P, 2, D])
        gains = sb("c_gains", [P, 2, D])
        act1 = sb("c_act1", [P, 2, WIDE])
        junk = sb("c_junk", [P, D], mybir.dt.bfloat16)
        pin = sb("c_pin", [P, 2, PLE])
        ident = sb("c_ident", [P, P])
        eps = sb("c_eps", [P, 1])
        ss = sb("c_ss", [P, 4, TILES + 1])
        rs = sb("c_rs", [P, 4, TILES + 1])
        assert top[0] <= nc.sbuf_usable_end, (top[0], nc.sbuf_usable_end)
        banks = [ctx.enter_context(nc.psum_tensor(f"c_bank{n}", [P, 512], F32)) for n in range(8)]
        ACC = banks[0:5]
        TB = banks[5:7]
        PB = banks[7]
        consts_in = sem("c_consts_in")
        ready0 = sem("c_eps_written")
        raw_in = [sem(f"c_raw_in{n}") for n in range(RAW)]
        w_hi = sem("c_w_hi")
        w_ready = sem("c_w_ready")
        w_used = sem("c_w_used")
        mix_in = sem("c_mix_in")
        mix_hi = sem("c_mix_hi")
        mix_ready = sem("c_mix_ready")
        xr_in = [sem(f"c_xr_in{n}") for n in range(2)]
        gain_in = [sem(f"c_gain_in{n}") for n in range(2)]
        p_in = [sem(f"c_p_in{n}") for n in range(2)]
        acc_done = sem("c_acc_done")
        acc_free = sem("c_acc_free")
        std = [sem(f"c_std{n}") for n in range(4)]
        act_chain = sem("c_act_chain")
        dve_chain = sem("c_dve_chain")
        mo_ready = sem("c_mo_ready")
        x1_ready = sem("c_x1_ready")
        x1_out = sem("c_x1_out")
        hn_ready = sem("c_hn_ready")
        tp_done = sem("c_transposed")
        t_hi = sem("c_T_hi")
        t_lo = sem("c_T_lo")
        pair_done = sem("c_gate_up_done")
        silu_done = sem("c_silu")
        f_ready = sem("c_f")
        f_hi = sem("c_f_hi")
        f_lo = sem("c_f_lo")
        spair_done = sem("c_sample_gate_up_done")
        ssilu_done = sem("c_sample_silu")
        sf_ready = sem("c_sample_f")
        fo_ready = sem("c_fo_ready")
        x2_ready = sem("c_x2_ready")
        pt_done = sem("c_p_transposed")
        pt_hi = sem("c_pT_hi")
        pt_lo = sem("c_pT_lo")
        proj_done = sem("c_proj_done")
        proj_free = sem("c_proj_free")
        sig_ready = sem("c_sigmoid")
        v_ready = sem("c_v_ready")
        y_ready = sem("c_y_ready")
        y_out = sem("c_y_out")
        pool_turn = sem("c_pool_turn")

        rows = lambda name: io[name][0].rearrange("(k p) n -> p k n", p=P)
        wo, wg, wu, wd, wp, wpg = (rows(n) for n in ("w_out", "ffn_w_gate", "ffn_w_up", "ffn_w_down", "ple_w_proj", "ple_w_gate"))

        def chunk(c):
            if c < UP0:
                return [(wo[:, c % 2 * 4:c % 2 * 4 + 4, c // 2 * 512:c // 2 * 512 + 512], lambda v: v.rearrange("p (k n) -> p k n", n=512))]
            if c < DOWN0:
                b = c - UP0
                return [(s[:, :, b * P:b * P + P], lambda v, n=n: v[:, n * 1024:n * 1024 + 1024].rearrange("p (k n) -> p k n", n=P)) for n, s in enumerate((wg, wu))]
            if c < MIXED:
                return [(wd[:, 4 * (c - DOWN0):4 * (c - DOWN0) + 4, 0:512], lambda v: v.rearrange("p (k n) -> p k n", n=512))]
            if c == MIXED:
                return [(wd[:, 20:22, n * 512:n * 512 + 512], lambda v, n=n: v[:, n * 1024:n * 1024 + 1024].rearrange("p (k n) -> p k n", n=512)) for n in range(2)]
            if c < PROJ:
                b = 4 * (c - MIXED - 1)
                return [(wd[:, b:b + 4, 512:1024], lambda v: v.rearrange("p (k n) -> p k n", n=512))]
            if c == PROJ:
                return [(wp, lambda v: v.rearrange("p (k n) -> p k n", n=1024))]
            g = c - GATE0
            return [(wpg[:, g % 2 * 4:g % 2 * 4 + 4, g // 2 * 512:g // 2 * 512 + 512], lambda v: v.rearrange("p (k n) -> p k n", n=512))]

        DMAS = [len(chunk(c)) for c in range(CH)]

        def arrived(i, c):
            return 16 * (sum(DMAS[c % RAW::RAW]) * i + sum(DMAS[c % RAW:c + 1:RAW]))

        ACCS = 6 * TILES

        def acc_job(i, last, phase, d, t):
            n = TILES + 1 if last else TILES
            return ACCS * i + n * (2 * phase + d) + t + 1

        x_v = io["x_prompt"].rearrange("b (g t p) d -> (b g) t p d", g=GROUPS, p=P)
        y_v = io["y_prompt"].rearrange("b (g t p) d -> (b g) t p d", g=GROUPS, p=P)
        x1_v = io["x1"][0:SEQ].rearrange("(g t p) d -> g t p d", g=GROUPS, p=P)
        p_v = io["p_prompt"].rearrange("l b (g t p) e -> (l b g) t p e", g=GROUPS, p=P)
        mix_v = io["mixT"].rearrange("(k p) t -> p k t", p=P)

        def tile_of(view, sample, i, t):
            return sample if t == TILES else view[i, t]

        x_s = io["x_sample"].rearrange("b s d -> (b s) d")
        y_s = io["y_sample"].rearrange("b s d -> (b s) d")
        p_s = io["p_sample"].rearrange("l b s e -> (l b s) e")
        x1_s = io["x1"][SEQ:SEQ + NS]
        GAINS = ("norm_post_mix", "norm_pre_ffn", "norm_post_ffn", "ple_norm")
        PRJ = (PB, banks[4])
        T_PER = 4 * TILES

        def chunk_used(eng, i, c, last):
            if c < 0:
                if isinstance(i, int) and i == 0:
                    return
                i, c, last = i - 1, c + CH, False
            if c in ENDS:
                phase, d = ENDS[c]
                eng.wait_ge(acc_done, acc_job(i, last, phase, d, TILES if last else TILES - 1))
            elif UP0 <= c < DOWN0:
                eng.wait_ge(pair_done, 2 * FJOBS * i + 2 * (c - UP0) + 2)
                if last:
                    eng.wait_ge(spair_done, 2 * (c - UP0) + 2)
            elif c == PROJ:
                eng.wait_ge(proj_done, 2 * TILES * i + 2 * (TILES + 1 if last else TILES))
            else:
                eng.wait_ge(w_used, len(PLAIN) * i + PLAIN.index(c) + 1)

        ENDS = {1: (0, 0), 3: (0, 1), PROJ - 1: (1, 1), GATE0 + 1: (2, 0), GATE0 + 3: (2, 1)}
        PLAIN = [c for c in range(CH) if c not in ENDS and not UP0 <= c < DOWN0 and c != PROJ]

        block = ctx.enter_context(nc.Block())

        @block.sync
        def _(sp):
            def load(c):
                for src, place in chunk(c):
                    sp.dma_start(place(raw[:, c % RAW]), src).then_inc(raw_in[c % RAW], 16)

            sp.dma_start(mix[:, :, 0:GROUP], mix_v[:, :, 0:GROUP]).then_inc(mix_in, 16)
            for c in range(AHEAD):
                load(c)
            sp.dma_start(ident[:], io["ident"]).then_inc(consts_in, 16)

            def group(i, last):
                for c in range(AHEAD, CH):
                    sp.wait_ge(w_ready, CH * i + c - RAW + 1)
                    load(c)
                if not last:
                    sp.wait_ge(acc_done, acc_job(i, last, 1, 1, TILES - 1))
                    sp.dma_start(mix[:, :, 0:GROUP], mix_v[:, :, bass.ts(i + 1, GROUP)]).then_inc(mix_in, 16)
                    for c in range(AHEAD):
                        sp.wait_ge(w_ready, CH * i + CH + c - RAW + 1)
                        load(c)

            with sp.Fori(0, GROUPS - 2) as i:
                group(i, False)
            group(GROUPS - 2, False)
            sp.dma_start(mix[:, :, GROUP:], mix_v[:, :, SEQ:]).then_inc(mix_in, 16)
            group(GROUPS - 1, True)

        @block.gpsimd
        def _(pool):
            def load(dst, src, arrived):
                pool.sem_inc(pool_turn, 1)
                pool.dma_start(dst, src).then_inc(arrived, 16)

            def load_gain(n):
                load(gains[:, n % 2], io[GAINS[n]].broadcast_to([P, D]), gain_in[n % 2])

            def group(i, last):
                tiles = group_tiles(last)

                def load_rows(t, n, view, sample):
                    load(xr[0:n, t % 2], tile_of(view, sample, i, t), xr_in[t % 2])

                pool.wait_ge(y_ready, TILES * i)
                for n in range(2):
                    load_gain(n)
                for t, _, n in tiles[0:2]:
                    load_rows(t, n, x_v, x_s)
                for t, _, n in tiles:
                    pool.wait_ge(x1_ready, TILES * i + t + 1)
                    load(tile_of(x1_v, x1_s, i, t), x1[0:n, t], x1_out)
                    if t + 2 < len(tiles):
                        load_rows(t + 2, tiles[t + 2][2], x_v, x_s)
                pool.wait_ge(hn_ready, TILES * i + len(tiles))
                for n in range(2, 4):
                    load_gain(n)
                pool.wait_ge(x1_out, 16 * (TILES * i + len(tiles)))
                for t, _, n in tiles[0:2]:
                    load_rows(t, n, x1_v, x1_s)
                for t, _, n in tiles:
                    if t >= 2:
                        pool.wait_ge(pt_done, TILES * i + t - 1)
                    load(pin[0:n, t % 2], tile_of(p_v, p_s, i, t), p_in[t % 2])
                for t, _, n in tiles[2:]:
                    pool.wait_ge(x2_ready, TILES * i + t - 1)
                    load_rows(t, n, x1_v, x1_s)
                for t, _, n in tiles:
                    pool.wait_ge(y_ready, TILES * i + t + 1)
                    load(tile_of(y_v, y_s, i, t), x2[0:n, t], y_out)

            with pool.Fori(0, GROUPS - 1) as i:
                group(i, False)
            group(GROUPS - 1, True)
            pool.wait_ge(y_out, 16 * (TILES * GROUPS + 1))
            pool.wait_ge(x1_out, 16 * (TILES * GROUPS + 1))

        @block.scalar
        def _(act):
            A = nc.scalar
            NORMS = 4 * TILES

            def split(i, c, last):
                act.wait_ge(raw_in[c % RAW], arrived(i, c))
                chunk_used(act, i, c - RING, last)
                A.activation(w[:, c % RING, 0], raw[:, c % RAW], ACT.Copy).then_inc(w_hi, 1)

            def norm(i, link, k, t, n, ready, src):
                act.wait_ge(ready, TILES * i + t + 1)
                link(A.activation(junk[0:n], src[0:n, t], ACT.Square, accum_out=ss[0:n, k, t:t + 1]))
                A.activation(rs[0:n, k, t:t + 1], ss[0:n, k, t:t + 1], ACT.Sqrt, bias=eps[0:n], scale=1.0 / D).then_inc(std[k], 1)

            def hi_halves(i, last, phase, t, col, n, dst):
                for half in range(2):
                    act.wait_ge(tp_done, T_PER * i + 2 * len(group_tiles(last)) * phase + 2 * t + half + 1)
                    A.activation(dst[:, 0, 4 * half:4 * half + 4, col:col + n], TB[half][:, 0:4 * n].rearrange("p (k t) -> p k t", k=4), ACT.Copy).then_inc(t_hi, 1)

            act.wait_ge(ready0, 1)
            act.wait_ge(raw_in[0], 16)
            A.activation(w[:, 0, 0], raw[:, 0], ACT.Copy).then_inc(w_hi, 1)
            act.wait_ge(raw_in[1], 16)
            A.activation(w[:, 1, 0], raw[:, 1], ACT.Copy).then_inc(w_hi, 1)

            def group(i, last):
                tiles = group_tiles(last)
                wide = WIDE if last else GROUP
                link = Chain(act, act_chain, NORMS * i)
                act.wait_ge(mix_in, 16 * (i + 1) + (16 if last else 0))
                act.wait_ge(x2_ready, TILES * i)
                A.activation(hT[:, 0, :, 0:wide], mix[:, :, 0:wide], ACT.Copy).then_inc(mix_hi, 1)
                for c in range(CH):
                    if c + AHEAD < CH:
                        split(i, c + AHEAD, last)
                    elif not last:
                        split(i + 1, c + AHEAD - CH, False)
                    if c == 3:
                        for s in range(len(tiles) + 2):
                            if s < len(tiles):
                                norm(i, link, 0, *tiles[s][::2], mo_ready, mo)
                            if 1 <= s <= len(tiles):
                                norm(i, link, 1, *tiles[s - 1][::2], x1_ready, x1)
                            if s >= 2:
                                hi_halves(i, last, 0, *tiles[s - 2], hT)
                    if UP0 <= c < DOWN0:
                        b = c - UP0
                        act.wait_ge(pair_done, 2 * FJOBS * i + 2 * b + 1)
                        act.wait_ge(f_lo, FJOBS * i + max(b - 1, 0))
                        A.activation(act1[:, b % 2, 0:GROUP], ACC[b % 2 * 2][:], ACT.Silu).then_inc(silu_done, 1)
                        if last:
                            act.wait_ge(spair_done, 2 * b + 1)
                            A.activation(act1[:, b % 2, GROUP:], TB[0][:, 0:NS], ACT.Silu).then_inc(ssilu_done, 1)
                        act.wait_ge(f_ready, FJOBS * i + b + 1)
                        if last:
                            act.wait_ge(sf_ready, b + 1)
                        if b == 0:
                            act.wait_ge(x1_out, 16 * (TILES * i + len(tiles)))
                        A.activation(fT[:, b, 0, 0:wide], act1[:, b % 2, 0:wide], ACT.Copy).then_inc(f_hi, 1)
                    if c == MIXED + 1:
                        for t, col, n in tiles:
                            act.wait_ge(pt_done, TILES * i + t + 1)
                            A.activation(pT[:, 0, :, col:col + n], PB[:, 0:2 * n].rearrange("p (k t) -> p k t", k=2), ACT.Copy).then_inc(pt_hi, 1)
                    if c == PROJ:
                        for s in range(len(tiles) + 3):
                            if s < len(tiles):
                                norm(i, link, 2, *tiles[s][::2], fo_ready, fo)
                                t, _, n = tiles[s]
                                for d in range(2):
                                    act.wait_ge(proj_done, 2 * TILES * i + 2 * t + d + 1)
                                    A.activation(pr[0:n, t, d * 512:d * 512 + 512], PRJ[d][0:n], ACT.Copy).then_inc(proj_free, 1)
                            if s >= 3:
                                hi_halves(i, last, 1, *tiles[s - 3], x2T)
                    if c in (GATE0 + 1, GATE0 + 3):
                        d = (c - GATE0) // 2
                        for t, _, n in tiles:
                            act.wait_ge(acc_done, acc_job(i, last, 2, d, t))
                            act.wait_ge(v_ready, 2 * TILES * i + max(len(tiles) * d + t - 1, 0))
                            A.activation(act1[0:n, (len(tiles) * d + t) % 2, 0:512], ACC[t][0:n], ACT.Sigmoid).then_inc(sig_ready, 1)
                for t, _, n in tiles:
                    act.wait_ge(v_ready, 2 * TILES * i + len(tiles) + t + 1)
                    link(A.activation(junk[0:n], pr[0:n, t], ACT.Square, accum_out=ss[0:n, 3, t:t + 1]))
                    A.activation(rs[0:n, 3, t:t + 1], ss[0:n, 3, t:t + 1], ACT.Sqrt, bias=eps[0:n], scale=1.0 / D).then_inc(std[3], 1)

            with act.Fori(0, GROUPS - 1) as i:
                group(i, False)
            group(GROUPS - 1, True)

        @block.vector
        def _(dve):
            V = nc.vector
            V.memset(eps[:], EPS).then_inc(ready0, 1)

            def split_lo(n, c):
                dve.wait_ge(w_hi, n)
                V.tensor_tensor(w[:, c % RING, 1], raw[:, c % RAW], w[:, c % RING, 0].bitcast(F32), ALU.subtract).then_inc(w_ready, 1)

            for c in range(AHEAD):
                split_lo(c + 1, c)

            def group(i, last, link):
                tiles = group_tiles(last)
                wide = WIDE if last else GROUP
                dve.wait_ge(mix_hi, i + 1)
                V.tensor_tensor(hT[:, 1, :, 0:wide], mix[:, :, 0:wide], hT[:, 0, :, 0:wide].bitcast(F32), ALU.subtract).then_inc(mix_ready, 1)

                def copies(phase, d, dst, ready):
                    for t, _, n in tiles:
                        dve.wait_ge(acc_done, acc_job(i, last, phase, d, t))
                        V.tensor_copy(dst[0:n, t, d * 512:d * 512 + 512], ACC[t][0:n]).then_inc(acc_free, 1)

                def scaled(k, t, n, src, dst):
                    dve.wait_ge(std[k], TILES * i + t + 1)
                    link(V.reciprocal(rs[0:n, k, t:t + 1], rs[0:n, k, t:t + 1]))
                    if t == 0:
                        dve.wait_ge(gain_in[k % 2], 16 * (2 * i + k // 2 + 1))
                    return V.scalar_tensor_tensor(dst, src, rs[0:n, k, t:t + 1], gains[0:n, k % 2], ALU.mult, ALU.mult)

                def lo_halves(phase, t, col, n, dst):
                    for half in range(2):
                        dve.wait_ge(t_hi, T_PER * i + 2 * len(tiles) * phase + 2 * t + half + 1)
                        to = dst[:, :, 4 * half:4 * half + 4, col:col + n]
                        V.tensor_tensor(to[:, 1], TB[half][:, 0:4 * n].rearrange("p (k t) -> p k t", k=4), to[:, 0].bitcast(F32), ALU.subtract).then_inc(t_lo, 1)

                for c in range(CH):
                    if c + AHEAD < CH or not last:
                        split_lo(CH * i + c + AHEAD + 1, (c + AHEAD) % CH)
                    if c == 1:
                        copies(0, 0, mo, None)
                    if c == 3:
                        for s in range(len(tiles) + 2):
                            if s < len(tiles):
                                t, _, n = tiles[s]
                                dve.wait_ge(acc_done, acc_job(i, last, 0, 1, t))
                                link(V.tensor_copy(mo[0:n, t, 512:], ACC[t][0:n]))
                                V.nop().then_inc(mo_ready, 1)
                            if 1 <= s <= len(tiles):
                                t, _, n = tiles[s - 1]
                                if t == 0:
                                    dve.wait_ge(y_out, 16 * TILES * i)
                                link(scaled(0, t, n, mo[0:n, t], mo[0:n, t]))
                                dve.wait_ge(xr_in[t % 2], XR * i + 16 * (t // 2 + 1))
                                V.tensor_tensor(x1[0:n, t], mo[0:n, t], xr[0:n, t % 2], ALU.add).then_inc(x1_ready, 1)
                            if s >= 2:
                                t, col, n = tiles[s - 2]
                                if t >= 2:
                                    dve.wait_ge(tp_done, T_PER * i + 2 * (t - 1))
                                scaled(1, t, n, x1[0:n, t], hn[0:n, t % 2]).then_inc(hn_ready, 1)
                                lo_halves(0, t, col, n, hT)
                    if UP0 <= c < DOWN0:
                        b = c - UP0
                        dve.wait_ge(pair_done, 2 * FJOBS * i + 2 * b + 2)
                        dve.wait_ge(silu_done, FJOBS * i + b + 1)
                        V.tensor_tensor(act1[:, b % 2, 0:GROUP], act1[:, b % 2, 0:GROUP], ACC[b % 2 * 2 + 1][:], ALU.mult).then_inc(f_ready, 1)
                        if last:
                            dve.wait_ge(spair_done, 2 * b + 2)
                            dve.wait_ge(ssilu_done, b + 1)
                            V.tensor_tensor(act1[:, b % 2, GROUP:], act1[:, b % 2, GROUP:], TB[1][:, 0:NS], ALU.mult).then_inc(sf_ready, 1)
                        dve.wait_ge(f_hi, FJOBS * i + b + 1)
                        V.tensor_tensor(fT[:, b, 1, 0:wide], act1[:, b % 2, 0:wide], fT[:, b, 0, 0:wide].bitcast(F32), ALU.subtract).then_inc(f_lo, 1)
                    if c == MIXED:
                        for t, _, n in tiles:
                            dve.wait_ge(acc_done, acc_job(i, last, 1, 0, t))
                            V.tensor_copy(fo[0:n, t, 0:512], ACC[t][0:n]).then_inc(acc_free, 1)
                    if c == MIXED + 1:
                        for t, col, n in tiles:
                            dve.wait_ge(pt_hi, TILES * i + t + 1)
                            V.tensor_tensor(pT[:, 1, :, col:col + n], PB[:, 0:2 * n].rearrange("p (k t) -> p k t", k=2),
                                            pT[:, 0, :, col:col + n].bitcast(F32), ALU.subtract).then_inc(pt_lo, 1)
                    if c == PROJ - 1:
                        for t, _, n in tiles:
                            dve.wait_ge(acc_done, acc_job(i, last, 1, 1, t))
                            link(V.tensor_copy(fo[0:n, t, 512:], ACC[t][0:n]))
                            V.nop().then_inc(fo_ready, 1)
                    if c == PROJ:
                        for s in range(len(tiles) + 3):
                            if s < len(tiles):
                                t, _, n = tiles[s]
                                link(scaled(2, t, n, fo[0:n, t], fo[0:n, t]))
                                if t < 2:
                                    dve.wait_ge(xr_in[t % 2], XR * i + 16 * (len(tiles[t::2]) + 1))
                                else:
                                    dve.wait_ge(xr_in[t % 2], XR * i + 16 * (len(tiles[t % 2::2]) + t // 2 + 1))
                                V.tensor_tensor(x2[0:n, t], fo[0:n, t], xr[0:n, t % 2], ALU.add).then_inc(x2_ready, 1)
                            if s >= 3:
                                t, col, n = tiles[s - 3]
                                lo_halves(1, t, col, n, x2T)
                    if c in (GATE0 + 1, GATE0 + 3):
                        d = (c - GATE0) // 2
                        for t, _, n in tiles:
                            j = len(tiles) * d + t
                            dve.wait_ge(sig_ready, 2 * TILES * i + j + 1)
                            if d == 0:
                                dve.wait_ge(proj_free, 2 * TILES * i + 2 * t + 2)
                            half = pr[0:n, t, d * 512:d * 512 + 512]
                            V.tensor_tensor(half, half, act1[0:n, j % 2, 0:512], ALU.mult).then_inc(v_ready, 1)
                for t, _, n in tiles:
                    link(scaled(3, t, n, pr[0:n, t], pr[0:n, t]))
                    V.tensor_tensor(x2[0:n, t], pr[0:n, t], x2[0:n, t], ALU.add).then_inc(y_ready, 1)

            XR = 64
            LINKS = 9 * TILES
            with dve.Fori(0, GROUPS - 1) as i:
                link = Chain(dve, dve_chain, LINKS * i)
                group(i, False, link)
                assert link.n == LINKS, (link.n, LINKS)
            group(GROUPS - 1, True, Chain(dve, dve_chain, LINKS * (GROUPS - 1)))

        @block.tensor
        def _(pe):
            pe.wait_ge(consts_in, 16)

            def products(out, blocks, lhs, rhs, first=True, end=True):
                for k in range(blocks):
                    for n, (a, b) in enumerate(PRODUCTS):
                        ins = nc.tensor.matmul(out, lhs(k, a), rhs(k, b), start=first and k == 0 and n == 0,
                                               stop=end and k == blocks - 1 and n == 2)
                return ins

            def group(i, last):
                tiles = group_tiles(last)
                per = len(tiles)
                pe.wait_ge(mix_ready, i + 1)

                def transposes(phase, t, n, ready, src, slot):
                    pe.wait_ge(ready, TILES * i + t + 1)
                    for half in range(2):
                        pe.wait_ge(t_lo, T_PER * i + max(2 * per * phase + 2 * t + half - 1, 0))
                        for k in range(4):
                            kk = 4 * half + k
                            ins = nc.tensor.transpose(TB[half][:, k * n:k * n + n], src[0:n, slot, kk * P:kk * P + P], ident[0:n, 0:n])
                        ins.then_inc(tp_done, 1)

                def accumulate(phase, d, blocks, lhs, rhs, first, end, plain):
                    for t, col, n in tiles:
                        if first and (t < TILES or phase or d):
                            pe.wait_ge(acc_free_of(phase, d, t)[0], acc_free_of(phase, d, t)[1])
                        ins = products(ACC[t][0:n], blocks, lambda k, a: lhs(k, a)[:, col:col + n], rhs, first, end)
                        if end:
                            ins.then_inc(acc_done, 1)
                    if not end and plain:
                        ins.then_inc(w_used, 1)

                def acc_free_of(phase, d, t):
                    if phase == 0 and d == 0:
                        return sig_ready, 2 * TILES * i
                    if phase == 0:
                        return acc_free, 2 * TILES * i + t + 1
                    if phase == 1 and d == 0:
                        return (f_ready, FJOBS * (i + 1)) if t < 4 else (mo_ready, TILES * i + per)
                    if phase == 1:
                        return acc_free, 2 * TILES * i + per + t + 1
                    if d == 0:
                        return (fo_ready, TILES * i + t + 1) if t < 4 else (proj_free, 2 * TILES * i + 2 * per)
                    return sig_ready, 2 * TILES * i + t + 1

                for c in range(CH):
                    pe.wait_ge(w_ready, CH * i + c + 1)
                    wv = w[:, c % RING].rearrange("p a (k n) -> p a k n", n=512)
                    if c < UP0:
                        kh = 4 * (c % 2)
                        accumulate(0, c // 2, 4, lambda k, a: hT[:, a, kh + k], lambda k, b: wv[:, b, k], c % 2 == 0, c % 2 == 1, True)
                    if c == UP0 - 1:
                        for t, _, n in tiles:
                            transposes(0, t, n, hn_ready, hn, t % 2)
                        pe.wait_ge(t_lo, T_PER * i + 2 * per)
                    if UP0 <= c < DOWN0:
                        b = c - UP0
                        wb = w[:, c % RING].rearrange("p a (g k n) -> p a g k n", g=2, n=P)
                        for g in range(2):
                            if g == 0:
                                if b >= 2:
                                    pe.wait_ge(f_ready, FJOBS * i + b - 1)
                                else:
                                    pe.wait_ge(mo_ready, TILES * i + per)
                            products(ACC[b % 2 * 2 + g][:], KD, lambda k, a: wb[:, a, g, k], lambda k, r: hT[:, r, k, 0:GROUP]).then_inc(pair_done, 1)
                            if last:
                                if b:
                                    pe.wait_ge(sf_ready, b)
                                products(TB[g][:, 0:NS], KD, lambda k, a: wb[:, a, g, k], lambda k, r: hT[:, r, k, GROUP:]).then_inc(spair_done, 1)
                    if c == DOWN0:
                        pe.wait_ge(f_lo, FJOBS * (i + 1))
                    if DOWN0 <= c < MIXED:
                        kb = 4 * (c - DOWN0)
                        accumulate(1, 0, 4, lambda k, a: fT[:, kb + k, a], lambda k, b: wv[:, b, k], c == DOWN0, False, True)
                    if c == MIXED:
                        accumulate(1, 0, 2, lambda k, a: fT[:, 20 + k, a], lambda k, b: wv[:, b, k], False, True, False)
                        accumulate(1, 1, 2, lambda k, a: fT[:, 20 + k, a], lambda k, b: wv[:, b, 2 + k], True, False, True)
                    if MIXED < c < PROJ:
                        kb = 4 * (c - MIXED - 1)
                        accumulate(1, 1, 4, lambda k, a: fT[:, kb + k, a], lambda k, b: wv[:, b, k], False, c == PROJ - 1, True)
                    if c == MIXED + 1:
                        for t, _, n in tiles:
                            pe.wait_ge(p_in[t % 2], 16 * (2 * i + t // 2 + 1))
                            pe.wait_ge(pt_lo, TILES * i + t)
                            pe.wait_ge(proj_free, 2 * TILES * i)
                            for k in range(2):
                                ins = nc.tensor.transpose(PB[:, k * n:k * n + n], pin[0:n, t % 2, k * P:k * P + P], ident[0:n, 0:n])
                            ins.then_inc(pt_done, 1)
                    if c == PROJ:
                        pe.wait_ge(pt_lo, TILES * i + per)
                        if last:
                            pe.wait_ge(fo_ready, TILES * i + per)
                        wq = w[:, c % RING].rearrange("p a (k d n) -> p a k d n", k=2, d=2)
                        for t, col, n in tiles:
                            for d in range(2):
                                pe.wait_ge(proj_free, 2 * TILES * i + max(2 * t + d - 1, 0))
                                products(PRJ[d][0:n], 2, lambda k, a: pT[:, a, k, col:col + n], lambda k, b: wq[:, b, k, d]).then_inc(proj_done, 1)
                        for t, _, n in tiles:
                            transposes(1, t, n, x2_ready, x2, t)
                        pe.wait_ge(t_lo, T_PER * i + 4 * per)
                    if c >= GATE0:
                        g = c - GATE0
                        kh = 4 * (g % 2)
                        accumulate(2, g // 2, 4, lambda k, a: x2T[:, a, kh + k], lambda k, b: wv[:, b, k], g % 2 == 0, g % 2 == 1, True)

            with pe.Fori(0, GROUPS - 1) as i:
                group(i, False)
            group(GROUPS - 1, True)


def build(nc, io):
    with ExitStack() as sems:
        for stage in (project, attend_prompt, attend_sample, mix_and_feed):
            stage(nc, io, sems)


_INS = ["x_prompt", "x_sample", "cache_k", "cache_v", "state_conv", "state_h", "page_table", "p_prompt", "p_sample",
        "norm_pre_mix", "w_in", "conv_w", "conv_b", "lru_w_a", "lru_b_a", "lru_w_x", "lru_b_x", "lru_L",
        "lambda_q1", "lambda_k1", "lambda_q2", "lambda_k2", "subln_g", "w_out", "norm_post_mix",
        "norm_pre_ffn", "ffn_w_gate", "ffn_w_up", "ffn_w_down", "norm_post_ffn",
        "ple_w_gate", "ple_w_proj", "ple_norm"]
_OUTS = [("y_prompt", (1, SEQ, D)), ("y_sample", (NS, 1, D)),
         ("k_prompt", (1, 1, SEQ, HEADS, P)), ("v_prompt", (1, 1, SEQ, HEADS, P)),
         ("conv_prompt", (1, 1, TAPS - 1, LRU)), ("h_prompt", (1, 1, LRU)),
         ("k_sample", (1, NS, 1, HEADS, P)), ("v_sample", (1, NS, 1, HEADS, P)),
         ("conv_sample", (1, NS, TAPS - 1, LRU)), ("h_sample", (1, NS, LRU))]
_SCRATCH = [("q", (SEQ + NS, LRU)), ("mixT", (D, SEQ + NS)), ("x1", (SEQ + NS, D))]


def _constants():
    inv = np.float32(500000.0) ** (-np.arange(0, ROT, 2, dtype=np.float32) / np.float32(ROT))
    positions = np.concatenate([np.arange(SEQ), np.full(NS, PAGES * PAGE)]).astype(np.float32)
    angle = positions[:, None] * inv[None, :]
    key, query = np.arange(P)[None, :], np.arange(P)[:, None]
    return {
        "rope": np.stack([np.cos(angle), np.sin(angle)], 1).astype(np.float32),
        "ident": np.eye(P, dtype=np.float32),
        "mask": np.where(key > query, np.float32(-1e30), np.float32(0.0)).astype(np.float32),
        "sel": np.tile(np.eye(2, dtype=np.float32), (NS * HEADS, 1)),
    }


def kernel(**inputs):
    import concourse.bacc as _bacc
    from concourse.bass_utils import run_bass_kernel_spmd as _run

    nc = _bacc.Bacc("TRN2", target_bir_lowering=False, num_devices=1, dynamic_dma_scratch_size=4096)
    arrays, io = {}, {}
    for name, a in [(n, inputs[n]) for n in _INS] + list(_constants().items()):
        a = np.ascontiguousarray(a)
        arrays[f"in_{name}"] = a
        io[name] = nc.dram_tensor(f"in_{name}", a.shape, mybir.dt.from_np(a.dtype), kind="ExternalInput").ap()
    for name, shape in _OUTS:
        io[name] = nc.dram_tensor(f"out_{name}", shape, F32, kind="ExternalOutput").ap()
    for name, shape in _SCRATCH:
        io[name] = nc.dram_tensor(f"scratch_{name}", shape, F32, kind="Internal").ap()
    build(nc, io)
    r = _run(nc, [arrays], core_ids=[0])
    return tuple(r.results[0][f"out_{name}"] for name, _ in _OUTS)
```

```python
from contextlib import ExitStack

import numpy as np

import concourse.bass as bass
from concourse import mybir

F32 = mybir.dt.float32
F32R = mybir.dt.float32r
I32 = mybir.dt.int32
ALU = mybir.AluOpType
ACT = mybir.ActivationFunctionType
AX = mybir.AxisListType.X

P = 128
D = 1024
SEQ = 2048
GROUP = 512
GROUPS = SEQ // GROUP
TILES = GROUP // P
NS = 8
WIDE = GROUP + NS
KD = D // P
LRU = 512
LC = LRU // P
TAPS = 4
HEADS = 4
HD = 64
COMP = 2 * HEADS
ROT = HD // 4
HALF = ROT // 2
PAGE = 128
PAGES = 4
FF = 2816
FB = FF // P
PLE = 256
EPS = 1e-6
EPS_SUBLN = 1e-5
LAM_INIT = 0.2
QSCALE = HD ** -0.5

PRODUCTS = ((0, 0), (0, 1), (1, 0))


class Chain:

    def __init__(self, eng, sem, base=0):
        self.eng, self.sem, self.base, self.n = eng, sem, base, 0

    def __call__(self, instruction):
        self.n += 1
        instruction.then_inc(self.sem, 1)
        self.eng.wait_ge(self.sem, self.base + self.n)


def group_tiles(last):
    return [(t, t * P, P) for t in range(TILES)] + ([(TILES, GROUP, NS)] if last else [])


def project(nc, io, sems):
    ctx = ExitStack()
    sb = lambda name, shape, dt=F32: ctx.enter_context(nc.sbuf_tensor(name, shape, dt))
    sem = lambda name: sems.enter_context(nc.semaphore(name))
    CH = 10
    SLOT = (0, 1, 2, 3, 0, 1, 2, 3, 1, 2)
    FREED = [max([b + 1 - (CH if b >= c else 0) for b in range(CH) if SLOT[b] == SLOT[c] and b != c and b < c] or
                 [max(b for b in range(CH) if SLOT[b] == SLOT[c]) + 1 - CH]) for c in range(CH)]
    RAW = 2
    AHEAD = 2
    JOBS = 20
    with ctx:
        ident = sb("a_ident", [P, P])
        gain = sb("a_gain", [P, D])
        convw = sb("a_convw", [P, LC, TAPS])
        convb = sb("a_convb", [P, LC])
        gate_b = sb("a_gate_b", [P, 2, LC])
        gate_w = sb("a_gate_w", [P, 2, LC, P])
        lru_l = sb("a_lru_l", [P, LC])
        sp_t = sb("a_sp_t", [P, 6, LC])
        sp8 = sb("a_sp8", [P, LC])
        nsp8 = sb("a_nsp8", [P, LC])
        eps = sb("a_eps", [P, 1])
        rope = sb("a_rope", [P, SEQ // P, 2, HALF])
        rope_s = sb("a_rope_s", [NS, 2, HALF])
        x = sb("a_x", [P, 2, D])
        junk = sb("a_junk", [P, D], mybir.dt.bfloat16)
        ssq = sb("a_ssq", [P, TILES + 1])
        rstd = sb("a_rstd", [P, TILES + 1])
        hn = sb("a_hn", [P, 2, D])
        hT = sb("a_hT", [P, 2, KD, WIDE], F32R)
        raw = sb("a_raw", [P, RAW, 2048])
        w = sb("a_w", [P, max(SLOT) + 1, 2, 2048], F32R)
        xpad = sb("a_xpad", [P, LC, TAPS - 1 + GROUP])
        xc = sb("a_xc", [P, LC, GROUP])
        gg = sb("a_gg", [P, LC, GROUP])
        ri = sb("a_ri", [P, 2, GROUP])
        u = sb("a_u", [P, GROUP])
        aa = sb("a_aa", [P, 2, GROUP])
        rec = sb("a_rec", [P, GROUP])
        qq = sb("a_qq", [P, GROUP])
        igx = sb("a_igx", [P, 2, GROUP])
        sq = sb("a_sq", [P, GROUP])
        hs = sb("a_hs", [P, 2, GROUP])
        hlast = sb("a_hlast", [P, LC])
        lo_out = sb("a_lo_out", [P, 2, GROUP])
        rows = sb("a_rows", [P, 3, 512])
        rt = sb("a_rt", [P, 4, COMP, HALF])
        s_xl = sb("a_s_xl", [P, LC, NS])
        s_gg = sb("a_s_gg", [P, LC, NS])
        s_conv = sb("a_s_conv", [P, LC, TAPS - 1, NS])
        s_h = sb("a_s_h", [P, LC, NS])
        s_w = sb("a_s_w", [P, 12, LC, NS])
        s_ri = sb("a_s_ri", [P, 2, LC, NS])
        banks = [ctx.enter_context(nc.psum_tensor(f"a_bank{n}", [P, 512], F32)) for n in range(8)]
        TB = banks[0:2]
        ACC = banks[2:6]
        SB_, GB = banks[6], (banks[7], banks[0])
        consts_in = sem("a_consts_in")
        ready0 = sem("a_memsets")
        eps_ready = sem("a_eps_ready")
        sp_chain_a = sem("a_softplus_act")
        sp_ready = sem("a_softplus_ready")
        x_in = [sem(f"a_x_in{n}") for n in range(2)]
        act_chain = sem("a_act_chain")
        dve_chain = sem("a_dve_chain")
        std_ready = sem("a_std_ready")
        hn_ready = sem("a_hn_ready")
        tp_done = sem("a_transposed")
        hi_ready = sem("a_hT_hi")
        lo_ready = sem("a_hT_ready")
        raw_in = [sem(f"a_raw_in{n}") for n in range(RAW)]
        w_hi = sem("a_w_hi")
        w_ready = sem("a_w_ready")
        half_used = sem("a_half_used")
        job_done = sem("a_job_done")
        job_free = sem("a_job_free")
        sjob_done = sem("a_sample_job_done")
        sjob_free = sem("a_sample_job_free")
        xc_ready = sem("a_xc_ready")
        gate_done = sem("a_gate_done")
        gate_free = sem("a_gate_free")
        tanh_ready = sem("a_tanh_ready")
        quot_ready = sem("a_quotient_ready")
        root_ready = sem("a_root_ready")
        lru_done = sem("a_lru_done")
        rows_ready = sem("a_rows_ready")
        rows_out = [sem(f"a_rows_out{n}") for n in range(3)]
        lru_out = [sem(f"a_lru_out{n}") for n in range(2)]
        small_in = sem("a_small_in")
        small_ready = sem("a_small_ready")
        small_out = sem("a_small_out")
        pool_turn = sem("a_pool_turn")
        s_chain = sem("a_s_act_chain")
        s_xc_ready = sem("a_s_xc_ready")
        s_gate_done = sem("a_s_gate_done")
        s_r_ready = sem("a_s_r_ready")
        s_u_ready = sem("a_s_u_ready")
        s_t_ready = sem("a_s_t_ready")
        s_q_ready = sem("a_s_q_ready")
        s_root = sem("a_s_root")

        x_v = io["x_prompt"].rearrange("b (g t p) d -> (b g) t p d", g=GROUPS, p=P)
        w_v = io["w_in"][0].rearrange("(k p) n -> p k n", p=P)

        def chunk(c):
            return w_v[:, :, c * 256:c * 256 + 256] if c < 4 else (
                w_v[:, (c % 2) * 4:(c % 2) * 4 + 4, 1024 + (c - 4) // 2 * 512:1536 + (c - 4) // 2 * 512])

        def width(c):
            return 256 if c < 4 else 512

        def job_bank(j):
            return ACC[j % 4]

        q_v = io["q"][0:SEQ].rearrange("(g t p) n -> g t p n", g=GROUPS, p=P)
        k_v = io["k_prompt"].rearrange("l b (g t p) h e -> (l b g) t p (h e)", g=GROUPS, p=P)
        v_v = io["v_prompt"].rearrange("l b (g t p) h e -> (l b g) t p (h e)", g=GROUPS, p=P)
        s_rows = [io["q"][SEQ:SEQ + NS], io["k_sample"].rearrange("l b s h e -> (l b s) (h e)"),
                  io["v_sample"].rearrange("l b s h e -> (l b s) (h e)")]
        mix_v = io["mixT"][0:LRU].rearrange("(c p) t -> c p t", p=P)

        block = ctx.enter_context(nc.Block())

        @block.sync
        def _(sp):
            sp.dma_start(x[:, 0], x_v[0, 0]).then_inc(x_in[0], 16)
            sp.dma_start(gain[:], io["norm_pre_mix"].broadcast_to([P, D])).then_inc(consts_in, 16)
            sp.dma_start(ident[:], io["ident"]).then_inc(consts_in, 16)
            sp.dma_start(x[:, 1], x_v[0, 1]).then_inc(x_in[1], 16)
            for c in range(AHEAD):
                sp.dma_start(raw[:, c].rearrange("p (k n) -> p k n", n=width(c)), chunk(c)).then_inc(raw_in[c], 16)
            sp.dma_start(rope[:], io["rope"][0:SEQ].rearrange("(t p) a f -> p t a f", p=P)).then_inc(consts_in, 16)
            sp.dma_start(rope_s[:], io["rope"][SEQ:SEQ + NS]).then_inc(consts_in, 16)
            with nc.allow_non_contiguous_dma("a few vectors, channels onto partitions"):
                for c in range(LC):
                    sp.dma_start(convw[:, c], io["conv_w"][0, :, c * P:(c + 1) * P].rearrange("j p -> p j")).then_inc(consts_in, 16)
                sp.dma_start(convb[:], io["conv_b"][0].rearrange("(c p) -> p c", p=P)).then_inc(consts_in, 16)
                sp.dma_start(lru_l[:], io["lru_L"][0].rearrange("(c p) -> p c", p=P)).then_inc(consts_in, 16)
                for n, name in enumerate(("lru_b_a", "lru_b_x")):
                    sp.dma_start(gate_b[:, n], io[name][0].rearrange("(c h) j -> (h j) c", h=2)).then_inc(consts_in, 16)
                sp.wait_ge(ready0, 1)
                for n, name in enumerate(("lru_w_a", "lru_w_x")):
                    for h in range(2):
                        sp.dma_start(gate_w[h * 64:h * 64 + 64, n, :, h * 64:h * 64 + 64],
                                     io[name][0].rearrange("(c h) i j -> h i c j", h=2)[h]).then_inc(consts_in, 16)
                for c in range(LC):
                    for j in range(TAPS - 1):
                        sp.dma_start(s_conv[:, c, j], io["state_conv"][0, :, j, c * P:(c + 1) * P].rearrange("b p -> p b")).then_inc(small_in, 16)
                    sp.dma_start(s_h[:, c], io["state_h"][0, :, c * P:(c + 1) * P].rearrange("b p -> p b")).then_inc(small_in, 16)

            def group(i, last):
                for t, _, n in group_tiles(last):
                    if last or t >= 2:
                        sp.wait_ge(hn_ready, 4 * i + t - 1)
                    if last and t == TILES:
                        sp.dma_start(x[0:n, 0], io["x_sample"].rearrange("b s d -> (b s) d")).then_inc(x_in[0], 16)
                    elif t >= 2:
                        sp.dma_start(x[:, t % 2], x_v[i, t]).then_inc(x_in[t % 2], 16)
                for c in range(AHEAD, CH):
                    sp.wait_ge(w_ready, CH * i + c - RAW + 1)
                    sp.dma_start(raw[:, c % RAW].rearrange("p (k n) -> p k n", n=width(c)), chunk(c)).then_inc(raw_in[c % RAW], 16)
                if not last:
                    for t in range(2):
                        sp.wait_ge(hn_ready, 4 * i + t + 3)
                        sp.dma_start(x[:, t], x_v[i + 1, t]).then_inc(x_in[t], 16)
                    for c in range(AHEAD):
                        sp.wait_ge(w_ready, CH * i + CH + c - RAW + 1)
                        sp.dma_start(raw[:, c].rearrange("p (k n) -> p k n", n=width(c)), chunk(c)).then_inc(raw_in[c], 16)

            with sp.Fori(0, GROUPS - 1) as i:
                group(i, False)
            group(GROUPS - 1, True)

        @block.gpsimd
        def _(pool):
            pool.memset(gate_w[:], 0.0).then_inc(ready0, 1)

            def group(i, last):
                for which in range(3):
                    for t, _, n in group_tiles(last):
                        r = 4 * which + t
                        if t < TILES:
                            pool.wait_ge(rows_ready, 12 * i + r + 1 + (which if last else 0))
                            slot = (12 * 3 + r + which) % 3 if last else r % 3
                            dst = (q_v, k_v, v_v)[which][i, t]
                        else:
                            pool.wait_ge(rows_ready, 12 * i + 4 * which + which + TILES + 1)
                            slot = (12 * 3 + 4 * which + which + TILES) % 3
                            dst = s_rows[which]
                        pool.sem_inc(pool_turn, 1)
                        pool.dma_start(dst, rows[0:n, slot]).then_inc(rows_out[slot], 16)
                    if which >= 1:
                        for g in ((0, 1), (2, 3))[which - 1]:
                            pool.wait_ge(lru_done, LC * i + g + 1)
                            pool.sem_inc(pool_turn, 1)
                            pool.dma_start(mix_v[g, :, bass.ts(i, GROUP)], lo_out[:, g % 2]).then_inc(lru_out[g % 2], 16)

            with pool.Fori(0, GROUPS - 1) as i:
                group(i, False)
            group(GROUPS - 1, True)
            with nc.allow_non_contiguous_dma("states, a few thousand values"):
                pool.wait_ge(small_ready, 2)
                for c in range(LC):
                    ch = slice(c * P, (c + 1) * P)
                    pool.dma_start(io["conv_prompt"][0, 0, :, ch].rearrange("j p -> p j"), xpad[:, c, GROUP:GROUP + 3]).then_inc(small_out, 16)
                    pool.dma_start(io["conv_sample"][0, :, 0, ch].rearrange("b p -> p b"), s_conv[:, c, 1]).then_inc(small_out, 16)
                    pool.dma_start(io["conv_sample"][0, :, 1, ch].rearrange("b p -> p b"), s_conv[:, c, 2]).then_inc(small_out, 16)
                    pool.dma_start(io["conv_sample"][0, :, 2, ch].rearrange("b p -> p b"), s_xl[:, c]).then_inc(small_out, 16)
                    pool.dma_start(io["h_sample"][0, :, ch].rearrange("b p -> p b"), s_w[:, 10, c]).then_inc(small_out, 16)
                    pool.dma_start(io["mixT"][ch, SEQ:SEQ + NS], s_w[:, 11, c]).then_inc(small_out, 16)
                pool.dma_start(io["h_prompt"][0, 0].rearrange("(c p) -> p c", p=P), hlast[:]).then_inc(small_out, 16)
            pool.wait_ge(small_out, 16 * (6 * LC + 1))
            for n in range(3):
                pool.wait_ge(rows_out[n], 16 * 17)
            for n in range(2):
                pool.wait_ge(lru_out[n], 16 * 2 * GROUPS)

        def chunk_used(eng, i, n, last):
            before, c = ((i - 1), n - 1 + CH) if n <= 0 else (i, n - 1)
            which = (c - 4) // 2
            if c >= 4 and c % 2 == 0:
                eng.wait_ge(half_used, 3 * before + which + 1)
            else:
                eng.wait_ge(job_done, JOBS * before + (2 * c + 2 if c < 4 else 8 + 4 * which + 4))
                if last and n > 0:
                    eng.wait_ge(sjob_done, 2 * c + 2 if c < 4 else 8 + which + 1)

        def row_slot(i, last, which, t):
            if last:
                r = 36 + 5 * which + t
                return r % 3, r, r // 3
            r = 4 * which + t
            return r % 3, 12 * i + r, 4 * i + r // 3

        @block.scalar
        def _(act):
            def split_first(c):
                act.wait_ge(raw_in[c], 16)
                nc.scalar.activation(w[:, c, 0], raw[:, c], ACT.Copy).then_inc(w_hi, 1)

            def root(i, g):
                act.wait_ge(quot_ready, LC * i + g + 1)
                act.wait_ge(lru_done, LC * i + g)
                nc.scalar.activation(sq[:], qq[:], ACT.Sqrt, scale=2.0).then_inc(root_ready, 1)

            act.wait_ge(sp_chain_a, 1)
            nc.scalar.activation(sp_t[:, 1], sp_t[:, 0], ACT.Exp, scale=-1.0).then_inc(eps_ready, 1)
            act.wait_ge(sp_chain_a, 2)
            nc.scalar.activation(sp_t[:, 3], sp_t[:, 2], ACT.Ln).then_inc(eps_ready, 1)
            for c in range(AHEAD):
                split_first(c)

            def group(i, last):
                for t, col, n in group_tiles(last):
                    act.wait_ge(x_in[t % 2], 16 * (2 * i + t // 2 + 1))
                    nc.scalar.activation(junk[0:n], x[0:n, t % 2], ACT.Square, accum_out=ssq[0:n, t:t + 1]).then_inc(act_chain, 1)
                    act.wait_ge(act_chain, 4 * i + t + 1)
                    nc.scalar.activation(ssq[0:n, t:t + 1], ssq[0:n, t:t + 1], ACT.Sqrt, bias=eps[0:n], scale=1.0 / D).then_inc(std_ready, 1)
                    if t >= 1:
                        hi_halves(i, t - 1, col - P, P)
                hi_halves(i, t, col, n)
                for c in range(CH):
                    if c + AHEAD < CH:
                        split_in(i, c + AHEAD, last)
                    elif not last:
                        split_in(i + 1, c + AHEAD - CH, False)
                    if c < 4:
                        for f in range(2):
                            j, fc = 2 * c + f, (2 * c + f) % 4
                            act.wait_ge(job_done, JOBS * i + j + 1)
                            if c < 2:
                                act.wait_ge(xc_ready, LC * i)
                                nc.scalar.activation(xpad[:, fc, 3:], job_bank(j)[:], ACT.Copy).then_inc(job_free, 1)
                            else:
                                act.wait_ge(lru_done, LC * i)
                                nc.scalar.activation(gg[:, fc], job_bank(j)[:], ACT.Gelu_apprx_tanh).then_inc(job_free, 1)
                            if last:
                                act.wait_ge(sjob_done, j + 1)
                                if c < 2:
                                    nc.scalar.activation(s_xl[:, fc], SB_[:, 0:NS], ACT.Copy).then_inc(sjob_free, 1)
                                else:
                                    nc.scalar.activation(s_gg[:, fc], SB_[:, 0:NS], ACT.Gelu_apprx_tanh).then_inc(sjob_free, 1)
                    if c >= 6 and c < 10:
                        root(i, c - 6)
                    if c >= 5 and c % 2 == 1:
                        which = (c - 5) // 2
                        for t, _, n in group_tiles(last):
                            slot, before, uses = row_slot(i, last, which, t)
                            act.wait_ge(rows_out[slot], 16 * uses)
                            if t < TILES:
                                act.wait_ge(job_done, JOBS * i + 8 + 4 * which + t + 1)
                                nc.scalar.activation(rows[:, slot], ACC[t][:], ACT.Copy).then_inc(job_free, 1)
                            else:
                                act.wait_ge(sjob_done, 8 + which + 1)
                                nc.scalar.activation(rows[0:n, slot], SB_[0:n], ACT.Copy).then_inc(sjob_free, 1)
                    if c >= 5 and c < 9:
                        gates(i, c - 5)
                if last:
                    sample_gates()

            def hi_halves(i, t, col, n):
                for half in range(2):
                    if t == 0 and half == 0:
                        act.wait_ge(job_done, JOBS * i)
                    act.wait_ge(tp_done, 8 * i + 2 * t + half + 1)
                    nc.scalar.activation(hT[:, 0, 4 * half:4 * half + 4, col:col + n],
                                         TB[half][:, 0:4 * n].rearrange("p (k t) -> p k t", k=4), ACT.Copy).then_inc(hi_ready, 1)

            def split_in(i, c, last):
                act.wait_ge(raw_in[c % RAW], 16 * (CH // RAW * i + c // RAW + 1))
                chunk_used(act, i, FREED[c] if c < AHEAD else max(FREED[c], 0), last)
                nc.scalar.activation(w[:, SLOT[c], 0], raw[:, c % RAW], ACT.Copy).then_inc(w_hi, 1)

            def gates(i, g):
                act.wait_ge(gate_done, LC * i + g + 1)
                act.wait_ge(quot_ready, LC * i + g)
                nc.scalar.activation(ri[:, 0], GB[0][:], ACT.Sigmoid, bias=gate_b[:, 0, g:g + 1]).then_inc(gate_free, 1)
                nc.scalar.activation(ri[:, 1], GB[1][:], ACT.Sigmoid, bias=gate_b[:, 1, g:g + 1]).then_inc(gate_free, 1)
                act.wait_ge(gate_free, 2 * (LC * i + g + 1))
                nc.scalar.activation(u[:], ri[:, 0], ACT.Tanh, scale=sp8[:, g:g + 1])
                act.wait_ge(lru_done, LC * i + max(g - 1, 0))
                nc.scalar.activation(aa[:, g % 2], ri[:, 0], ACT.Exp, scale=nsp8[:, g:g + 1]).then_inc(tanh_ready, 1)

            def sample_gates():
                act.wait_ge(s_r_ready, 1)
                nc.scalar.activation(s_ri[:], s_ri[:], ACT.Sigmoid).then_inc(s_chain, 1)
                act.wait_ge(s_t_ready, 1)
                nc.scalar.activation(s_w[:, 1], s_w[:, 0], ACT.Tanh)
                nc.scalar.activation(s_w[:, 2], s_w[:, 0], ACT.Exp, scale=-1.0).then_inc(s_chain, 1)
                act.wait_ge(s_q_ready, 1)
                nc.scalar.activation(s_w[:, 6], s_w[:, 5], ACT.Sqrt, scale=2.0).then_inc(s_chain, 1)

            act.wait_ge(sp_ready, 1)
            with act.Fori(0, GROUPS - 1) as i:
                group(i, False)
            group(GROUPS - 1, True)

        @block.vector
        def _(dve):
            N_CONST = 4 + LC + 4 + 4
            V = nc.vector
            V.memset(eps[:], EPS)
            V.memset(hlast[:], 0.0)
            V.memset(xpad[:], 0.0)
            link = Chain(dve, dve_chain)
            dve.wait_ge(consts_in, 16 * N_CONST)
            link(V.tensor_scalar(sp_t[:, 4], lru_l[:], -1.0, None, ALU.mult))
            V.tensor_tensor(sp_t[:, 0], sp_t[:, 4], lru_l[:], ALU.max).then_inc(sp_chain_a, 1)
            dve.wait_ge(eps_ready, 1)
            link(V.tensor_scalar(sp_t[:, 2], sp_t[:, 1], 1.0, None, ALU.add))
            V.tensor_scalar(sp_t[:, 5], sp_t[:, 2], -1.0, 1e-30, ALU.add, ALU.max).then_inc(sp_chain_a, 1)
            dve.wait_ge(eps_ready, 2)
            dve.wait_ge(sp_chain_a, 2)
            link(V.reciprocal(sp8[:], sp_t[:, 5]))
            link(V.tensor_tensor(sp8[:], sp8[:], sp_t[:, 3], ALU.mult))
            link(V.tensor_scalar(sp_t[:, 5], sp_t[:, 2], 1.0, None, ALU.is_equal))
            link(V.tensor_tensor(sp8[:], sp8[:], sp_t[:, 5], ALU.add))
            link(V.tensor_tensor(sp8[:], sp8[:], sp_t[:, 1], ALU.mult))
            link(V.tensor_scalar(sp_t[:, 4], sp_t[:, 4], 0.0, None, ALU.max))
            link(V.tensor_tensor(sp8[:], sp8[:], sp_t[:, 4], ALU.add))
            link(V.tensor_scalar(sp8[:], sp8[:], 8.0, None, ALU.mult))
            V.tensor_scalar(nsp8[:], sp8[:], -1.0, None, ALU.mult).then_inc(sp_ready, 1)
            links0 = link.n
            LINKS = 64

            def split_lo(n, c):
                dve.wait_ge(w_hi, n)
                V.tensor_tensor(w[:, SLOT[c], 1], raw[:, c % RAW], w[:, SLOT[c], 0].bitcast(F32), ALU.subtract).then_inc(w_ready, 1)

            for c in range(AHEAD):
                split_lo(c + 1, c)

            def lru_head(i, g):
                dve.wait_ge(tanh_ready, LC * i + g + 1)
                link(V.tensor_scalar(rec[:], u[:], 1.0, None, ALU.add))
                link(V.reciprocal(rec[:], rec[:]))
                V.tensor_tensor(igx[:, g % 2], ri[:, 1], xc[:, g], ALU.mult)
                link(V.tensor_tensor(qq[:], u[:], rec[:], ALU.mult))
                V.nop().then_inc(quot_ready, 1)

            def lru_tail(i, g):
                dve.wait_ge(root_ready, LC * i + g + 1)
                link(V.tensor_tensor(igx[:, g % 2], sq[:], igx[:, g % 2], ALU.mult))
                link(V.tensor_tensor_scan(hs[:, g % 2], aa[:, g % 2], igx[:, g % 2], hlast[:, g:g + 1], ALU.mult, ALU.add))
                V.tensor_copy(hlast[:, g:g + 1], hs[:, g % 2, GROUP - 1:GROUP])
                dve.wait_ge(lru_out[g % 2], 16 * (2 * i + g // 2))
                link(V.tensor_tensor(lo_out[:, g % 2], hs[:, g % 2], gg[:, g], ALU.mult))
                V.nop().then_inc(lru_done, 1)

            def group(i, last):
                for t, col, n in group_tiles(last):
                    dve.wait_ge(std_ready, 4 * i + t + 1)
                    link(V.reciprocal(rstd[0:n, t:t + 1], ssq[0:n, t:t + 1]))
                    if t >= 2:
                        dve.wait_ge(tp_done, 8 * i + 2 * (t - 1))
                    else:
                        dve.wait_ge(tp_done, 8 * i)
                    V.scalar_tensor_tensor(hn[0:n, t % 2], x[0:n, t % 2], rstd[0:n, t:t + 1], gain[0:n], ALU.mult, ALU.mult).then_inc(hn_ready, 1)
                    if t >= 1:
                        lo_halves(i, t - 1, col - P, P)
                lo_halves(i, t, col, n)
                for c in range(CH):
                    if c + AHEAD < CH:
                        split_lo(CH * i + c + AHEAD + 1, (c + AHEAD) % CH)
                    elif not last:
                        split_lo(CH * i + c + AHEAD + 1, (c + AHEAD) % CH)
                    if c < 2:
                        for f in range(2):
                            fc = 2 * c + f
                            dve.wait_ge(job_free, JOBS * i + fc + 1)
                            link(V.tensor_scalar(xc[:, fc], xpad[:, fc, 0:GROUP], convw[:, fc, 0:1], convb[:, fc:fc + 1], ALU.mult, ALU.add))
                            for j in range(1, TAPS):
                                link(V.scalar_tensor_tensor(xc[:, fc], xpad[:, fc, j:j + GROUP], convw[:, fc, j:j + 1], xc[:, fc], ALU.mult, ALU.add))
                            if not last:
                                link(V.tensor_copy(xpad[:, fc, 0:3], xpad[:, fc, GROUP:GROUP + 3]))
                            V.nop().then_inc(xc_ready, 1)
                    if c == 3 and last:
                        sample_conv()
                    if c >= 5 and c % 2 == 1:
                        which = (c - 5) // 2
                        for t, _, n in group_tiles(last):
                            slot, before, uses = row_slot(i, last, which, t)
                            if t < TILES:
                                dve.wait_ge(job_free, JOBS * i + 8 + 4 * which + t + 1)
                            else:
                                dve.wait_ge(sjob_free, 8 + which + 1)
                            if which < 2:
                                v = rows[0:n, slot].rearrange("p (c d) -> p c d", d=HD)
                                t1, t2 = v[:, :, 0:HALF], v[:, :, HALF:ROT]
                                table = rope[:, 4 * i + t] if t < TILES and isinstance(i, int) else (rope[:, bass.ds(4 * i + t, 1)].rearrange("p o a f -> p (o a) f") if t < TILES else rope_s[:])
                                cos = table[:, 0:1, :].broadcast_to([n, COMP, HALF])
                                sin = table[:, 1:2, :].broadcast_to([n, COMP, HALF])
                                V.tensor_tensor(rt[0:n, 0], t1, cos, ALU.mult)
                                V.tensor_tensor(rt[0:n, 1], t2, sin, ALU.mult)
                                V.tensor_tensor(rt[0:n, 2], t2, cos, ALU.mult)
                                link(V.tensor_tensor(rt[0:n, 3], t1, sin, ALU.mult))
                                V.tensor_tensor(t1, rt[0:n, 0], rt[0:n, 1], ALU.subtract)
                                link(V.tensor_tensor(t2, rt[0:n, 2], rt[0:n, 3], ALU.add))
                            V.nop().then_inc(rows_ready, 1)
                    if c >= 6:
                        lru_tail(i, c - 6)
                    if c >= 5 and c < 9:
                        lru_head(i, c - 5)
                if last:
                    sample_lru()
                    V.nop().then_inc(small_ready, 1)

            def lo_halves(i, t, col, n):
                for half in range(2):
                    dve.wait_ge(hi_ready, 8 * i + 2 * t + half + 1)
                    dst = hT[:, :, 4 * half:4 * half + 4, col:col + n]
                    V.tensor_tensor(dst[:, 1], TB[half][:, 0:4 * n].rearrange("p (k t) -> p k t", k=4),
                                    dst[:, 0].bitcast(F32), ALU.subtract).then_inc(lo_ready, 1)

            def over(v):
                return v.rearrange("p (c o) -> p c o", o=1).broadcast_to([P, LC, NS])

            def sample_conv():
                dve.wait_ge(small_in, 16 * 4 * LC)
                dve.wait_ge(sjob_free, 4)
                link(V.tensor_tensor(s_w[:, 0], s_conv[:, :, 0], over(convw[:, :, 0]), ALU.mult))
                link(V.tensor_tensor(s_w[:, 7], s_w[:, 0], over(convb[:]), ALU.add))
                for j in range(1, TAPS):
                    tap = s_conv[:, :, j] if j < 3 else s_xl[:]
                    link(V.tensor_tensor(s_w[:, 0], tap, over(convw[:, :, j]), ALU.mult))
                    link(V.tensor_tensor(s_w[:, 7], s_w[:, 7], s_w[:, 0], ALU.add))
                V.nop().then_inc(s_xc_ready, 1)

            def sample_lru():
                dve.wait_ge(s_gate_done, 1)
                V.tensor_tensor(s_ri[:, 0], GB[0][:, 0:LC * NS].rearrange("p (c b) -> p c b", b=NS), over(gate_b[:, 0]), ALU.add)
                link(V.tensor_tensor(s_ri[:, 1], GB[1][:, 0:LC * NS].rearrange("p (c b) -> p c b", b=NS), over(gate_b[:, 1]), ALU.add))
                V.nop().then_inc(s_r_ready, 1)
                dve.wait_ge(s_chain, 1)
                link(V.tensor_tensor(s_w[:, 0], s_ri[:, 0], over(sp8[:]), ALU.mult))
                V.nop().then_inc(s_t_ready, 1)
                link(V.tensor_tensor(s_w[:, 8], s_ri[:, 1], s_w[:, 7], ALU.mult))
                dve.wait_ge(s_chain, 2)
                link(V.tensor_scalar(s_w[:, 3], s_w[:, 1], 1.0, None, ALU.add))
                link(V.reciprocal(s_w[:, 4], s_w[:, 3]))
                link(V.tensor_tensor(s_w[:, 5], s_w[:, 1], s_w[:, 4], ALU.mult))
                V.nop().then_inc(s_q_ready, 1)
                link(V.tensor_tensor(s_w[:, 9], s_w[:, 2], s_h[:], ALU.mult))
                dve.wait_ge(s_chain, 3)
                link(V.tensor_tensor(s_w[:, 8], s_w[:, 8], s_w[:, 6], ALU.mult))
                link(V.tensor_tensor(s_w[:, 10], s_w[:, 8], s_w[:, 9], ALU.add))
                dve.wait_ge(sjob_free, 8)
                link(V.tensor_tensor(s_w[:, 11], s_w[:, 10], s_gg[:], ALU.mult))
                V.nop().then_inc(small_ready, 1)

            with dve.Fori(0, GROUPS - 1) as i:
                link = Chain(dve, dve_chain, LINKS * i + links0)
                group(i, False)
                assert link.n == LINKS, link.n
            link = Chain(dve, dve_chain, LINKS * (GROUPS - 1) + links0)
            group(GROUPS - 1, True)

        @block.tensor
        def _(pe):
            pe.wait_ge(consts_in, 16 * 16)

            def products(out, blocks, lhs, rhs, first=True, end=True):
                for k in range(blocks):
                    for n, (a, b) in enumerate(PRODUCTS):
                        ins = nc.tensor.matmul(out, lhs(k, a), rhs(k, b), start=first and k == 0 and n == 0,
                                               stop=end and k == blocks - 1 and n == 2)
                return ins

            def group(i, last):
                pe.wait_ge(gate_free, 2 * LC * i)
                for t, col, n in group_tiles(last):
                    pe.wait_ge(hn_ready, 4 * i + t + 1)
                    for half in range(2):
                        pe.wait_ge(lo_ready, 8 * i + 2 * t + half - 1 if t else 8 * i)
                        for k in range(4):
                            kk = 4 * half + k
                            ins = nc.tensor.transpose(TB[half][:, k * n:k * n + n], hn[0:n, t % 2, kk * P:kk * P + P], ident[0:n, 0:n])
                        ins.then_inc(tp_done, 1)
                pe.wait_ge(lo_ready, 8 * i + 2 * len(group_tiles(last)))
                for c in range(CH):
                    s = SLOT[c]
                    pe.wait_ge(w_ready, CH * i + c + 1)
                    wv = w[:, s].rearrange("p a (k n) -> p a k n", n=width(c))
                    if c < 4:
                        for f in range(2):
                            j = 2 * c + f
                            pe.wait_ge(job_free, JOBS * i + max(j - 3, 0))
                            ins = products(job_bank(j)[:], KD, lambda k, a: wv[:, a, k, f * P:f * P + P],
                                     lambda k, b: hT[:, b, k, 0:GROUP])
                            ins.then_inc(job_done, 1)
                            if last:
                                if j:
                                    pe.wait_ge(sjob_free, j)
                                ins = products(SB_[:, 0:NS], KD, lambda k, a: wv[:, a, k, f * P:f * P + P],
                                         lambda k, b: hT[:, b, k, GROUP:WIDE])
                                ins.then_inc(sjob_done, 1)
                    else:
                        which, kh = (c - 4) // 2, c % 2
                        for t, col, n in group_tiles(last):
                            if kh == 0:
                                if t < TILES:
                                    pe.wait_ge(job_free, JOBS * i + 8 + 4 * which + t - 3)
                                else:
                                    pe.wait_ge(sjob_free, 8 + which)
                            out = ACC[t][:] if t < TILES else SB_[0:n]
                            ins = products(out, 4, lambda k, a: hT[:, a, 4 * kh + k, col:col + n],
                                           lambda k, b: wv[:, b, k, :], kh == 0, kh == 1)
                            if kh == 1:
                                ins.then_inc(job_done if t < TILES else sjob_done, 1)
                    if c >= 4 and c % 2 == 0:
                        ins.then_inc(half_used, 1)
                    if 4 <= c < 8:
                        g = c - 4
                        pe.wait_ge(xc_ready, LC * i + g + 1)
                        pe.wait_ge(gate_free, 2 * (LC * i + g))
                        nc.tensor.matmul(GB[0][:], gate_w[:, 0, g], xc[:, g], start=True, stop=True)
                        nc.tensor.matmul(GB[1][:], gate_w[:, 1, g], xc[:, g], start=True, stop=True).then_inc(gate_done, 1)
                if last:
                    pe.wait_ge(s_xc_ready, 1)
                    pe.wait_ge(gate_free, 2 * LC * GROUPS)
                    for g in range(LC):
                        for n in range(2):
                            ins = nc.tensor.matmul(GB[n][:, g * NS:g * NS + NS], gate_w[:, n, g], s_w[:, 7, g], start=True, stop=True)
                    ins.then_inc(s_gate_done, 1)

            with pe.Fori(0, GROUPS - 1) as i:
                group(i, False)
            group(GROUPS - 1, True)


def attend_prompt(nc, io, sems):
    ctx = ExitStack()
    sb = lambda name, shape, dt=F32: ctx.enter_context(nc.sbuf_tensor(name, shape, dt))
    sem = lambda name: sems.enter_context(nc.semaphore(name))
    QT = SEQ // P
    NK = [i // 4 + 1 for i in range(QT)]
    size = lambda i, kc: 512 if kc < NK[i] - 1 else (i % 4 + 1) * P
    before = [sum(NK[:i]) for i in range(QT + 1)]
    CHUNKS = before[QT]
    SCORES = 2 * CHUNKS
    tile_of = [i for i in range(QT) for _ in range(NK[i])]
    RESCALED = [sum(n > 1 for n in NK[:i]) for i in range(QT + 1)]
    LAG, SPLIT, TURN = 5, 4, 3
    SLOTS = range(-SPLIT, CHUNKS + LAG + 2)
    PRING, QRING, TRING = 8, 4, 8
    WT_JOBS = CHUNKS + 4
    with ctx:
        ident = sb("b_ident", [P, P])
        ident_r = sb("b_ident_r", [P, P], F32R)
        mask_in = sb("b_mask_in", [P, P])
        mask = sb("b_mask", [P, P], F32R)
        lam_in = sb("b_lam_in", [P, 4, HD])
        lam_t = sb("b_lam_t", [P, 2, HD])
        lam_s = sb("b_lam_s", [P, 4])
        nlam = sb("b_nlam", [P, 1])
        gain = sb("b_gain", [P, 1])
        eps = sb("b_eps", [P, 1])
        raw = sb("b_raw", [P, 3, QT, P])
        kin = sb("b_kin", [P, 2, 2, 2, HD], F32R)
        qin = sb("b_qin", [P, 2, 2, 2, 2, HD], F32R)
        vv = sb("b_v", [P, QT, 2, P], F32R)
        kT = sb("b_kT", [P, 2, SEQ], F32R)
        qT = sb("b_qT", [P, QRING, 4, P], F32R)
        p = sb("b_p", [P, PRING, 2, 512])
        w = sb("b_w", [P, 2, 512])
        wT = sb("b_wT", [P, 2, 2, 512], F32R)
        m = sb("b_m", [P, TRING, 2, 4])
        nm = sb("b_nm", [P, TRING, 2, 4])
        ls = sb("b_l", [P, TRING, 2, 4])
        top = sb("b_top", [P, 2])
        dm = sb("b_dm", [P, 2, 4])
        al = sb("b_al", [P, 2, 4])
        la = sb("b_la", [P, 2, 4])
        rl = sb("b_rl", [P, 2])
        coef = sb("b_coef", [P, TRING, 2, 4])
        ob = sb("b_ob", [P, P])
        o = sb("b_o", [P, QT, P])
        osq = sb("b_osq", [P, QT, P])
        oss = sb("b_oss", [P, QT])
        ors = sb("b_ors", [P, QT])
        oT = sb("b_oT", [P, SEQ])
        S = [ctx.enter_context(nc.psum_tensor(f"b_S{n}", [P, 2, 512], F32)) for n in range(2)]
        WT = [ctx.enter_context(nc.psum_tensor(f"b_WT{n}", [P, 512], F32)) for n in range(2)]
        O = ctx.enter_context(nc.psum_tensor("b_O", [P, 512], F32))
        M = ctx.enter_context(nc.psum_tensor("b_M", [P, 512], F32))
        consts_in = sem("b_consts_in")
        setup = sem("b_setup")
        lam_sum = sem("b_lam_sum")
        lam_exp = sem("b_lam_exp")
        rows_in = [sem(f"b_rows_in{n}") for n in range(4)]
        split_hi = sem("b_split_hi")
        split = sem("b_split")
        m_done = sem("b_m_done")
        k_free = sem("b_kT_ready")
        q_free = sem("b_qT_ready")
        s_done = sem("b_scores")
        nm_ready = sem("b_nm_ready")
        exp_done = sem("b_exp_done")
        dm_ready = sem("b_dm_ready")
        al_ready = sem("b_al_ready")
        coef_ready = sem("b_coef_ready")
        t2_ready = sem("b_t2_ready")
        w_ready = sem("b_w_ready")
        wt_done = sem("b_wT_in_psum")
        wt_hi = sem("b_wT_hi")
        wt_lo = sem("b_wT_lo")
        pv_done = sem("b_pv_done")
        ob_ready = sem("b_ob_ready")
        o_ready = sem("b_o_ready")
        osq_ready = sem("b_osq_ready")
        oss_ready = sem("b_oss_ready")
        std_ready = sem("b_std_ready")
        on_ready = sem("b_on_ready")
        dve_chain = sem("b_dve_chain")
        stored = sem("b_stored")
        out_free = sem("b_out_free")
        pool_turn = sem("b_pool_turn")
        out_ready = sem("b_out_ready")
        rows_v = [io["q"][0:SEQ].rearrange("(t p) (h e) -> h p t e", p=P, e=P),
                  io["k_prompt"].rearrange("l b (t p) h e -> (l b h) p t e", p=P),
                  io["v_prompt"].rearrange("l b (t p) h e -> (l b h) p t e", p=P)]
        out_v = io["mixT"][LRU:, 0:SEQ].rearrange("(h e) t -> h e t", e=P)
        block = ctx.enter_context(nc.Block())

        @block.sync
        def _(sp):
            sp.dma_start(ident[:], io["ident"]).then_inc(consts_in, 16)
            sp.dma_start(mask_in[:], io["mask"]).then_inc(consts_in, 16)
            for n, name in enumerate(("lambda_q1", "lambda_k1", "lambda_q2", "lambda_k2")):
                sp.dma_start(lam_in[:, n], io[name].broadcast_to([P, HD])).then_inc(consts_in, 16)
            sp.dma_start(gain[:], io["subln_g"].rearrange("l (e o) -> (l e) o", o=1)).then_inc(consts_in, 16)
            for g in range(4):
                for n in range(3):
                    sp.dma_start(raw[:, n, 4 * g:4 * g + 4], rows_v[n][0, :, 4 * g:4 * g + 4]).then_inc(rows_in[g], 16)
            with sp.Fori(0, HEADS - 1) as h:
                for g in range(4):
                    sp.wait_ge(split, QT * h + 4 * g + 4)
                    for n in range(3):
                        sp.dma_start(raw[:, n, 4 * g:4 * g + 4], rows_v[n][h + 1, :, 4 * g:4 * g + 4]).then_inc(rows_in[g], 16)

        def tiles_at(s, ahead):
            return [t for t in range(QT) if before[t] == s + ahead]

        def wt_before(h, first):
            return (0 if first else WT_JOBS * h - 4), (0 if first else 4)

        def heads(eng, head):
            head(0, True)
            with eng.Fori(1, HEADS) as h:
                head(h, False)

        @block.gpsimd
        def _(pool):
            pool.sem_inc(out_free, 1)

            def head(h, first):
                for s in SLOTS:
                    if not first and s == 7:
                        pool.wait_ge(out_ready, 4 * h)
                        pool.sem_inc(pool_turn, 1)
                        pool.dma_start(out_v[h - 1], oT[:]).then_inc(stored, 16)
                    if not first and s == CHUNKS:
                        pool.wait_ge(stored, 16 * h)
                        pool.sem_inc(out_free, 1)
                    g = s - LAG + 1
                    if 0 <= g < CHUNKS:
                        i, kc = tile_of[g], g - before[tile_of[g]]
                        if kc == 0:
                            pool.wait_ge(coef_ready, QT * h + i + 1)
                            pool.sem_inc(pool_turn, 1)
                        part = p[:, g % PRING, 1, 0:size(i, kc)]
                        nc.gpsimd.tensor_scalar(part, part, coef[:, i % TRING, 1, kc:kc + 1], 1.0, ALU.mult, ALU.mult).then_inc(t2_ready, 1)

            heads(pool, head)
            pool.wait_ge(out_ready, 4 * HEADS)
            pool.dma_start(out_v[HEADS - 1], oT[:]).then_inc(stored, 16)
            pool.wait_ge(stored, 16 * HEADS)

        @block.scalar
        def _(act):
            A = nc.scalar
            act.wait_ge(lam_sum, 1)
            A.activation(lam_s[:, 2:4], lam_s[:, 0:2], ACT.Exp).then_inc(lam_exp, 1)
            act.wait_ge(consts_in, 16 * 7)
            A.activation(ident_r[:], ident[:], ACT.Copy)
            A.activation(mask[:], mask_in[:], ACT.Copy).then_inc(setup, 1)

            def square():
                A.activation(osq[:], o[:], ACT.Square).then_inc(osq_ready, 1)

            def root(heads_done):
                act.wait_ge(oss_ready, heads_done)
                A.activation(ors[:], oss[:], ACT.Sqrt, bias=eps[:], scale=1.0 / P).then_inc(std_ready, 1)

            def head(h, first):
                def prep(t):
                    if t % 4 == 0:
                        act.wait_ge(rows_in[t // 4], 48 * (h + 1))
                    if t >= 2:
                        act.wait_ge(m_done, 2 * (QT * h + t - 1))
                    k = raw[:, 1, t].rearrange("p (c d) -> p c d", d=HD)
                    q = raw[:, 0, t].rearrange("p (c o d) -> p c o d", o=1, d=HD).broadcast_to([P, 2, 2, HD])
                    A.activation(kin[:, t % 2, :, 0], k, ACT.Copy)
                    A.activation(qin[:, t % 2, :, 0], q, ACT.Copy)
                    if t == 0 and not first:
                        act.wait_ge(pv_done, CHUNKS * h)
                    A.activation(vv[:, t, 0], raw[:, 2, t], ACT.Copy).then_inc(split_hi, 1)

                def turned(t):
                    act.wait_ge(m_done, 2 * (QT * h + t) + 1)
                    A.activation(kT[:, :, t * P:t * P + P], M[:, 0:2 * P].rearrange("p (c t) -> p c t", c=2), ACT.Copy)
                    A.activation(qT[:, t % QRING, 0:2], M[:, 2 * P:4 * P].rearrange("p (a t) -> p a t", a=2), ACT.Copy).then_inc(k_free, 1)

                for s in SLOTS:
                    for t in tiles_at(s, SPLIT):
                        prep(t)
                    for t in tiles_at(s, TURN):
                        turned(t)
                    if not first and s == -1:
                        square()
                    if not first and s == 1:
                        root(h)
                    g = s - LAG - 1
                    if 0 <= g < CHUNKS:
                        i, kc = tile_of[g], g - before[tile_of[g]]
                        n, base = size(i, kc), wt_before(h, first)
                        if g >= 2:
                            act.wait_ge(pv_done, CHUNKS * h + g - 1)
                        act.wait_ge(wt_done, base[0] + base[1] + g + 1)
                        A.activation(wT[:, g % 2, 0, 0:n], WT[g % 2][:, 0:n], ACT.Copy).then_inc(wt_hi, 1)
                    if 0 <= s < CHUNKS:
                        i, kc = tile_of[s], s - before[tile_of[s]]
                        n = size(i, kc)
                        act.wait_ge(nm_ready, CHUNKS * h + s + 1)
                        if s >= PRING:
                            act.wait_ge(w_ready, CHUNKS * h + s - PRING + 1)
                        for c in range(2):
                            A.activation(p[:, s % PRING, c, 0:n], S[s % 2][:, c, 0:n], ACT.Exp, bias=nm[:, i % TRING, c, kc:kc + 1],
                                         scale=QSCALE, accum_out=ls[:, i % TRING, c, kc:kc + 1]).then_inc(exp_done, 1)
                    g = s - LAG + 2
                    for i in range(QT):
                        if before[i] == g and NK[i] > 1:
                            act.wait_ge(dm_ready, RESCALED[QT] * h + RESCALED[i] + 1)
                            A.activation(al[:, :, 0:NK[i]], dm[:, :, 0:NK[i]], ACT.Exp, scale=QSCALE).then_inc(al_ready, 1)
                    g = s - LAG - 2
                    if 0 <= g < CHUNKS and g + 1 == before[tile_of[g] + 1]:
                        i = tile_of[g]
                        act.wait_ge(pv_done, CHUNKS * h + g + 1)
                        act.wait_ge(o_ready, QT * h + i) if i else None
                        A.activation(ob[:], O[:, P:2 * P], ACT.Copy).then_inc(ob_ready, 1)

            heads(act, head)
            act.wait_ge(o_ready, QT * HEADS)
            square()
            root(HEADS)

        @block.vector
        def _(dve):
            V = nc.vector
            V.memset(eps[:], EPS_SUBLN)
            link = Chain(dve, dve_chain)
            dve.wait_ge(consts_in, 16 * 7)
            link(V.tensor_tensor(lam_t[:], lam_in[:, 0:4:2], lam_in[:, 1:4:2], ALU.mult))
            V.reduce_sum(lam_s[:, 0:2], lam_t[:], axis=AX).then_inc(lam_sum, 1)
            dve.wait_ge(lam_exp, 1)
            link(V.tensor_tensor(nlam[:], lam_s[:, 3:4], lam_s[:, 2:3], ALU.subtract))
            link(V.tensor_scalar(nlam[:], nlam[:], -LAM_INIT, None, ALU.add))
            link(V.tensor_scalar(gain[:], gain[:], 1.0 - LAM_INIT, None, ALU.mult))
            links0 = link.n
            LINKS = CHUNKS + 5 * RESCALED[QT] + QT - RESCALED[QT] + 1

            def sum_squares(heads_done):
                dve.wait_ge(osq_ready, heads_done)
                V.reduce_sum(oss[:], osq[:], axis=AX).then_inc(oss_ready, 1)

            def normed(link, heads_done):
                dve.wait_ge(std_ready, heads_done)
                link(V.reciprocal(ors[:], ors[:]))
                V.tensor_tensor(osq[:], o[:], ors[:].rearrange("p (t o) -> p t o", o=1).broadcast_to([P, QT, P]), ALU.mult).then_inc(on_ready, 1)

            def out_part(b, jobs):
                dve.wait_ge(wt_done, jobs + b + 1)
                V.tensor_scalar(oT[:, b * 512:b * 512 + 512], WT[b % 2][:], gain[:], None, ALU.mult).then_inc(out_ready, 1)

            def head(h, first):
                link = Chain(dve, dve_chain, links0 + (0 if first else LINKS * h - 1))

                def prep(t):
                    dve.wait_ge(split_hi, QT * h + t + 1)
                    k = raw[:, 1, t].rearrange("p (c d) -> p c d", d=HD)
                    q = raw[:, 0, t].rearrange("p (c o d) -> p c o d", o=1, d=HD).broadcast_to([P, 2, 2, HD])
                    V.tensor_tensor(kin[:, t % 2, :, 1], k, kin[:, t % 2, :, 0].bitcast(F32), ALU.subtract)
                    V.tensor_tensor(qin[:, t % 2, :, 1], q, qin[:, t % 2, :, 0].bitcast(F32), ALU.subtract)
                    V.tensor_tensor(vv[:, t, 1], raw[:, 2, t], vv[:, t, 0].bitcast(F32), ALU.subtract).then_inc(split, 1)

                def stats(i):
                    b, n = i % TRING, NK[i]
                    dve.wait_ge(exp_done, SCORES * h + 2 * before[i + 1])
                    if n > 1:
                        link(V.reduce_max(top[:], m[:, b, :, 0:n], axis=AX))
                        V.tensor_tensor(dm[:, :, 0:n], m[:, b, :, 0:n], top[:].rearrange("p (c o) -> p c o", o=1).broadcast_to([P, 2, n]),
                                        ALU.subtract).then_inc(dm_ready, 1)
                        dve.wait_ge(al_ready, RESCALED[QT] * h + RESCALED[i] + 1)
                        link(V.tensor_tensor(la[:, :, 0:n], ls[:, b, :, 0:n], al[:, :, 0:n], ALU.mult))
                        link(V.reduce_sum(rl[:], la[:, :, 0:n], axis=AX))
                        link(V.reciprocal(rl[:], rl[:]))
                        link(V.tensor_tensor(rl[:, 1:2], rl[:, 1:2], nlam[:], ALU.mult))
                        V.tensor_tensor(coef[:, b, :, 0:n], al[:, :, 0:n], rl[:].rearrange("p (c o) -> p c o", o=1).broadcast_to([P, 2, n]),
                                        ALU.mult).then_inc(coef_ready, 1)
                    else:
                        link(V.reciprocal(coef[:, b, :, 0:1], ls[:, b, :, 0:1]))
                        V.tensor_tensor(coef[:, b, 1, 0:1], coef[:, b, 1, 0:1], nlam[:], ALU.mult).then_inc(coef_ready, 1)

                for s in SLOTS:
                    for t in tiles_at(s, SPLIT):
                        prep(t)
                    if not first:
                        if s == 0:
                            sum_squares(h)
                        if s == 2:
                            normed(link, h)
                    g = s - LAG
                    if 0 <= g < CHUNKS:
                        i, kc = tile_of[g], g - before[tile_of[g]]
                        n = size(i, kc)
                        dve.wait_ge(t2_ready, CHUNKS * h + g + 1)
                        if g >= 2:
                            dve.wait_ge(wt_hi, CHUNKS * h + g - 1)
                        V.scalar_tensor_tensor(w[:, g % 2, 0:n], p[:, g % PRING, 0, 0:n], coef[:, i % TRING, 0, kc:kc + 1],
                                               p[:, g % PRING, 1, 0:n], ALU.mult, ALU.add).then_inc(w_ready, 1)
                    if 0 <= s < CHUNKS:
                        i, kc = tile_of[s], s - before[tile_of[s]]
                        n = size(i, kc)
                        dve.wait_ge(s_done, CHUNKS * h + s + 1)
                        link(V.reduce_max(m[:, i % TRING, :, kc], S[s % 2][:, :, 0:n], axis=AX))
                        V.tensor_scalar(nm[:, i % TRING, :, kc], m[:, i % TRING, :, kc], -QSCALE, None, ALU.mult).then_inc(nm_ready, 1)
                    g = s - LAG - 1
                    if 0 <= g < CHUNKS:
                        n = size(tile_of[g], g - before[tile_of[g]])
                        dve.wait_ge(wt_hi, CHUNKS * h + g + 1)
                        V.tensor_tensor(wT[:, g % 2, 1, 0:n], WT[g % 2][:, 0:n], wT[:, g % 2, 0, 0:n].bitcast(F32), ALU.subtract).then_inc(wt_lo, 1)
                    if not first and 3 <= s < 7:
                        if s == 3:
                            dve.wait_ge(out_free, h)
                        out_part(s - 3, wt_before(h, first)[0])
                    for t in tiles_at(s, TURN):
                        dve.wait_ge(m_done, 2 * (QT * h + t) + 2)
                        V.tensor_copy(qT[:, t % QRING, 2:4].rearrange("p a t -> p (a t)"), M[:, 0:2 * P]).then_inc(q_free, 1)
                    for i in range(QT):
                        if before[i] == s - LAG + 2:
                            stats(i)
                    g = s - LAG - 2
                    if 0 <= g < CHUNKS and g + 1 == before[tile_of[g] + 1]:
                        dve.wait_ge(ob_ready, QT * h + tile_of[g] + 1)
                        V.tensor_tensor(o[:, tile_of[g]], O[:, 0:P], ob[:], ALU.add).then_inc(o_ready, 1)
                assert link.n == LINKS - (1 if first else 0), (link.n, LINKS)

            heads(dve, head)
            sum_squares(HEADS)
            normed(Chain(dve, dve_chain, links0 + LINKS * HEADS - 1), HEADS)
            dve.wait_ge(out_free, HEADS)
            for b in range(4):
                out_part(b, WT_JOBS * HEADS - 4)

        @block.tensor
        def _(pe):
            pe.wait_ge(setup, 1)

            def turn_out(b, h):
                if b >= 2:
                    pe.wait_ge(out_ready, 4 * h - 4 + b - 1)
                for t in range(4):
                    ins = nc.tensor.transpose(WT[b % 2][:, t * P:t * P + P], osq[:, 4 * b + t], ident[:])
                ins.then_inc(wt_done, 1)

            def head(h, first):
                def turn(t, job):
                    if job == 0:
                        pe.wait_ge(split, QT * h + t + 1)
                        if t or not first:
                            pe.wait_ge(q_free, QT * h + t)
                        for c in range(2):
                            nc.tensor.transpose(M[:, c * P:c * P + P], kin[:, t % 2, c].bitcast(F32).rearrange("p a d -> p (a d)"), ident[:])
                    else:
                        pe.wait_ge(k_free, QT * h + t + 1)
                    for a in range(2):
                        at = (2 * (1 - job) + a) * P
                        ins = nc.tensor.transpose(M[:, at:at + P], qin[:, t % 2, job, a].bitcast(F32).rearrange("p a d -> p (a d)"), ident[:])
                    ins.then_inc(m_done, 1)

                for s in SLOTS:
                    if 0 <= s + 1 < CHUNKS:
                        j = s + 1
                        i, kc = tile_of[j], j - before[tile_of[j]]
                        n = size(i, kc)
                        if kc == 0:
                            pe.wait_ge(q_free, QT * h + i + 1)
                        if j >= 2:
                            pe.wait_ge(exp_done, SCORES * h + 2 * (j - 1))
                        diagonal = kc == NK[i] - 1
                        for c in range(2):
                            for a in range(2):
                                ins = nc.tensor.matmul(S[j % 2][:, c, 0:n], qT[:, i % QRING, 2 * c + a], kT[:, c, kc * 512:kc * 512 + n],
                                                       start=a == 0, stop=a == 1 and not diagonal)
                            if diagonal:
                                ins = nc.tensor.matmul(S[j % 2][:, c, n - P:n], ident_r[:], mask[:], start=False, stop=True)
                        ins.then_inc(s_done, 1)
                    for t in tiles_at(s, TURN):
                        turn(t, 0)
                    g = s - LAG
                    if 0 <= g < CHUNKS:
                        i, kc = tile_of[g], g - before[tile_of[g]]
                        pe.wait_ge(w_ready, CHUNKS * h + g + 1)
                        if g >= 2:
                            pe.wait_ge(wt_lo, CHUNKS * h + g - 1)
                        elif not first:
                            pe.wait_ge(out_ready, 4 * h - 1 + g)
                        for t in range(size(i, kc) // P):
                            ins = nc.tensor.transpose(WT[g % 2][:, t * P:t * P + P], w[:, g % 2, t * P:t * P + P], ident[:])
                        ins.then_inc(wt_done, 1)
                    if not first and 2 <= s < 5:
                        if s == 2:
                            pe.wait_ge(on_ready, h)
                        for b in ((0,), (1,), (2, 3))[s - 2]:
                            turn_out(b, h)
                    g = s - LAG - 2
                    if 0 <= g < CHUNKS:
                        i, kc = tile_of[g], g - before[tile_of[g]]
                        pe.wait_ge(wt_lo, CHUNKS * h + g + 1)
                        if kc == 0 and (i or not first):
                            pe.wait_ge(o_ready, QT * h + i)
                        for t in range(size(i, kc) // P):
                            k = kc * 4 + t
                            nc.tensor.matmul(O[:, 0:2 * P], wT[:, g % 2, 0, t * P:t * P + P], vv[:, k].rearrange("p a e -> p (a e)"),
                                             start=k == 0, stop=False)
                            ins = nc.tensor.matmul(O[:, 0:P], wT[:, g % 2, 1, t * P:t * P + P], vv[:, k, 0], start=False, stop=k == i)
                        ins.then_inc(pv_done, 1)
                    for t in tiles_at(s, TURN):
                        turn(t, 1)

            heads(pe, head)
            pe.wait_ge(on_ready, HEADS)
            for b in range(4):
                turn_out(b, HEADS)


def attend_sample(nc, io, sems):
    ctx = ExitStack()
    sb = lambda name, shape, dt=F32: ctx.enter_context(nc.sbuf_tensor(name, shape, dt))
    sem = lambda name: sems.enter_context(nc.semaphore(name))
    W = HEADS * P
    R = NS * COMP
    RH = NS * HEADS
    N_PHYS = io["cache_k"].shape[1]
    with ctx:
        table = sb("d_table", [1, NS * PAGES], I32)
        kp = sb("d_k", [P, NS, PAGES, W])
        vp = sb("d_v", [P, NS, PAGES, W])
        qb = sb("d_q", [P, NS, W])
        prod = sb("d_prod", [P, 2, PAGES, W])
        sc = sb("d_scores", [P, PAGES, R])
        ident = sb("d_ident", [P, P])
        ones = sb("d_ones", [P, P])
        sel = sb("d_sel", [R, 2])
        lam_in = sb("d_lam_in", [P, 4, HD])
        lam_t = sb("d_lam_t", [P, 2, HD])
        lam_s = sb("d_lam_s", [P, 4])
        nlam = sb("d_nlam", [P, 1])
        gain = sb("d_gain", [P, 1])
        eps = sb("d_eps", [P, 1])
        q64 = sb("d_q64", [R, HD])
        k64 = sb("d_k64", [R, HD])
        v32 = sb("d_v32", [RH, P])
        own = sb("d_own", [R, 1])
        pp = sb("d_p", [R, PAGES * PAGE])
        st = sb("d_st", [R, 8])
        wn = sb("d_wn", [R, P])
        cp = sb("d_cp", [P, PAGES * R])
        ws = sb("d_ws", [P, PAGES, RH])
        wnb = sb("d_wnb", [P, R])
        wo = sb("d_wo", [P, RH])
        vT = sb("d_vT", [P, RH])
        o = sb("d_o", [P, RH])
        osq = sb("d_osq", [P, RH])
        ors = sb("d_ors", [P, RH])
        res = sb("d_res", [P, HEADS, NS])
        ST = ctx.enter_context(nc.psum_tensor("d_ST", [P, 512], F32))
        PT = ctx.enter_context(nc.psum_tensor("d_PT", [P, 512], F32))
        OT = ctx.enter_context(nc.psum_tensor("d_OT", [P, 512], F32))
        VT = ctx.enter_context(nc.psum_tensor("d_VT", [P, 512], F32))
        WB = ctx.enter_context(nc.psum_tensor("d_WB", [P, 512], F32))
        SS = ctx.enter_context(nc.psum_tensor("d_SS", [P, 512], F32))
        table_in = sem("d_table_in")
        consts_in = sem("d_consts_in")
        k_in = [sem(f"d_k_in{b}") for b in range(NS // 2)]
        v_in = [sem(f"d_v_in{b}") for b in range(NS // 2)]
        q_in = sem("d_q_in")
        chain = sem("d_dve_chain")
        to_act = sem("d_to_act")
        from_act = sem("d_from_act")
        to_pe = sem("d_to_pe")
        from_pe = sem("d_from_pe")
        res_ready = sem("d_res_ready")
        stored = sem("d_stored")
        rows = [io["q"][SEQ:SEQ + NS], io["k_sample"].rearrange("l b s h e -> (l b s) (h e)"),
                io["v_sample"].rearrange("l b s h e -> (l b s) (h e)")]
        ck = io["cache_k"].rearrange("l n t h e -> (l n) t (h e)")
        cv = io["cache_v"].rearrange("l n t h e -> (l n) t (h e)")
        block = ctx.enter_context(nc.Block())

        def pages(eng, cache, dst, arrived):
            eng.wait_ge(table_in, 16)
            for b in range(NS):
                for n in range(PAGES):
                    page = eng.value_load(table[0:1, b * PAGES + n:b * PAGES + n + 1], min_val=0, max_val=N_PHYS - 1)
                    eng.dma_start(dst[:, b, n], cache[page]).then_inc(arrived[b // 2], 16)

        @block.sync
        def _(sp):
            sp.dma_start(table[:], io["page_table"].rearrange("(o b) n -> o (b n)", o=1)).then_inc(table_in, 16)
            for b in range(NS):
                sp.dma_start(qb[:, b], rows[0][b:b + 1].broadcast_to([P, W])).then_inc(q_in, 16)
            pages(sp, ck, kp, k_in)
            sp.wait_ge(res_ready, 1)
            for h in range(HEADS):
                sp.dma_start(io["mixT"][LRU + h * P:LRU + h * P + P, SEQ:SEQ + NS], res[:, h]).then_inc(stored, 16)
            sp.wait_ge(stored, 16 * HEADS)

        @block.scalar
        def _(act):
            A = nc.scalar
            act.dma_start(ident[:], io["ident"]).then_inc(consts_in, 16)
            act.dma_start(sel[:], io["sel"]).then_inc(consts_in, 16)
            for n, name in enumerate(("lambda_q1", "lambda_k1", "lambda_q2", "lambda_k2")):
                act.dma_start(lam_in[:, n], io[name].broadcast_to([P, HD])).then_inc(consts_in, 16)
            act.dma_start(gain[:], io["subln_g"].rearrange("l (e o) -> (l e) o", o=1)).then_inc(consts_in, 16)
            act.dma_start(q64[:], rows[0].rearrange("b (c d) -> (b c) d", d=HD)).then_inc(consts_in, 16)
            act.dma_start(k64[:], rows[1].rearrange("b (c d) -> (b c) d", d=HD)).then_inc(consts_in, 16)
            act.dma_start(v32[:], rows[2].rearrange("b (h e) -> (b h) e", e=P)).then_inc(consts_in, 16)
            pages(act, cv, vp, v_in)
            act.wait_ge(to_act, 1)
            A.activation(lam_s[:, 2:4], lam_s[:, 0:2], ACT.Exp).then_inc(from_act, 1)
            act.wait_ge(to_act, 2)
            A.activation(pp[:], ST[0:R], ACT.Exp, bias=st[:, 1:2], scale=QSCALE, accum_out=st[:, 2:3])
            A.activation(st[:, 3:4], own[:], ACT.Exp, bias=st[:, 1:2], scale=QSCALE).then_inc(from_act, 1)
            act.wait_ge(from_pe, 2)
            A.activation(cp[:], PT[:, 0:PAGES * R], ACT.Copy)
            A.activation(wnb[:], WB[:, 0:R], ACT.Copy).then_inc(from_act, 1)
            act.wait_ge(from_pe, 4)
            A.activation(ors[:], SS[:, 0:RH], ACT.Sqrt, bias=eps[:], scale=1.0 / P).then_inc(from_act, 1)

        @block.vector
        def _(dve):
            V = nc.vector
            link = Chain(dve, chain)
            V.memset(ones[:], 1.0)
            link(V.memset(eps[:], EPS_SUBLN))
            dve.wait_ge(consts_in, 16 * 10)
            link(V.tensor_tensor(lam_t[:], lam_in[:, 0:4:2], lam_in[:, 1:4:2], ALU.mult))
            V.reduce_sum(lam_s[:, 0:2], lam_t[:], axis=AX).then_inc(to_act, 1)
            dve.wait_ge(from_act, 1)
            link(V.tensor_tensor(nlam[:], lam_s[:, 3:4], lam_s[:, 2:3], ALU.subtract))
            link(V.tensor_scalar(nlam[:], nlam[:], -LAM_INIT, None, ALU.add))
            link(V.tensor_scalar(gain[:], gain[:], 1.0 - LAM_INIT, None, ALU.mult))
            link(V.scalar_tensor_tensor(st[:, 5:6], sel[:, 1:2], nlam[0:R], sel[:, 0:1], ALU.mult, ALU.add))
            link(V.tensor_tensor(q64[:], q64[:], k64[:], ALU.mult))
            link(V.reduce_sum(own[:], q64[:], axis=AX))
            dve.wait_ge(q_in, 16 * NS)
            for b in range(NS):
                dve.wait_ge(k_in[b // 2], 2 * 16 * PAGES)
                link(V.tensor_tensor(prod[:, b % 2], kp[:, b], qb[:, b:b + 1].broadcast_to([P, PAGES, W]), ALU.mult))
                ins = V.reduce_sum(sc[:, :, b * COMP:(b + 1) * COMP], prod[:, b % 2].rearrange("p n (c d) -> p n c d", d=HD), axis=AX)
            ins.then_inc(to_pe, 1)
            dve.wait_ge(from_pe, 1)
            link(V.reduce_max(st[:, 0:1], ST[0:R], axis=AX))
            link(V.tensor_tensor(st[:, 0:1], st[:, 0:1], own[:], ALU.max))
            V.tensor_scalar(st[:, 1:2], st[:, 0:1], -QSCALE, None, ALU.mult).then_inc(to_act, 1)
            dve.wait_ge(from_act, 2)
            link(V.tensor_tensor(st[:, 4:5], st[:, 2:3], st[:, 3:4], ALU.add))
            link(V.reciprocal(st[:, 4:5], st[:, 4:5]))
            link(V.tensor_tensor(st[:, 4:5], st[:, 4:5], st[:, 5:6], ALU.mult))
            V.tensor_scalar(pp[:], pp[:], st[:, 4:5], None, ALU.mult)
            link(V.tensor_tensor(st[:, 6:7], st[:, 3:4], st[:, 4:5], ALU.mult))
            V.tensor_scalar(wn[:], ones[0:R], st[:, 6:7], None, ALU.mult).then_inc(to_pe, 1)
            dve.wait_ge(from_act, 3)
            c4 = cp[:].rearrange("p (n r c) -> p n r c", n=PAGES, c=2)
            V.tensor_tensor(ws[:], c4[:, :, :, 0], c4[:, :, :, 1], ALU.add).then_inc(to_pe, 1)
            w2 = wnb[:].rearrange("p (r c) -> p r c", c=2)
            link(V.tensor_tensor(wo[:], w2[:, :, 0], w2[:, :, 1], ALU.add))
            dve.wait_ge(from_pe, 2)
            link(V.tensor_copy(vT[:], VT[:, 0:RH]))
            link(V.tensor_tensor(wo[:], wo[:], vT[:], ALU.mult))
            dve.wait_ge(from_pe, 3)
            link(V.tensor_tensor(o[:], OT[:, 0:RH], wo[:], ALU.add))
            V.tensor_tensor(osq[:], o[:], o[:], ALU.mult).then_inc(to_pe, 1)
            dve.wait_ge(from_act, 4)
            link(V.reciprocal(ors[:], ors[:]))
            link(V.tensor_tensor(o[:], o[:], ors[:], ALU.mult))
            V.tensor_scalar(res[:].rearrange("p h b -> p b h"), o[:].rearrange("p (b h) -> p b h", h=HEADS), gain[:], None, ALU.mult).then_inc(res_ready, 1)

        @block.tensor
        def _(pe):
            T = nc.tensor
            pe.wait_ge(consts_in, 16 * 10)
            pe.wait_ge(to_pe, 1)
            for n in range(PAGES):
                ins = T.transpose(ST[0:R, n * PAGE:(n + 1) * PAGE], sc[:, n], ident[:])
            ins.then_inc(from_pe, 1)
            pe.wait_ge(to_pe, 2)
            T.transpose(VT[:, 0:RH], v32[:], ident[0:RH, 0:RH])
            for n in range(PAGES):
                T.transpose(PT[:, n * R:(n + 1) * R], pp[:, n * PAGE:(n + 1) * PAGE], ident[0:R, 0:R])
            T.matmul(WB[:, 0:R], wn[:], ident[0:R, 0:R], start=True, stop=True).then_inc(from_pe, 1)
            pe.wait_ge(to_pe, 3)
            for b in range(NS):
                pe.wait_ge(v_in[b // 2], 2 * 16 * PAGES)
                for h in range(HEADS):
                    for n in range(PAGES):
                        ins = T.matmul(OT[:, b * HEADS + h:b * HEADS + h + 1], vp[:, b, n, h * P:(h + 1) * P],
                                       ws[:, n, b * HEADS + h:b * HEADS + h + 1], start=n == 0, stop=n == PAGES - 1)
            ins.then_inc(from_pe, 1)
            pe.wait_ge(to_pe, 4)
            T.matmul(SS[:, 0:RH], ones[:], osq[:], start=True, stop=True).then_inc(from_pe, 1)


def mix_and_feed(nc, io, sems):
    ctx = ExitStack()
    sem = lambda name: sems.enter_context(nc.semaphore(name))
    CH, RING, RAW, AHEAD = 42, 3, 2, 2
    UP0, DOWN0, PROJ, GATE0 = 4, 26, 37, 38
    MIXED = DOWN0 + 5
    FJOBS = FB
    with ctx:
        base = nc.sbuf_base
        base += -base % 64
        top = [base]

        def sb(name, shape, dt=F32, at=None):
            n = int(np.prod(shape[1:])) * (2 if dt == mybir.dt.bfloat16 else 4)
            if at is None:
                at, top[0] = top[0], top[0] + n + -n % 32
            return nc.alloc_sbuf_tensor_at(name, shape, dt, offset=at)

        w = sb("c_w", [P, RING, 2, 2048], F32R)
        raw = sb("c_raw", [P, RAW, 2048])
        h_at = top[0]
        hT = sb("c_hT", [P, 2, KD, WIDE], F32R)
        f_at = top[0]
        fT = sb("c_fT", [P, FB, 2, WIDE], F32R)
        x2T = sb("c_x2T", [P, 2, KD, WIDE], F32R, at=f_at)
        hn = sb("c_hn", [P, 2, D], at=f_at)
        at = f_at + 2 * KD * WIDE * 4
        mix = sb("c_mix", [P, KD, WIDE], at=at)
        at += KD * WIDE * 4
        x1 = sb("c_x1", [P, TILES + 1, D], at=at)
        x2 = sb("c_x2", [P, TILES + 1, D], at=at)
        at += (TILES + 1) * D * 4
        mo = sb("c_mo", [P, TILES + 1, D], at=at)
        pr = sb("c_pr", [P, TILES + 1, D], at=at)
        assert at + (TILES + 1) * D * 4 <= top[0]
        fo = sb("c_fo", [P, TILES + 1, D], at=h_at)
        pT = sb("c_pT", [P, 2, 2, WIDE], F32R)
        xr = sb("c_xr", [P, 2, D])
        gains = sb("c_gains", [P, 2, D])
        act1 = sb("c_act1", [P, 2, WIDE])
        junk = sb("c_junk", [P, D], mybir.dt.bfloat16)
        pin = sb("c_pin", [P, 2, PLE])
        ident = sb("c_ident", [P, P])
        eps = sb("c_eps", [P, 1])
        ss = sb("c_ss", [P, 4, TILES + 1])
        rs = sb("c_rs", [P, 4, TILES + 1])
        assert top[0] <= nc.sbuf_usable_end, (top[0], nc.sbuf_usable_end)
        banks = [ctx.enter_context(nc.psum_tensor(f"c_bank{n}", [P, 512], F32)) for n in range(8)]
        ACC = banks[0:5]
        TB = banks[5:7]
        PB = banks[7]
        consts_in = sem("c_consts_in")
        ready0 = sem("c_eps_written")
        raw_in = [sem(f"c_raw_in{n}") for n in range(RAW)]
        w_hi = sem("c_w_hi")
        w_ready = sem("c_w_ready")
        w_used = sem("c_w_used")
        mix_in = sem("c_mix_in")
        mix_hi = sem("c_mix_hi")
        mix_ready = sem("c_mix_ready")
        xr_in = [sem(f"c_xr_in{n}") for n in range(2)]
        gain_in = [sem(f"c_gain_in{n}") for n in range(2)]
        p_in = [sem(f"c_p_in{n}") for n in range(2)]
        acc_done = sem("c_acc_done")
        acc_free = sem("c_acc_free")
        std = [sem(f"c_std{n}") for n in range(4)]
        act_chain = sem("c_act_chain")
        dve_chain = sem("c_dve_chain")
        mo_ready = sem("c_mo_ready")
        x1_ready = sem("c_x1_ready")
        x1_out = sem("c_x1_out")
        hn_ready = sem("c_hn_ready")
        tp_done = sem("c_transposed")
        t_hi = sem("c_T_hi")
        t_lo = sem("c_T_lo")
        pair_done = sem("c_gate_up_done")
        silu_done = sem("c_silu")
        f_ready = sem("c_f")
        f_hi = sem("c_f_hi")
        f_lo = sem("c_f_lo")
        spair_done = sem("c_sample_gate_up_done")
        ssilu_done = sem("c_sample_silu")
        sf_ready = sem("c_sample_f")
        fo_ready = sem("c_fo_ready")
        x2_ready = sem("c_x2_ready")
        pt_done = sem("c_p_transposed")
        pt_hi = sem("c_pT_hi")
        pt_lo = sem("c_pT_lo")
        proj_done = sem("c_proj_done")
        proj_free = sem("c_proj_free")
        sig_ready = sem("c_sigmoid")
        v_ready = sem("c_v_ready")
        y_ready = sem("c_y_ready")
        y_out = sem("c_y_out")
        pool_turn = sem("c_pool_turn")

        rows = lambda name: io[name][0].rearrange("(k p) n -> p k n", p=P)
        wo, wg, wu, wd, wp, wpg = (rows(n) for n in ("w_out", "ffn_w_gate", "ffn_w_up", "ffn_w_down", "ple_w_proj", "ple_w_gate"))

        def chunk(c):
            if c < UP0:
                return [(wo[:, c % 2 * 4:c % 2 * 4 + 4, c // 2 * 512:c // 2 * 512 + 512], lambda v: v.rearrange("p (k n) -> p k n", n=512))]
            if c < DOWN0:
                b = c - UP0
                return [(s[:, :, b * P:b * P + P], lambda v, n=n: v[:, n * 1024:n * 1024 + 1024].rearrange("p (k n) -> p k n", n=P)) for n, s in enumerate((wg, wu))]
            if c < MIXED:
                return [(wd[:, 4 * (c - DOWN0):4 * (c - DOWN0) + 4, 0:512], lambda v: v.rearrange("p (k n) -> p k n", n=512))]
            if c == MIXED:
                return [(wd[:, 20:22, n * 512:n * 512 + 512], lambda v, n=n: v[:, n * 1024:n * 1024 + 1024].rearrange("p (k n) -> p k n", n=512)) for n in range(2)]
            if c < PROJ:
                b = 4 * (c - MIXED - 1)
                return [(wd[:, b:b + 4, 512:1024], lambda v: v.rearrange("p (k n) -> p k n", n=512))]
            if c == PROJ:
                return [(wp, lambda v: v.rearrange("p (k n) -> p k n", n=1024))]
            g = c - GATE0
            return [(wpg[:, g % 2 * 4:g % 2 * 4 + 4, g // 2 * 512:g // 2 * 512 + 512], lambda v: v.rearrange("p (k n) -> p k n", n=512))]

        DMAS = [len(chunk(c)) for c in range(CH)]

        def arrived(i, c):
            return 16 * (sum(DMAS[c % RAW::RAW]) * i + sum(DMAS[c % RAW:c + 1:RAW]))

        ACCS = 6 * TILES

        def acc_job(i, last, phase, d, t):
            n = TILES + 1 if last else TILES
            return ACCS * i + n * (2 * phase + d) + t + 1

        x_v = io["x_prompt"].rearrange("b (g t p) d -> (b g) t p d", g=GROUPS, p=P)
        y_v = io["y_prompt"].rearrange("b (g t p) d -> (b g) t p d", g=GROUPS, p=P)
        x1_v = io["x1"][0:SEQ].rearrange("(g t p) d -> g t p d", g=GROUPS, p=P)
        p_v = io["p_prompt"].rearrange("l b (g t p) e -> (l b g) t p e", g=GROUPS, p=P)
        mix_v = io["mixT"].rearrange("(k p) t -> p k t", p=P)

        def tile_of(view, sample, i, t):
            return sample if t == TILES else view[i, t]

        x_s = io["x_sample"].rearrange("b s d -> (b s) d")
        y_s = io["y_sample"].rearrange("b s d -> (b s) d")
        p_s = io["p_sample"].rearrange("l b s e -> (l b s) e")
        x1_s = io["x1"][SEQ:SEQ + NS]
        GAINS = ("norm_post_mix", "norm_pre_ffn", "norm_post_ffn", "ple_norm")
        PRJ = (PB, banks[4])
        T_PER = 4 * TILES

        def chunk_used(eng, i, c, last):
            if c < 0:
                if isinstance(i, int) and i == 0:
                    return
                i, c, last = i - 1, c + CH, False
            if c in ENDS:
                phase, d = ENDS[c]
                eng.wait_ge(acc_done, acc_job(i, last, phase, d, TILES if last else TILES - 1))
            elif UP0 <= c < DOWN0:
                eng.wait_ge(pair_done, 2 * FJOBS * i + 2 * (c - UP0) + 2)
                if last:
                    eng.wait_ge(spair_done, 2 * (c - UP0) + 2)
            elif c == PROJ:
                eng.wait_ge(proj_done, 2 * TILES * i + 2 * (TILES + 1 if last else TILES))
            else:
                eng.wait_ge(w_used, len(PLAIN) * i + PLAIN.index(c) + 1)

        ENDS = {1: (0, 0), 3: (0, 1), PROJ - 1: (1, 1), GATE0 + 1: (2, 0), GATE0 + 3: (2, 1)}
        PLAIN = [c for c in range(CH) if c not in ENDS and not UP0 <= c < DOWN0 and c != PROJ]

        block = ctx.enter_context(nc.Block())

        @block.sync
        def _(sp):
            def load(c):
                for src, place in chunk(c):
                    sp.dma_start(place(raw[:, c % RAW]), src).then_inc(raw_in[c % RAW], 16)

            sp.dma_start(mix[:, :, 0:GROUP], mix_v[:, :, 0:GROUP]).then_inc(mix_in, 16)
            for c in range(AHEAD):
                load(c)
            sp.dma_start(ident[:], io["ident"]).then_inc(consts_in, 16)

            def group(i, last):
                for c in range(AHEAD, CH):
                    sp.wait_ge(w_ready, CH * i + c - RAW + 1)
                    load(c)
                if not last:
                    sp.wait_ge(acc_done, acc_job(i, last, 1, 1, TILES - 1))
                    sp.dma_start(mix[:, :, 0:GROUP], mix_v[:, :, bass.ts(i + 1, GROUP)]).then_inc(mix_in, 16)
                    for c in range(AHEAD):
                        sp.wait_ge(w_ready, CH * i + CH + c - RAW + 1)
                        load(c)

            with sp.Fori(0, GROUPS - 2) as i:
                group(i, False)
            group(GROUPS - 2, False)
            sp.dma_start(mix[:, :, GROUP:], mix_v[:, :, SEQ:]).then_inc(mix_in, 16)
            group(GROUPS - 1, True)

        @block.gpsimd
        def _(pool):
            def load(dst, src, arrived):
                pool.sem_inc(pool_turn, 1)
                pool.dma_start(dst, src).then_inc(arrived, 16)

            def load_gain(n):
                load(gains[:, n % 2], io[GAINS[n]].broadcast_to([P, D]), gain_in[n % 2])

            def group(i, last):
                tiles = group_tiles(last)

                def load_rows(t, n, view, sample):
                    load(xr[0:n, t % 2], tile_of(view, sample, i, t), xr_in[t % 2])

                pool.wait_ge(y_ready, TILES * i)
                for n in range(2):
                    load_gain(n)
                for t, _, n in tiles[0:2]:
                    load_rows(t, n, x_v, x_s)
                for t, _, n in tiles:
                    pool.wait_ge(x1_ready, TILES * i + t + 1)
                    load(tile_of(x1_v, x1_s, i, t), x1[0:n, t], x1_out)
                    if t + 2 < len(tiles):
                        load_rows(t + 2, tiles[t + 2][2], x_v, x_s)
                pool.wait_ge(hn_ready, TILES * i + len(tiles))
                for n in range(2, 4):
                    load_gain(n)
                pool.wait_ge(x1_out, 16 * (TILES * i + len(tiles)))
                for t, _, n in tiles[0:2]:
                    load_rows(t, n, x1_v, x1_s)
                for t, _, n in tiles:
                    if t >= 2:
                        pool.wait_ge(pt_done, TILES * i + t - 1)
                    load(pin[0:n, t % 2], tile_of(p_v, p_s, i, t), p_in[t % 2])
                for t, _, n in tiles[2:]:
                    pool.wait_ge(x2_ready, TILES * i + t - 1)
                    load_rows(t, n, x1_v, x1_s)
                for t, _, n in tiles:
                    pool.wait_ge(y_ready, TILES * i + t + 1)
                    load(tile_of(y_v, y_s, i, t), x2[0:n, t], y_out)

            with pool.Fori(0, GROUPS - 1) as i:
                group(i, False)
            group(GROUPS - 1, True)
            pool.wait_ge(y_out, 16 * (TILES * GROUPS + 1))
            pool.wait_ge(x1_out, 16 * (TILES * GROUPS + 1))

        @block.scalar
        def _(act):
            A = nc.scalar
            NORMS = 4 * TILES

            def split(i, c, last):
                act.wait_ge(raw_in[c % RAW], arrived(i, c))
                chunk_used(act, i, c - RING, last)
                A.activation(w[:, c % RING, 0], raw[:, c % RAW], ACT.Copy).then_inc(w_hi, 1)

            def norm(i, link, k, t, n, ready, src):
                act.wait_ge(ready, TILES * i + t + 1)
                link(A.activation(junk[0:n], src[0:n, t], ACT.Square, accum_out=ss[0:n, k, t:t + 1]))
                A.activation(rs[0:n, k, t:t + 1], ss[0:n, k, t:t + 1], ACT.Sqrt, bias=eps[0:n], scale=1.0 / D).then_inc(std[k], 1)

            def hi_halves(i, last, phase, t, col, n, dst):
                for half in range(2):
                    act.wait_ge(tp_done, T_PER * i + 2 * len(group_tiles(last)) * phase + 2 * t + half + 1)
                    A.activation(dst[:, 0, 4 * half:4 * half + 4, col:col + n], TB[half][:, 0:4 * n].rearrange("p (k t) -> p k t", k=4), ACT.Copy).then_inc(t_hi, 1)

            act.wait_ge(ready0, 1)
            act.wait_ge(raw_in[0], 16)
            A.activation(w[:, 0, 0], raw[:, 0], ACT.Copy).then_inc(w_hi, 1)
            act.wait_ge(raw_in[1], 16)
            A.activation(w[:, 1, 0], raw[:, 1], ACT.Copy).then_inc(w_hi, 1)

            def group(i, last):
                tiles = group_tiles(last)
                wide = WIDE if last else GROUP
                link = Chain(act, act_chain, NORMS * i)
                act.wait_ge(mix_in, 16 * (i + 1) + (16 if last else 0))
                act.wait_ge(x2_ready, TILES * i)
                A.activation(hT[:, 0, :, 0:wide], mix[:, :, 0:wide], ACT.Copy).then_inc(mix_hi, 1)
                for c in range(CH):
                    if c + AHEAD < CH:
                        split(i, c + AHEAD, last)
                    elif not last:
                        split(i + 1, c + AHEAD - CH, False)
                    if c == 3:
                        for s in range(len(tiles) + 2):
                            if s < len(tiles):
                                norm(i, link, 0, *tiles[s][::2], mo_ready, mo)
                            if 1 <= s <= len(tiles):
                                norm(i, link, 1, *tiles[s - 1][::2], x1_ready, x1)
                            if s >= 2:
                                hi_halves(i, last, 0, *tiles[s - 2], hT)
                    if UP0 <= c < DOWN0:
                        b = c - UP0
                        act.wait_ge(pair_done, 2 * FJOBS * i + 2 * b + 1)
                        act.wait_ge(f_lo, FJOBS * i + max(b - 1, 0))
                        A.activation(act1[:, b % 2, 0:GROUP], ACC[b % 2 * 2][:], ACT.Silu).then_inc(silu_done, 1)
                        if last:
                            act.wait_ge(spair_done, 2 * b + 1)
                            A.activation(act1[:, b % 2, GROUP:], TB[0][:, 0:NS], ACT.Silu).then_inc(ssilu_done, 1)
                        act.wait_ge(f_ready, FJOBS * i + b + 1)
                        if last:
                            act.wait_ge(sf_ready, b + 1)
                        if b == 0:
                            act.wait_ge(x1_out, 16 * (TILES * i + len(tiles)))
                        A.activation(fT[:, b, 0, 0:wide], act1[:, b % 2, 0:wide], ACT.Copy).then_inc(f_hi, 1)
                    if c == MIXED + 1:
                        for t, col, n in tiles:
                            act.wait_ge(pt_done, TILES * i + t + 1)
                            A.activation(pT[:, 0, :, col:col + n], PB[:, 0:2 * n].rearrange("p (k t) -> p k t", k=2), ACT.Copy).then_inc(pt_hi, 1)
                    if c == PROJ:
                        for s in range(len(tiles) + 3):
                            if s < len(tiles):
                                norm(i, link, 2, *tiles[s][::2], fo_ready, fo)
                                t, _, n = tiles[s]
                                for d in range(2):
                                    act.wait_ge(proj_done, 2 * TILES * i + 2 * t + d + 1)
                                    A.activation(pr[0:n, t, d * 512:d * 512 + 512], PRJ[d][0:n], ACT.Copy).then_inc(proj_free, 1)
                            if s >= 3:
                                hi_halves(i, last, 1, *tiles[s - 3], x2T)
                    if c in (GATE0 + 1, GATE0 + 3):
                        d = (c - GATE0) // 2
                        for t, _, n in tiles:
                            act.wait_ge(acc_done, acc_job(i, last, 2, d, t))
                            act.wait_ge(v_ready, 2 * TILES * i + max(len(tiles) * d + t - 1, 0))
                            A.activation(act1[0:n, (len(tiles) * d + t) % 2, 0:512], ACC[t][0:n], ACT.Sigmoid).then_inc(sig_ready, 1)
                for t, _, n in tiles:
                    act.wait_ge(v_ready, 2 * TILES * i + len(tiles) + t + 1)
                    link(A.activation(junk[0:n], pr[0:n, t], ACT.Square, accum_out=ss[0:n, 3, t:t + 1]))
                    A.activation(rs[0:n, 3, t:t + 1], ss[0:n, 3, t:t + 1], ACT.Sqrt, bias=eps[0:n], scale=1.0 / D).then_inc(std[3], 1)

            with act.Fori(0, GROUPS - 1) as i:
                group(i, False)
            group(GROUPS - 1, True)

        @block.vector
        def _(dve):
            V = nc.vector
            V.memset(eps[:], EPS).then_inc(ready0, 1)

            def split_lo(n, c):
                dve.wait_ge(w_hi, n)
                V.tensor_tensor(w[:, c % RING, 1], raw[:, c % RAW], w[:, c % RING, 0].bitcast(F32), ALU.subtract).then_inc(w_ready, 1)

            for c in range(AHEAD):
                split_lo(c + 1, c)

            def group(i, last, link):
                tiles = group_tiles(last)
                wide = WIDE if last else GROUP
                dve.wait_ge(mix_hi, i + 1)
                V.tensor_tensor(hT[:, 1, :, 0:wide], mix[:, :, 0:wide], hT[:, 0, :, 0:wide].bitcast(F32), ALU.subtract).then_inc(mix_ready, 1)

                def copies(phase, d, dst, ready):
                    for t, _, n in tiles:
                        dve.wait_ge(acc_done, acc_job(i, last, phase, d, t))
                        V.tensor_copy(dst[0:n, t, d * 512:d * 512 + 512], ACC[t][0:n]).then_inc(acc_free, 1)

                def scaled(k, t, n, src, dst):
                    dve.wait_ge(std[k], TILES * i + t + 1)
                    link(V.reciprocal(rs[0:n, k, t:t + 1], rs[0:n, k, t:t + 1]))
                    if t == 0:
                        dve.wait_ge(gain_in[k % 2], 16 * (2 * i + k // 2 + 1))
                    return V.scalar_tensor_tensor(dst, src, rs[0:n, k, t:t + 1], gains[0:n, k % 2], ALU.mult, ALU.mult)

                def lo_halves(phase, t, col, n, dst):
                    for half in range(2):
                        dve.wait_ge(t_hi, T_PER * i + 2 * len(tiles) * phase + 2 * t + half + 1)
                        to = dst[:, :, 4 * half:4 * half + 4, col:col + n]
                        V.tensor_tensor(to[:, 1], TB[half][:, 0:4 * n].rearrange("p (k t) -> p k t", k=4), to[:, 0].bitcast(F32), ALU.subtract).then_inc(t_lo, 1)

                for c in range(CH):
                    if c + AHEAD < CH or not last:
                        split_lo(CH * i + c + AHEAD + 1, (c + AHEAD) % CH)
                    if c == 1:
                        copies(0, 0, mo, None)
                    if c == 3:
                        for s in range(len(tiles) + 2):
                            if s < len(tiles):
                                t, _, n = tiles[s]
                                dve.wait_ge(acc_done, acc_job(i, last, 0, 1, t))
                                link(V.tensor_copy(mo[0:n, t, 512:], ACC[t][0:n]))
                                V.nop().then_inc(mo_ready, 1)
                            if 1 <= s <= len(tiles):
                                t, _, n = tiles[s - 1]
                                if t == 0:
                                    dve.wait_ge(y_out, 16 * TILES * i)
                                link(scaled(0, t, n, mo[0:n, t], mo[0:n, t]))
                                dve.wait_ge(xr_in[t % 2], XR * i + 16 * (t // 2 + 1))
                                V.tensor_tensor(x1[0:n, t], mo[0:n, t], xr[0:n, t % 2], ALU.add).then_inc(x1_ready, 1)
                            if s >= 2:
                                t, col, n = tiles[s - 2]
                                if t >= 2:
                                    dve.wait_ge(tp_done, T_PER * i + 2 * (t - 1))
                                scaled(1, t, n, x1[0:n, t], hn[0:n, t % 2]).then_inc(hn_ready, 1)
                                lo_halves(0, t, col, n, hT)
                    if UP0 <= c < DOWN0:
                        b = c - UP0
                        dve.wait_ge(pair_done, 2 * FJOBS * i + 2 * b + 2)
                        dve.wait_ge(silu_done, FJOBS * i + b + 1)
                        V.tensor_tensor(act1[:, b % 2, 0:GROUP], act1[:, b % 2, 0:GROUP], ACC[b % 2 * 2 + 1][:], ALU.mult).then_inc(f_ready, 1)
                        if last:
                            dve.wait_ge(spair_done, 2 * b + 2)
                            dve.wait_ge(ssilu_done, b + 1)
                            V.tensor_tensor(act1[:, b % 2, GROUP:], act1[:, b % 2, GROUP:], TB[1][:, 0:NS], ALU.mult).then_inc(sf_ready, 1)
                        dve.wait_ge(f_hi, FJOBS * i + b + 1)
                        V.tensor_tensor(fT[:, b, 1, 0:wide], act1[:, b % 2, 0:wide], fT[:, b, 0, 0:wide].bitcast(F32), ALU.subtract).then_inc(f_lo, 1)
                    if c == MIXED:
                        for t, _, n in tiles:
                            dve.wait_ge(acc_done, acc_job(i, last, 1, 0, t))
                            V.tensor_copy(fo[0:n, t, 0:512], ACC[t][0:n]).then_inc(acc_free, 1)
                    if c == MIXED + 1:
                        for t, col, n in tiles:
                            dve.wait_ge(pt_hi, TILES * i + t + 1)
                            V.tensor_tensor(pT[:, 1, :, col:col + n], PB[:, 0:2 * n].rearrange("p (k t) -> p k t", k=2),
                                            pT[:, 0, :, col:col + n].bitcast(F32), ALU.subtract).then_inc(pt_lo, 1)
                    if c == PROJ - 1:
                        for t, _, n in tiles:
                            dve.wait_ge(acc_done, acc_job(i, last, 1, 1, t))
                            link(V.tensor_copy(fo[0:n, t, 512:], ACC[t][0:n]))
                            V.nop().then_inc(fo_ready, 1)
                    if c == PROJ:
                        for s in range(len(tiles) + 3):
                            if s < len(tiles):
                                t, _, n = tiles[s]
                                link(scaled(2, t, n, fo[0:n, t], fo[0:n, t]))
                                if t < 2:
                                    dve.wait_ge(xr_in[t % 2], XR * i + 16 * (len(tiles[t::2]) + 1))
                                else:
                                    dve.wait_ge(xr_in[t % 2], XR * i + 16 * (len(tiles[t % 2::2]) + t // 2 + 1))
                                V.tensor_tensor(x2[0:n, t], fo[0:n, t], xr[0:n, t % 2], ALU.add).then_inc(x2_ready, 1)
                            if s >= 3:
                                t, col, n = tiles[s - 3]
                                lo_halves(1, t, col, n, x2T)
                    if c in (GATE0 + 1, GATE0 + 3):
                        d = (c - GATE0) // 2
                        for t, _, n in tiles:
                            j = len(tiles) * d + t
                            dve.wait_ge(sig_ready, 2 * TILES * i + j + 1)
                            if d == 0:
                                dve.wait_ge(proj_free, 2 * TILES * i + 2 * t + 2)
                            half = pr[0:n, t, d * 512:d * 512 + 512]
                            V.tensor_tensor(half, half, act1[0:n, j % 2, 0:512], ALU.mult).then_inc(v_ready, 1)
                for t, _, n in tiles:
                    link(scaled(3, t, n, pr[0:n, t], pr[0:n, t]))
                    V.tensor_tensor(x2[0:n, t], pr[0:n, t], x2[0:n, t], ALU.add).then_inc(y_ready, 1)

            XR = 64
            LINKS = 9 * TILES
            with dve.Fori(0, GROUPS - 1) as i:
                link = Chain(dve, dve_chain, LINKS * i)
                group(i, False, link)
                assert link.n == LINKS, (link.n, LINKS)
            group(GROUPS - 1, True, Chain(dve, dve_chain, LINKS * (GROUPS - 1)))

        @block.tensor
        def _(pe):
            pe.wait_ge(consts_in, 16)

            def products(out, blocks, lhs, rhs, first=True, end=True):
                for k in range(blocks):
                    for n, (a, b) in enumerate(PRODUCTS):
                        ins = nc.tensor.matmul(out, lhs(k, a), rhs(k, b), start=first and k == 0 and n == 0,
                                               stop=end and k == blocks - 1 and n == 2)
                return ins

            def group(i, last):
                tiles = group_tiles(last)
                per = len(tiles)
                pe.wait_ge(mix_ready, i + 1)

                def transposes(phase, t, n, ready, src, slot):
                    pe.wait_ge(ready, TILES * i + t + 1)
                    for half in range(2):
                        pe.wait_ge(t_lo, T_PER * i + max(2 * per * phase + 2 * t + half - 1, 0))
                        for k in range(4):
                            kk = 4 * half + k
                            ins = nc.tensor.transpose(TB[half][:, k * n:k * n + n], src[0:n, slot, kk * P:kk * P + P], ident[0:n, 0:n])
                        ins.then_inc(tp_done, 1)

                def accumulate(phase, d, blocks, lhs, rhs, first, end, plain):
                    for t, col, n in tiles:
                        if first and (t < TILES or phase or d):
                            pe.wait_ge(acc_free_of(phase, d, t)[0], acc_free_of(phase, d, t)[1])
                        ins = products(ACC[t][0:n], blocks, lambda k, a: lhs(k, a)[:, col:col + n], rhs, first, end)
                        if end:
                            ins.then_inc(acc_done, 1)
                    if not end and plain:
                        ins.then_inc(w_used, 1)

                def acc_free_of(phase, d, t):
                    if phase == 0 and d == 0:
                        return sig_ready, 2 * TILES * i
                    if phase == 0:
                        return acc_free, 2 * TILES * i + t + 1
                    if phase == 1 and d == 0:
                        return (f_ready, FJOBS * (i + 1)) if t < 4 else (mo_ready, TILES * i + per)
                    if phase == 1:
                        return acc_free, 2 * TILES * i + per + t + 1
                    if d == 0:
                        return (fo_ready, TILES * i + t + 1) if t < 4 else (proj_free, 2 * TILES * i + 2 * per)
                    return sig_ready, 2 * TILES * i + t + 1

                for c in range(CH):
                    pe.wait_ge(w_ready, CH * i + c + 1)
                    wv = w[:, c % RING].rearrange("p a (k n) -> p a k n", n=512)
                    if c < UP0:
                        kh = 4 * (c % 2)
                        accumulate(0, c // 2, 4, lambda k, a: hT[:, a, kh + k], lambda k, b: wv[:, b, k], c % 2 == 0, c % 2 == 1, True)
                    if c == UP0 - 1:
                        for t, _, n in tiles:
                            transposes(0, t, n, hn_ready, hn, t % 2)
                        pe.wait_ge(t_lo, T_PER * i + 2 * per)
                    if UP0 <= c < DOWN0:
                        b = c - UP0
                        wb = w[:, c % RING].rearrange("p a (g k n) -> p a g k n", g=2, n=P)
                        for g in range(2):
                            if g == 0:
                                if b >= 2:
                                    pe.wait_ge(f_ready, FJOBS * i + b - 1)
                                else:
                                    pe.wait_ge(mo_ready, TILES * i + per)
                            products(ACC[b % 2 * 2 + g][:], KD, lambda k, a: wb[:, a, g, k], lambda k, r: hT[:, r, k, 0:GROUP]).then_inc(pair_done, 1)
                            if last:
                                if b:
                                    pe.wait_ge(sf_ready, b)
                                products(TB[g][:, 0:NS], KD, lambda k, a: wb[:, a, g, k], lambda k, r: hT[:, r, k, GROUP:]).then_inc(spair_done, 1)
                    if c == DOWN0:
                        pe.wait_ge(f_lo, FJOBS * (i + 1))
                    if DOWN0 <= c < MIXED:
                        kb = 4 * (c - DOWN0)
                        accumulate(1, 0, 4, lambda k, a: fT[:, kb + k, a], lambda k, b: wv[:, b, k], c == DOWN0, False, True)
                    if c == MIXED:
                        accumulate(1, 0, 2, lambda k, a: fT[:, 20 + k, a], lambda k, b: wv[:, b, k], False, True, False)
                        accumulate(1, 1, 2, lambda k, a: fT[:, 20 + k, a], lambda k, b: wv[:, b, 2 + k], True, False, True)
                    if MIXED < c < PROJ:
                        kb = 4 * (c - MIXED - 1)
                        accumulate(1, 1, 4, lambda k, a: fT[:, kb + k, a], lambda k, b: wv[:, b, k], False, c == PROJ - 1, True)
                    if c == MIXED + 1:
                        for t, _, n in tiles:
                            pe.wait_ge(p_in[t % 2], 16 * (2 * i + t // 2 + 1))
                            pe.wait_ge(pt_lo, TILES * i + t)
                            pe.wait_ge(proj_free, 2 * TILES * i)
                            for k in range(2):
                                ins = nc.tensor.transpose(PB[:, k * n:k * n + n], pin[0:n, t % 2, k * P:k * P + P], ident[0:n, 0:n])
                            ins.then_inc(pt_done, 1)
                    if c == PROJ:
                        pe.wait_ge(pt_lo, TILES * i + per)
                        if last:
                            pe.wait_ge(fo_ready, TILES * i + per)
                        wq = w[:, c % RING].rearrange("p a (k d n) -> p a k d n", k=2, d=2)
                        for t, col, n in tiles:
                            for d in range(2):
                                pe.wait_ge(proj_free, 2 * TILES * i + max(2 * t + d - 1, 0))
                                products(PRJ[d][0:n], 2, lambda k, a: pT[:, a, k, col:col + n], lambda k, b: wq[:, b, k, d]).then_inc(proj_done, 1)
                        for t, _, n in tiles:
                            transposes(1, t, n, x2_ready, x2, t)
                        pe.wait_ge(t_lo, T_PER * i + 4 * per)
                    if c >= GATE0:
                        g = c - GATE0
                        kh = 4 * (g % 2)
                        accumulate(2, g // 2, 4, lambda k, a: x2T[:, a, kh + k], lambda k, b: wv[:, b, k], g % 2 == 0, g % 2 == 1, True)

            with pe.Fori(0, GROUPS - 1) as i:
                group(i, False)
            group(GROUPS - 1, True)


def build(nc, io):
    with ExitStack() as sems:
        for stage in (project, attend_prompt, attend_sample, mix_and_feed):
            stage(nc, io, sems)


_INS = ["x_prompt", "x_sample", "cache_k", "cache_v", "state_conv", "state_h", "page_table", "p_prompt", "p_sample",
        "norm_pre_mix", "w_in", "conv_w", "conv_b", "lru_w_a", "lru_b_a", "lru_w_x", "lru_b_x", "lru_L",
        "lambda_q1", "lambda_k1", "lambda_q2", "lambda_k2", "subln_g", "w_out", "norm_post_mix",
        "norm_pre_ffn", "ffn_w_gate", "ffn_w_up", "ffn_w_down", "norm_post_ffn",
        "ple_w_gate", "ple_w_proj", "ple_norm"]
_OUTS = [("y_prompt", (1, SEQ, D)), ("y_sample", (NS, 1, D)),
         ("k_prompt", (1, 1, SEQ, HEADS, P)), ("v_prompt", (1, 1, SEQ, HEADS, P)),
         ("conv_prompt", (1, 1, TAPS - 1, LRU)), ("h_prompt", (1, 1, LRU)),
         ("k_sample", (1, NS, 1, HEADS, P)), ("v_sample", (1, NS, 1, HEADS, P)),
         ("conv_sample", (1, NS, TAPS - 1, LRU)), ("h_sample", (1, NS, LRU))]
_SCRATCH = [("q", (SEQ + NS, LRU)), ("mixT", (D, SEQ + NS)), ("x1", (SEQ + NS, D))]


def _constants():
    inv = np.float32(500000.0) ** (-np.arange(0, ROT, 2, dtype=np.float32) / np.float32(ROT))
    positions = np.concatenate([np.arange(SEQ), np.full(NS, PAGES * PAGE)]).astype(np.float32)
    angle = positions[:, None] * inv[None, :]
    key, query = np.arange(P)[None, :], np.arange(P)[:, None]
    return {
        "rope": np.stack([np.cos(angle), np.sin(angle)], 1).astype(np.float32),
        "ident": np.eye(P, dtype=np.float32),
        "mask": np.where(key > query, np.float32(-1e30), np.float32(0.0)).astype(np.float32),
        "sel": np.tile(np.eye(2, dtype=np.float32), (NS * HEADS, 1)),
    }


def kernel(**inputs):
    import concourse.bacc as _bacc
    from concourse.bass_utils import run_bass_kernel_spmd as _run

    nc = _bacc.Bacc("TRN2", target_bir_lowering=False, num_devices=1, dynamic_dma_scratch_size=4096)
    arrays, io = {}, {}
    for name, a in [(n, inputs[n]) for n in _INS] + list(_constants().items()):
        a = np.ascontiguousarray(a)
        arrays[f"in_{name}"] = a
        io[name] = nc.dram_tensor(f"in_{name}", a.shape, mybir.dt.from_np(a.dtype), kind="ExternalInput").ap()
    for name, shape in _OUTS:
        io[name] = nc.dram_tensor(f"out_{name}", shape, F32, kind="ExternalOutput").ap()
    for name, shape in _SCRATCH:
        io[name] = nc.dram_tensor(f"scratch_{name}", shape, F32, kind="Internal").ap()
    build(nc, io)
    r = _run(nc, [arrays], core_ids=[0])
    return tuple(r.results[0][f"out_{name}"] for name, _ in _OUTS)
```

```python
from contextlib import ExitStack

import numpy as np

import concourse.bass as bass
from concourse import mybir

F32 = mybir.dt.float32
F32R = mybir.dt.float32r
I32 = mybir.dt.int32
ALU = mybir.AluOpType
ACT = mybir.ActivationFunctionType
AX = mybir.AxisListType.X

P = 128
D = 1024
SEQ = 2048
GROUP = 512
GROUPS = SEQ // GROUP
TILES = GROUP // P
NS = 8
WIDE = GROUP + NS
KD = D // P
LRU = 512
LC = LRU // P
TAPS = 4
HEADS = 4
HD = 64
COMP = 2 * HEADS
ROT = HD // 4
HALF = ROT // 2
PAGE = 128
PAGES = 4
FF = 2816
FB = FF // P
PLE = 256
EPS = 1e-6
EPS_SUBLN = 1e-5
LAM_INIT = 0.2
QSCALE = HD ** -0.5

PRODUCTS = ((0, 0), (0, 1), (1, 0))


class Chain:

    def __init__(self, eng, sem, base=0):
        self.eng, self.sem, self.base, self.n = eng, sem, base, 0

    def __call__(self, instruction):
        self.n += 1
        instruction.then_inc(self.sem, 1)
        self.eng.wait_ge(self.sem, self.base + self.n)


def wait_if_any(eng, sem, count):
    if not isinstance(count, int) or count > 0:
        eng.wait_ge(sem, count)


def first_turn(i):
    return isinstance(i, int) and i == 0


def group_tiles(last):
    return [(t, t * P, P) for t in range(TILES)] + ([(TILES, GROUP, NS)] if last else [])


def project(nc, io, sems, pool_turn):
    ctx = ExitStack()
    sb = lambda name, shape, dt=F32: ctx.enter_context(nc.sbuf_tensor(name, shape, dt))
    sem = lambda name: sems.enter_context(nc.semaphore(name))
    CH = 10
    SLOT = (0, 1, 2, 3, 0, 1, 2, 3, 1, 2)
    FREED = [max([b + 1 - (CH if b >= c else 0) for b in range(CH) if SLOT[b] == SLOT[c] and b != c and b < c] or
                 [max(b for b in range(CH) if SLOT[b] == SLOT[c]) + 1 - CH]) for c in range(CH)]
    RAW = 2
    AHEAD = 2
    N_CONST = 2 + LC + 4 + 4
    JOBS = 20
    with ctx:
        ident = sb("a_ident", [P, P])
        gain = sb("a_gain", [P, D])
        convw = sb("a_convw", [P, LC, TAPS])
        convb = sb("a_convb", [P, LC])
        gate_b = sb("a_gate_b", [P, 2, LC])
        gate_w = sb("a_gate_w", [P, 2, LC, P])
        lru_l = sb("a_lru_l", [P, LC])
        sp_t = sb("a_sp_t", [P, 6, LC])
        sp8 = sb("a_sp8", [P, LC])
        nsp8 = sb("a_nsp8", [P, LC])
        eps = sb("a_eps", [P, 1])
        rope = sb("a_rope", [P, SEQ // P, 2, HALF])
        rope_s = sb("a_rope_s", [NS, 2, HALF])
        x = sb("a_x", [P, TILES, D])
        junk = sb("a_junk", [P, D], mybir.dt.bfloat16)
        ssq = sb("a_ssq", [P, TILES + 1])
        rstd = sb("a_rstd", [P, TILES + 1])
        hn = sb("a_hn", [P, 2, D])
        hT = sb("a_hT", [P, 2, KD, WIDE], F32R)
        raw = sb("a_raw", [P, RAW, 2048])
        w = sb("a_w", [P, max(SLOT) + 1, 2, 2048], F32R)
        xpad = sb("a_xpad", [P, LC, TAPS - 1 + GROUP])
        xc = sb("a_xc", [P, LC, GROUP])
        gg = sb("a_gg", [P, LC, GROUP])
        ri = sb("a_ri", [P, 2, GROUP])
        u = sb("a_u", [P, GROUP])
        aa = sb("a_aa", [P, 2, GROUP])
        rec = sb("a_rec", [P, GROUP])
        igx = sb("a_igx", [P, 2, GROUP])
        hs = sb("a_hs", [P, 2, GROUP])
        hlast = sb("a_hlast", [P, LC])
        lo_out = sb("a_lo_out", [P, 2, GROUP])
        rows = sb("a_rows", [P, 3, 512])
        rt = sb("a_rt", [P, 4, COMP, HALF])
        s_xl = sb("a_s_xl", [P, LC, NS])
        s_gg = sb("a_s_gg", [P, LC, NS])
        s_conv = sb("a_s_conv", [P, LC, TAPS - 1, NS])
        s_h = sb("a_s_h", [P, LC, NS])
        s_w = sb("a_s_w", [P, 12, LC, NS])
        s_ri = sb("a_s_ri", [P, 2, LC, NS])
        banks = [ctx.enter_context(nc.psum_tensor(f"a_bank{n}", [P, 512], F32)) for n in range(8)]
        TB = banks[0:2]
        ACC = banks[2:6]
        SB_, GB = banks[6], (banks[7], banks[0])
        norm_in = sem("a_norm_consts_in")
        consts_in = sem("a_consts_in")
        ready0 = sem("a_memsets")
        eps_ready = sem("a_eps_ready")
        sp_chain_a = sem("a_softplus_act")
        sp_ready = sem("a_softplus_ready")
        x_in = [sem(f"a_x_in{n}") for n in range(2)]
        act_chain = sem("a_act_chain")
        dve_chain = sem("a_dve_chain")
        std_ready = sem("a_std_ready")
        hn_ready = sem("a_hn_ready")
        tp_done = sem("a_transposed")
        hi_ready = sem("a_hT_hi")
        lo_ready = sem("a_hT_ready")
        raw_in = [sem(f"a_raw_in{n}") for n in range(RAW)]
        w_hi = sem("a_w_hi")
        w_ready = sem("a_w_ready")
        half_used = sem("a_half_used")
        job_done = sem("a_job_done")
        job_free = sem("a_job_free")
        sjob_done = sem("a_sample_job_done")
        sjob_free = sem("a_sample_job_free")
        xc_ready = sem("a_xc_ready")
        gate_done = sem("a_gate_done")
        gate_free = sem("a_gate_free")
        tanh_ready = sem("a_tanh_ready")
        quot_ready = sem("a_quotient_ready")
        root_ready = sem("a_root_ready")
        lru_done = sem("a_lru_done")
        rows_ready = sem("a_rows_ready")
        rows_out = [sem(f"a_rows_out{n}") for n in range(3)]
        lru_out = [sem(f"a_lru_out{n}") for n in range(2)]
        small_in = sem("a_small_in")
        small_ready = sem("a_small_ready")
        small_out = sem("a_small_out")
        s_chain = sem("a_s_act_chain")
        s_xc_ready = sem("a_s_xc_ready")
        s_gate_done = sem("a_s_gate_done")
        s_r_ready = sem("a_s_r_ready")
        s_t_ready = sem("a_s_t_ready")
        s_q_ready = sem("a_s_q_ready")

        x_v = io["x_prompt"].rearrange("b (g t p) d -> (b g) t p d", g=GROUPS, p=P)
        w_v = io["w_in"][0].rearrange("(k p) n -> p k n", p=P)

        def chunk(c):
            return w_v[:, :, c * 256:c * 256 + 256] if c < 4 else (
                w_v[:, (c % 2) * 4:(c % 2) * 4 + 4, 1024 + (c - 4) // 2 * 512:1536 + (c - 4) // 2 * 512])

        def width(c):
            return 256 if c < 4 else 512

        def job_bank(j):
            return ACC[j % 4]

        q_v = io["q"][0:SEQ].rearrange("(g t p) n -> g t p n", g=GROUPS, p=P)
        k_v = io["k_prompt"].rearrange("l b (g t p) h e -> (l b g) t p (h e)", g=GROUPS, p=P)
        v_v = io["v_prompt"].rearrange("l b (g t p) h e -> (l b g) t p (h e)", g=GROUPS, p=P)
        s_rows = [io["q"][SEQ:SEQ + NS], io["k_sample"].rearrange("l b s h e -> (l b s) (h e)"),
                  io["v_sample"].rearrange("l b s h e -> (l b s) (h e)")]
        mix_v = io["mixT"][0:LRU].rearrange("(c p) t -> c p t", p=P)

        block = ctx.enter_context(nc.Block())

        @block.sync
        def _(sp):
            def load_x(i, pair):
                sp.dma_start(x[:, 2 * pair:2 * pair + 2], x_v[i, 2 * pair:2 * pair + 2].rearrange("t p d -> p t d")).then_inc(x_in[pair], 16)

            load_x(0, 0)
            sp.dma_start(gain[:], io["norm_pre_mix"].broadcast_to([P, D])).then_inc(norm_in, 16)
            sp.dma_start(ident[:], io["ident"]).then_inc(norm_in, 16)
            load_x(0, 1)
            for c in range(AHEAD):
                sp.dma_start(raw[:, c].rearrange("p (k n) -> p k n", n=width(c)), chunk(c)).then_inc(raw_in[c], 16)
            sp.dma_start(rope[:], io["rope"][0:SEQ].rearrange("(t p) a f -> p t a f", p=P)).then_inc(consts_in, 16)
            sp.dma_start(rope_s[:], io["rope"][SEQ:SEQ + NS]).then_inc(consts_in, 16)
            with nc.allow_non_contiguous_dma("a few vectors, channels onto partitions"):
                for c in range(LC):
                    sp.dma_start(convw[:, c], io["conv_w"][0, :, c * P:(c + 1) * P].rearrange("j p -> p j")).then_inc(consts_in, 16)
                sp.dma_start(convb[:], io["conv_b"][0].rearrange("(c p) -> p c", p=P)).then_inc(consts_in, 16)
                sp.dma_start(lru_l[:], io["lru_L"][0].rearrange("(c p) -> p c", p=P)).then_inc(consts_in, 16)
                for n, name in enumerate(("lru_b_a", "lru_b_x")):
                    sp.dma_start(gate_b[:, n], io[name][0].rearrange("(c h) j -> (h j) c", h=2)).then_inc(consts_in, 16)
                sp.wait_ge(ready0, 1)
                for n, name in enumerate(("lru_w_a", "lru_w_x")):
                    for h in range(2):
                        sp.dma_start(gate_w[h * 64:h * 64 + 64, n, :, h * 64:h * 64 + 64],
                                     io[name][0].rearrange("(c h) i j -> h i c j", h=2)[h]).then_inc(consts_in, 16)
                for c in range(LC):
                    for j in range(TAPS - 1):
                        sp.dma_start(s_conv[:, c, j], io["state_conv"][0, :, j, c * P:(c + 1) * P].rearrange("b p -> p b")).then_inc(small_in, 16)
                    sp.dma_start(s_h[:, c], io["state_h"][0, :, c * P:(c + 1) * P].rearrange("b p -> p b")).then_inc(small_in, 16)

            sp.dma_start(io["conv_sample"][0, :, 0:2], io["state_conv"][0, :, 1:3]).then_inc(small_out, 16)

            def group(i, last):
                if last:
                    sp.wait_ge(hn_ready, 4 * i + 1)
                    sp.dma_start(x[0:NS, 0], io["x_sample"].rearrange("b s d -> (b s) d")).then_inc(x_in[0], 16)
                for c in range(AHEAD, CH):
                    sp.wait_ge(w_ready, CH * i + c - RAW + 1)
                    sp.dma_start(raw[:, c % RAW].rearrange("p (k n) -> p k n", n=width(c)), chunk(c)).then_inc(raw_in[c % RAW], 16)
                    if not last and c in (3, 4):
                        sp.wait_ge(hn_ready, 4 * i + 2 * (c - 3) + 2)
                        load_x(i + 1, c - 3)
                if not last:
                    for c in range(AHEAD):
                        sp.wait_ge(w_ready, CH * i + CH + c - RAW + 1)
                        sp.dma_start(raw[:, c].rearrange("p (k n) -> p k n", n=width(c)), chunk(c)).then_inc(raw_in[c], 16)

            group(0, False)
            with sp.Fori(1, GROUPS - 1) as i:
                group(i, False)
            group(GROUPS - 1, True)
            with nc.allow_non_contiguous_dma("states, a few thousand values"):
                sp.wait_ge(xc_ready, LC * GROUPS)
                sp.wait_ge(s_xc_ready, 1)
                for c in range(LC):
                    ch = slice(c * P, (c + 1) * P)
                    sp.dma_start(io["conv_prompt"][0, 0, :, ch].rearrange("j p -> p j"), xpad[:, c, GROUP:GROUP + 3]).then_inc(small_out, 16)
                    sp.dma_start(io["conv_sample"][0, :, 2, ch].rearrange("b p -> p b"), s_xl[:, c]).then_inc(small_out, 16)
                sp.wait_ge(small_ready, 2)
                sp.dma_start(io["h_prompt"][0, 0].rearrange("(c p) -> p c", p=P), hlast[:]).then_inc(small_out, 16)
                for c in range(LC):
                    ch = slice(c * P, (c + 1) * P)
                    sp.dma_start(io["h_sample"][0, :, ch].rearrange("b p -> p b"), s_w[:, 10, c]).then_inc(small_out, 16)
                    sp.dma_start(io["mixT"][ch, SEQ:SEQ + NS], s_w[:, 11, c]).then_inc(small_out, 16)

        @block.gpsimd
        def _(pool):
            pool.memset(eps[:], EPS)
            pool.memset(gate_w[:], 0.0).then_inc(ready0, 1)

            def group(i, last):
                for which in range(3):
                    for t, _, n in group_tiles(last):
                        r = 4 * which + t
                        if t < TILES:
                            pool.wait_ge(rows_ready, 12 * i + r + 1 + (which if last else 0))
                            slot = (12 * 3 + r + which) % 3 if last else r % 3
                            dst = (q_v, k_v, v_v)[which][i, t]
                        else:
                            pool.wait_ge(rows_ready, 12 * i + 4 * which + which + TILES + 1)
                            slot = (12 * 3 + 4 * which + which + TILES) % 3
                            dst = s_rows[which]
                        pool.sem_inc(pool_turn, 1)
                        pool.dma_start(dst, rows[0:n, slot]).then_inc(rows_out[slot], 16)
                    if which >= 1:
                        for g in ((0, 1), (2, 3))[which - 1]:
                            pool.wait_ge(lru_done, LC * i + g + 1)
                            pool.sem_inc(pool_turn, 1)
                            pool.dma_start(mix_v[g, :, bass.ts(i, GROUP)], lo_out[:, g % 2]).then_inc(lru_out[g % 2], 16)

            group(0, False)
            with pool.Fori(1, GROUPS - 1) as i:
                group(i, False)
            group(GROUPS - 1, True)
            pool.wait_ge(small_out, 16 * (4 * LC + 2))
            for n in range(3):
                pool.wait_ge(rows_out[n], 16 * 17)
            for n in range(2):
                pool.wait_ge(lru_out[n], 16 * 2 * GROUPS)

        def chunk_used(eng, i, n, last):
            before, c = ((i - 1), n - 1 + CH) if n <= 0 else (i, n - 1)
            which = (c - 4) // 2
            if c >= 4 and c % 2 == 0:
                eng.wait_ge(half_used, 3 * before + which + 1)
            else:
                wait_if_any(eng, job_done, JOBS * before + (2 * c + 2 if c < 4 else 8 + 4 * which + 4))
                if last and n > 0:
                    eng.wait_ge(sjob_done, 2 * c + 2 if c < 4 else 8 + which + 1)

        def row_slot(i, last, which, t):
            if last:
                r = 36 + 5 * which + t
                return r % 3, r, r // 3
            r = 4 * which + t
            return r % 3, 12 * i + r, 4 * i + r // 3

        @block.scalar
        def _(act):
            def split_first(c):
                act.wait_ge(raw_in[c], 16)
                nc.scalar.activation(w[:, c, 0], raw[:, c], ACT.Copy).then_inc(w_hi, 1)

            def softplus():
                act.wait_ge(sp_chain_a, 1)
                nc.scalar.activation(sp_t[:, 1], sp_t[:, 0], ACT.Exp, scale=-1.0).then_inc(eps_ready, 1)
                act.wait_ge(sp_chain_a, 2)
                nc.scalar.activation(sp_t[:, 3], sp_t[:, 2], ACT.Ln).then_inc(eps_ready, 1)
                act.wait_ge(sp_ready, 1)

            def root(i, g):
                act.wait_ge(quot_ready, LC * i + g + 1)
                wait_if_any(act, lru_done, LC * i + g)
                nc.scalar.activation(rec[:], rec[:], ACT.Sqrt, scale=2.0).then_inc(root_ready, 1)

            for c in range(AHEAD):
                split_first(c)
            act.wait_ge(ready0, 1)

            def group(i, last):
                for t, col, n in group_tiles(last):
                    act.wait_ge(x_in[t % TILES // 2], 16 * (i + 1 + t // TILES))
                    nc.scalar.activation(junk[0:n], x[0:n, t % TILES], ACT.Square, accum_out=ssq[0:n, t:t + 1]).then_inc(act_chain, 1)
                    act.wait_ge(act_chain, 4 * i + t + 1)
                    nc.scalar.activation(ssq[0:n, t:t + 1], ssq[0:n, t:t + 1], ACT.Sqrt, bias=eps[0:n], scale=1.0 / D).then_inc(std_ready, 1)
                    if t >= 1:
                        hi_halves(i, t - 1, col - P, P)
                hi_halves(i, t, col, n)
                for c in range(CH):
                    if c + AHEAD < CH:
                        split_in(i, c + AHEAD, last)
                    elif not last:
                        split_in(i + 1, c + AHEAD - CH, False)
                    if c == 0 and first_turn(i):
                        softplus()
                    if c < 4:
                        for f in range(2):
                            j, fc = 2 * c + f, (2 * c + f) % 4
                            act.wait_ge(job_done, JOBS * i + j + 1)
                            if c < 2:
                                wait_if_any(act, xc_ready, LC * i)
                                nc.scalar.activation(xpad[:, fc, 3:], job_bank(j)[:], ACT.Copy).then_inc(job_free, 1)
                            else:
                                wait_if_any(act, lru_done, LC * i)
                                nc.scalar.activation(gg[:, fc], job_bank(j)[:], ACT.Gelu_apprx_tanh).then_inc(job_free, 1)
                            if last:
                                act.wait_ge(sjob_done, j + 1)
                                if c < 2:
                                    nc.scalar.activation(s_xl[:, fc], SB_[:, 0:NS], ACT.Copy).then_inc(sjob_free, 1)
                                else:
                                    nc.scalar.activation(s_gg[:, fc], SB_[:, 0:NS], ACT.Gelu_apprx_tanh).then_inc(sjob_free, 1)
                    if c >= 6 and c < 10:
                        root(i, c - 6)
                    if c >= 5 and c % 2 == 1:
                        which = (c - 5) // 2
                        for t, _, n in group_tiles(last):
                            slot, before, uses = row_slot(i, last, which, t)
                            wait_if_any(act, rows_out[slot], 16 * uses)
                            if t < TILES:
                                act.wait_ge(job_done, JOBS * i + 8 + 4 * which + t + 1)
                                nc.scalar.activation(rows[:, slot], ACC[t][:], ACT.Copy).then_inc(job_free, 1)
                            else:
                                act.wait_ge(sjob_done, 8 + which + 1)
                                nc.scalar.activation(rows[0:n, slot], SB_[0:n], ACT.Copy).then_inc(sjob_free, 1)
                    if c >= 5 and c < 9:
                        gates(i, c - 5)
                if last:
                    sample_gates()

            def hi_halves(i, t, col, n):
                for half in range(2):
                    if t == 0 and half == 0:
                        wait_if_any(act, job_done, JOBS * i)
                    act.wait_ge(tp_done, 8 * i + 2 * t + half + 1)
                    nc.scalar.activation(hT[:, 0, 4 * half:4 * half + 4, col:col + n],
                                         TB[half][:, 0:4 * n].rearrange("p (k t) -> p k t", k=4), ACT.Copy).then_inc(hi_ready, 1)

            def split_in(i, c, last):
                act.wait_ge(raw_in[c % RAW], 16 * (CH // RAW * i + c // RAW + 1))
                chunk_used(act, i, FREED[c] if c < AHEAD else max(FREED[c], 0), last)
                nc.scalar.activation(w[:, SLOT[c], 0], raw[:, c % RAW], ACT.Copy).then_inc(w_hi, 1)

            def gates(i, g):
                act.wait_ge(gate_done, LC * i + g + 1)
                wait_if_any(act, quot_ready, LC * i + g)
                nc.scalar.activation(ri[:, 0], GB[0][:], ACT.Sigmoid, bias=gate_b[:, 0, g:g + 1]).then_inc(gate_free, 1)
                nc.scalar.activation(ri[:, 1], GB[1][:], ACT.Sigmoid, bias=gate_b[:, 1, g:g + 1]).then_inc(gate_free, 1)
                act.wait_ge(gate_free, 2 * (LC * i + g + 1))
                nc.scalar.activation(u[:], ri[:, 0], ACT.Tanh, scale=sp8[:, g:g + 1])
                wait_if_any(act, lru_done, LC * i + max(g - 1, 0))
                nc.scalar.activation(aa[:, g % 2], ri[:, 0], ACT.Exp, scale=nsp8[:, g:g + 1]).then_inc(tanh_ready, 1)

            def sample_gates():
                act.wait_ge(s_r_ready, 1)
                nc.scalar.activation(s_ri[:], s_ri[:], ACT.Sigmoid).then_inc(s_chain, 1)
                act.wait_ge(s_t_ready, 1)
                nc.scalar.activation(s_w[:, 1], s_w[:, 0], ACT.Tanh)
                nc.scalar.activation(s_w[:, 2], s_w[:, 0], ACT.Exp, scale=-1.0).then_inc(s_chain, 1)
                act.wait_ge(s_q_ready, 1)
                nc.scalar.activation(s_w[:, 6], s_w[:, 5], ACT.Sqrt, scale=2.0).then_inc(s_chain, 1)

            group(0, False)
            with act.Fori(1, GROUPS - 1) as i:
                group(i, False)
            group(GROUPS - 1, True)

        @block.vector
        def _(dve):
            V = nc.vector
            V.memset(hlast[:], 0.0)
            V.memset(xpad[:], 0.0)
            def softplus():
                dve.wait_ge(consts_in, 16 * N_CONST)
                link(V.tensor_scalar(sp_t[:, 4], lru_l[:], -1.0, None, ALU.mult))
                V.tensor_tensor(sp_t[:, 0], sp_t[:, 4], lru_l[:], ALU.max).then_inc(sp_chain_a, 1)
                dve.wait_ge(eps_ready, 1)
                link(V.tensor_scalar(sp_t[:, 2], sp_t[:, 1], 1.0, None, ALU.add))
                V.tensor_scalar(sp_t[:, 5], sp_t[:, 2], -1.0, 1e-30, ALU.add, ALU.max).then_inc(sp_chain_a, 1)
                dve.wait_ge(eps_ready, 2)
                dve.wait_ge(sp_chain_a, 2)
                link(V.reciprocal(sp8[:], sp_t[:, 5]))
                link(V.tensor_tensor(sp8[:], sp8[:], sp_t[:, 3], ALU.mult))
                link(V.tensor_scalar(sp_t[:, 5], sp_t[:, 2], 1.0, None, ALU.is_equal))
                link(V.tensor_tensor(sp8[:], sp8[:], sp_t[:, 5], ALU.add))
                link(V.tensor_tensor(sp8[:], sp8[:], sp_t[:, 1], ALU.mult))
                link(V.tensor_scalar(sp_t[:, 4], sp_t[:, 4], 0.0, None, ALU.max))
                link(V.tensor_tensor(sp8[:], sp8[:], sp_t[:, 4], ALU.add))
                link(V.tensor_scalar(sp8[:], sp8[:], 8.0, None, ALU.mult))
                V.tensor_scalar(nsp8[:], sp8[:], -1.0, None, ALU.mult).then_inc(sp_ready, 1)

            links0 = 10
            LINKS = 64

            def split_lo(n, c):
                dve.wait_ge(w_hi, n)
                V.tensor_tensor(w[:, SLOT[c], 1], raw[:, c % RAW], w[:, SLOT[c], 0].bitcast(F32), ALU.subtract).then_inc(w_ready, 1)

            for c in range(AHEAD):
                split_lo(c + 1, c)

            def lru_head(i, g):
                dve.wait_ge(tanh_ready, LC * i + g + 1)
                link(V.tensor_scalar(rec[:], u[:], 1.0, None, ALU.add))
                link(V.reciprocal(rec[:], rec[:]))
                V.tensor_tensor(igx[:, g % 2], ri[:, 1], xc[:, g], ALU.mult)
                link(V.tensor_tensor(rec[:], u[:], rec[:], ALU.mult))
                V.nop().then_inc(quot_ready, 1)

            def lru_tail(i, g):
                dve.wait_ge(root_ready, LC * i + g + 1)
                link(V.tensor_tensor(igx[:, g % 2], rec[:], igx[:, g % 2], ALU.mult))
                link(V.tensor_tensor_scan(hs[:, g % 2], aa[:, g % 2], igx[:, g % 2], hlast[:, g:g + 1], ALU.mult, ALU.add))
                V.tensor_copy(hlast[:, g:g + 1], hs[:, g % 2, GROUP - 1:GROUP])
                wait_if_any(dve, lru_out[g % 2], 16 * (2 * i + g // 2))
                link(V.tensor_tensor(lo_out[:, g % 2], hs[:, g % 2], gg[:, g], ALU.mult))
                V.nop().then_inc(lru_done, 1)

            def group(i, last):
                if first_turn(i):
                    dve.wait_ge(norm_in, 32)
                for t, col, n in group_tiles(last):
                    dve.wait_ge(std_ready, 4 * i + t + 1)
                    link(V.reciprocal(rstd[0:n, t:t + 1], ssq[0:n, t:t + 1]))
                    if t >= 2:
                        dve.wait_ge(tp_done, 8 * i + 2 * (t - 1))
                    else:
                        wait_if_any(dve, tp_done, 8 * i)
                    V.scalar_tensor_tensor(hn[0:n, t % 2], x[0:n, t % TILES], rstd[0:n, t:t + 1], gain[0:n], ALU.mult, ALU.mult).then_inc(hn_ready, 1)
                    if t >= 1:
                        lo_halves(i, t - 1, col - P, P)
                lo_halves(i, t, col, n)
                for c in range(CH):
                    if c + AHEAD < CH:
                        split_lo(CH * i + c + AHEAD + 1, (c + AHEAD) % CH)
                    elif not last:
                        split_lo(CH * i + c + AHEAD + 1, (c + AHEAD) % CH)
                    if c == 0 and first_turn(i):
                        softplus()
                    if c < 2:
                        for f in range(2):
                            fc = 2 * c + f
                            dve.wait_ge(job_free, JOBS * i + fc + 1)
                            link(V.tensor_scalar(xc[:, fc], xpad[:, fc, 0:GROUP], convw[:, fc, 0:1], convb[:, fc:fc + 1], ALU.mult, ALU.add))
                            for j in range(1, TAPS):
                                link(V.scalar_tensor_tensor(xc[:, fc], xpad[:, fc, j:j + GROUP], convw[:, fc, j:j + 1], xc[:, fc], ALU.mult, ALU.add))
                            if not last:
                                link(V.tensor_copy(xpad[:, fc, 0:3], xpad[:, fc, GROUP:GROUP + 3]))
                            V.nop().then_inc(xc_ready, 1)
                    if c == 3 and last:
                        sample_conv()
                    if c >= 5 and c % 2 == 1:
                        which = (c - 5) // 2
                        for t, _, n in group_tiles(last):
                            slot, before, uses = row_slot(i, last, which, t)
                            if t < TILES:
                                dve.wait_ge(job_free, JOBS * i + 8 + 4 * which + t + 1)
                            else:
                                dve.wait_ge(sjob_free, 8 + which + 1)
                            if which < 2:
                                v = rows[0:n, slot].rearrange("p (c d) -> p c d", d=HD)
                                t1, t2 = v[:, :, 0:HALF], v[:, :, HALF:ROT]
                                table = rope[:, 4 * i + t] if t < TILES and isinstance(i, int) else (rope[:, bass.ds(4 * i + t, 1)].rearrange("p o a f -> p (o a) f") if t < TILES else rope_s[:])
                                cos = table[:, 0:1, :].broadcast_to([n, COMP, HALF])
                                sin = table[:, 1:2, :].broadcast_to([n, COMP, HALF])
                                V.tensor_tensor(rt[0:n, 0], t1, cos, ALU.mult)
                                V.tensor_tensor(rt[0:n, 1], t2, sin, ALU.mult)
                                V.tensor_tensor(rt[0:n, 2], t2, cos, ALU.mult)
                                link(V.tensor_tensor(rt[0:n, 3], t1, sin, ALU.mult))
                                V.tensor_tensor(t1, rt[0:n, 0], rt[0:n, 1], ALU.subtract)
                                link(V.tensor_tensor(t2, rt[0:n, 2], rt[0:n, 3], ALU.add))
                            V.nop().then_inc(rows_ready, 1)
                    if c >= 6:
                        lru_tail(i, c - 6)
                    if c >= 5 and c < 9:
                        lru_head(i, c - 5)
                if last:
                    sample_lru()
                    V.nop().then_inc(small_ready, 1)

            def lo_halves(i, t, col, n):
                for half in range(2):
                    dve.wait_ge(hi_ready, 8 * i + 2 * t + half + 1)
                    dst = hT[:, :, 4 * half:4 * half + 4, col:col + n]
                    V.tensor_tensor(dst[:, 1], TB[half][:, 0:4 * n].rearrange("p (k t) -> p k t", k=4),
                                    dst[:, 0].bitcast(F32), ALU.subtract).then_inc(lo_ready, 1)

            def over(v):
                return v.rearrange("p (c o) -> p c o", o=1).broadcast_to([P, LC, NS])

            def sample_conv():
                dve.wait_ge(small_in, 16 * 4 * LC)
                dve.wait_ge(sjob_free, 4)
                link(V.tensor_tensor(s_w[:, 0], s_conv[:, :, 0], over(convw[:, :, 0]), ALU.mult))
                link(V.tensor_tensor(s_w[:, 7], s_w[:, 0], over(convb[:]), ALU.add))
                for j in range(1, TAPS):
                    tap = s_conv[:, :, j] if j < 3 else s_xl[:]
                    link(V.tensor_tensor(s_w[:, 0], tap, over(convw[:, :, j]), ALU.mult))
                    link(V.tensor_tensor(s_w[:, 7], s_w[:, 7], s_w[:, 0], ALU.add))
                V.nop().then_inc(s_xc_ready, 1)

            def sample_lru():
                dve.wait_ge(s_gate_done, 1)
                V.tensor_tensor(s_ri[:, 0], GB[0][:, 0:LC * NS].rearrange("p (c b) -> p c b", b=NS), over(gate_b[:, 0]), ALU.add)
                link(V.tensor_tensor(s_ri[:, 1], GB[1][:, 0:LC * NS].rearrange("p (c b) -> p c b", b=NS), over(gate_b[:, 1]), ALU.add))
                V.nop().then_inc(s_r_ready, 1)
                dve.wait_ge(s_chain, 1)
                link(V.tensor_tensor(s_w[:, 0], s_ri[:, 0], over(sp8[:]), ALU.mult))
                V.nop().then_inc(s_t_ready, 1)
                link(V.tensor_tensor(s_w[:, 8], s_ri[:, 1], s_w[:, 7], ALU.mult))
                dve.wait_ge(s_chain, 2)
                link(V.tensor_scalar(s_w[:, 3], s_w[:, 1], 1.0, None, ALU.add))
                link(V.reciprocal(s_w[:, 4], s_w[:, 3]))
                link(V.tensor_tensor(s_w[:, 5], s_w[:, 1], s_w[:, 4], ALU.mult))
                V.nop().then_inc(s_q_ready, 1)
                link(V.tensor_tensor(s_w[:, 9], s_w[:, 2], s_h[:], ALU.mult))
                dve.wait_ge(s_chain, 3)
                link(V.tensor_tensor(s_w[:, 8], s_w[:, 8], s_w[:, 6], ALU.mult))
                link(V.tensor_tensor(s_w[:, 10], s_w[:, 8], s_w[:, 9], ALU.add))
                dve.wait_ge(sjob_free, 8)
                link(V.tensor_tensor(s_w[:, 11], s_w[:, 10], s_gg[:], ALU.mult))
                V.nop().then_inc(small_ready, 1)

            link = Chain(dve, dve_chain)
            group(0, False)
            assert link.n == LINKS + links0, link.n
            with dve.Fori(1, GROUPS - 1) as i:
                link = Chain(dve, dve_chain, LINKS * i + links0)
                group(i, False)
                assert link.n == LINKS, link.n
            link = Chain(dve, dve_chain, LINKS * (GROUPS - 1) + links0)
            group(GROUPS - 1, True)

        @block.tensor
        def _(pe):
            pe.wait_ge(norm_in, 32)

            def products(out, blocks, lhs, rhs, first=True, end=True):
                for k in range(blocks):
                    for n, (a, b) in enumerate(PRODUCTS):
                        ins = nc.tensor.matmul(out, lhs(k, a), rhs(k, b), start=first and k == 0 and n == 0,
                                               stop=end and k == blocks - 1 and n == 2)
                return ins

            def group(i, last):
                wait_if_any(pe, gate_free, 2 * LC * i)
                for t, col, n in group_tiles(last):
                    pe.wait_ge(hn_ready, 4 * i + t + 1)
                    for half in range(2):
                        wait_if_any(pe, lo_ready, 8 * i + 2 * t + half - 1 if t else 8 * i)
                        for k in range(4):
                            kk = 4 * half + k
                            ins = nc.tensor.transpose(TB[half][:, k * n:k * n + n], hn[0:n, t % 2, kk * P:kk * P + P], ident[0:n, 0:n])
                        ins.then_inc(tp_done, 1)
                pe.wait_ge(lo_ready, 8 * i + 2 * len(group_tiles(last)))
                for c in range(CH):
                    s = SLOT[c]
                    pe.wait_ge(w_ready, CH * i + c + 1)
                    wv = w[:, s].rearrange("p a (k n) -> p a k n", n=width(c))
                    if c < 4:
                        for f in range(2):
                            j = 2 * c + f
                            wait_if_any(pe, job_free, JOBS * i + max(j - 3, 0))
                            ins = products(job_bank(j)[:], KD, lambda k, a: wv[:, a, k, f * P:f * P + P],
                                     lambda k, b: hT[:, b, k, 0:GROUP])
                            ins.then_inc(job_done, 1)
                            if last:
                                if j:
                                    pe.wait_ge(sjob_free, j)
                                ins = products(SB_[:, 0:NS], KD, lambda k, a: wv[:, a, k, f * P:f * P + P],
                                         lambda k, b: hT[:, b, k, GROUP:WIDE])
                                ins.then_inc(sjob_done, 1)
                    else:
                        which, kh = (c - 4) // 2, c % 2
                        for t, col, n in group_tiles(last):
                            if kh == 0:
                                if t < TILES:
                                    pe.wait_ge(job_free, JOBS * i + 8 + 4 * which + t - 3)
                                else:
                                    pe.wait_ge(sjob_free, 8 + which)
                            out = ACC[t][:] if t < TILES else SB_[0:n]
                            ins = products(out, 4, lambda k, a: hT[:, a, 4 * kh + k, col:col + n],
                                           lambda k, b: wv[:, b, k, :], kh == 0, kh == 1)
                            if kh == 1:
                                ins.then_inc(job_done if t < TILES else sjob_done, 1)
                    if c >= 4 and c % 2 == 0:
                        ins.then_inc(half_used, 1)
                    if 4 <= c < 8:
                        g = c - 4
                        if first_turn(i) and g == 0:
                            pe.wait_ge(consts_in, 16 * N_CONST)
                        pe.wait_ge(xc_ready, LC * i + g + 1)
                        wait_if_any(pe, gate_free, 2 * (LC * i + g))
                        nc.tensor.matmul(GB[0][:], gate_w[:, 0, g], xc[:, g], start=True, stop=True)
                        nc.tensor.matmul(GB[1][:], gate_w[:, 1, g], xc[:, g], start=True, stop=True).then_inc(gate_done, 1)
                if last:
                    pe.wait_ge(s_xc_ready, 1)
                    pe.wait_ge(gate_free, 2 * LC * GROUPS)
                    for g in range(LC):
                        for n in range(2):
                            ins = nc.tensor.matmul(GB[n][:, g * NS:g * NS + NS], gate_w[:, n, g], s_w[:, 7, g], start=True, stop=True)
                    ins.then_inc(s_gate_done, 1)

            group(0, False)
            with pe.Fori(1, GROUPS - 1) as i:
                group(i, False)
            group(GROUPS - 1, True)


def load_pages(eng, table, cache, dst, sequences, arrived):
    for b in sequences:
        for n in range(PAGES):
            page = eng.value_load(table[0:1, b * PAGES + n:b * PAGES + n + 1], min_val=0, max_val=cache.shape[0] - 1)
            eng.dma_start(dst[:, b, n], cache[page]).then_inc(arrived[b // 2], 16)


def attend_prompt(nc, io, sems, pool_turn, table, k_pages, k_in):
    ctx = ExitStack()
    sb = lambda name, shape, dt=F32: ctx.enter_context(nc.sbuf_tensor(name, shape, dt))
    sem = lambda name: sems.enter_context(nc.semaphore(name))
    QT = SEQ // P
    NK = [i // 4 + 1 for i in range(QT)]
    size = lambda i, kc: 512 if kc < NK[i] - 1 else (i % 4 + 1) * P
    before = [sum(NK[:i]) for i in range(QT + 1)]
    CHUNKS = before[QT]
    SCORES = 2 * CHUNKS
    tile_of = [i for i in range(QT) for _ in range(NK[i])]
    last_of = [before[i + 1] - 1 for i in range(QT)]
    RESCALED = [sum(n > 1 for n in NK[:i]) for i in range(QT + 1)]
    ROWS_HI, ROWS_LO, TURN_K, TURN_Q = -6, -5, -4, -3
    SCORE = -1
    SUM = 1
    V_HI, V_LO = 6, 7
    MULT, ADD, WHI, VAL = 5, 6, 7, 8
    OUT = 9
    SQUARE = 10
    ROOT = (last_of[7] + SQUARE + 1, last_of[15] + SQUARE + 1)
    SCALE = (ROOT[0] + 1, ROOT[1] + 1)
    TURN_O = (26, 30, CHUNKS + 13, CHUNKS + 16)
    STORE = (32, CHUNKS + 18)
    PRING, QRING, TRING = 8, 4, 8
    with ctx:
        ident = sb("b_ident", [P, P])
        ident_r = sb("b_ident_r", [P, P], F32R)
        mask_in = sb("b_mask_in", [P, P])
        mask = sb("b_mask", [P, P], F32R)
        lam_in = sb("b_lam_in", [P, 4, HD])
        lam_t = sb("b_lam_t", [P, 2, HD])
        lam_s = sb("b_lam_s", [P, 4])
        nlam = sb("b_nlam", [P, 1])
        gain = sb("b_gain", [P, 1])
        eps = sb("b_eps", [P, 1])
        raw = sb("b_raw", [P, 3, QT, P])
        kin = sb("b_kin", [P, QRING, 2, 2, HD], F32R)
        qin = sb("b_qin", [P, QRING, 2, 2, 2, HD], F32R)
        vv = sb("b_v", [P, QT, 2, P], F32R)
        kT = sb("b_kT", [P, 2, SEQ], F32R)
        qT = sb("b_qT", [P, QRING, 4, P], F32R)
        p = sb("b_p", [P, PRING, 2, 512])
        w = sb("b_w", [P, 2, 512])
        wT = sb("b_wT", [P, 2, 2, 512], F32R)
        m = sb("b_m", [P, TRING, 2, 4])
        nm = sb("b_nm", [P, TRING, 2, 4])
        ls = sb("b_l", [P, TRING, 2, 4])
        top = sb("b_top", [P, 2])
        dm = sb("b_dm", [P, 2, 4])
        al = sb("b_al", [P, 2, 4])
        la = sb("b_la", [P, 2, 4])
        rl = sb("b_rl", [P, 2])
        coef = sb("b_coef", [P, TRING, 2, 4])
        ob = sb("b_ob", [P, P])
        o = sb("b_o", [P, QT, P])
        junk = sb("b_junk", [P, P])
        oss = sb("b_oss", [P, QT])
        ors = sb("b_ors", [P, QT])
        oT = sb("b_oT", [P, SEQ])
        S = [ctx.enter_context(nc.psum_tensor(f"b_S{n}", [P, 2, 512], F32)) for n in range(2)]
        WT = [ctx.enter_context(nc.psum_tensor(f"b_WT{n}", [P, 512], F32)) for n in range(2)]
        O = ctx.enter_context(nc.psum_tensor("b_O", [P, 512], F32))
        M = ctx.enter_context(nc.psum_tensor("b_M", [P, 512], F32))
        table_in = sem("b_table_in")
        consts_in = sem("b_consts_in")
        setup = sem("b_setup")
        lam_sum = sem("b_lam_sum")
        rows_in = [sem(f"b_rows_in{n}") for n in range(4)]
        split_hi = sem("b_split_hi")
        split = sem("b_split")
        v_hi = sem("b_v_hi")
        v_lo = sem("b_v_ready")
        m_done = sem("b_m_done")
        k_free = sem("b_kT_ready")
        q_free = sem("b_qT_ready")
        s_done = sem("b_scores")
        nm_ready = sem("b_nm_ready")
        exp_done = sem("b_exp_done")
        dm_ready = sem("b_dm_ready")
        al_ready = sem("b_al_ready")
        coef_ready = sem("b_coef_ready")
        t2_ready = sem("b_t2_ready")
        w_ready = sem("b_w_ready")
        wt_done = sem("b_wT_in_psum")
        wt_hi = sem("b_wT_hi")
        wt_lo = sem("b_wT_lo")
        pv_done = sem("b_pv_done")
        ob_ready = sem("b_ob_ready")
        o_ready = sem("b_o_ready")
        osq_ready = sem("b_osq_ready")
        std_ready = sem("b_std_ready")
        on_ready = sem("b_on_ready")
        dve_chain = sem("b_dve_chain")
        o_turned = sem("b_o_transposed")
        stored = [sem(f"b_stored{n}") for n in range(2)]
        out_free = sem("b_out_free")
        out_ready = sem("b_out_ready")
        rows_v = [io["q"][0:SEQ].rearrange("(t p) (h e) -> h p t e", p=P, e=P),
                  io["k_prompt"].rearrange("l b (t p) h e -> (l b h) p t e", p=P),
                  io["v_prompt"].rearrange("l b (t p) h e -> (l b h) p t e", p=P)]
        out_v = io["mixT"][LRU:, 0:SEQ].rearrange("(h e) t -> h e t", e=P)
        block = ctx.enter_context(nc.Block())

        @block.sync
        def _(sp):
            sp.dma_start(ident[:], io["ident"]).then_inc(consts_in, 16)
            sp.dma_start(mask_in[:], io["mask"]).then_inc(consts_in, 16)
            for n, name in enumerate(("lambda_q1", "lambda_k1", "lambda_q2", "lambda_k2")):
                sp.dma_start(lam_in[:, n], io[name].broadcast_to([P, HD])).then_inc(consts_in, 16)
            sp.dma_start(gain[:], io["subln_g"].rearrange("l (e o) -> (l e) o", o=1)).then_inc(consts_in, 16)
            for g in range(4):
                for n in range(3):
                    sp.dma_start(raw[:, n, 4 * g:4 * g + 4], rows_v[n][0, :, 4 * g:4 * g + 4]).then_inc(rows_in[g], 16)
            sp.dma_start(table[:], io["page_table"].rearrange("(o b) n -> o (b n)", o=1)).then_inc(table_in, 16)
            sp.wait_ge(table_in, 16)
            load_pages(sp, table, io["cache_k"].rearrange("l n t h e -> (l n) t (h e)"), k_pages, range(NS), k_in)
            with sp.Fori(0, HEADS - 1) as h:
                for g in range(4):
                    sp.wait_ge(v_lo, QT * h + 4 * g + 4)
                    for n in range(3):
                        sp.dma_start(raw[:, n, 4 * g:4 * g + 4], rows_v[n][h + 1, :, 4 * g:4 * g + 4]).then_inc(rows_in[g], 16)

        def due(s, starts, offset, turns):
            found = [(x, *divmod(start + offset, CHUNKS)) for x, start in enumerate(starts)]
            return [(x, k) for x, k, at in found if at == s and k in turns]

        def heads(eng, turn):
            turn(-1, (-1,))
            turn(0, (0, -1))
            with eng.Fori(1, HEADS - 1) as h:
                turn(h, (1, 0, -1))
            turn(HEADS - 1, (1, 0))
            turn(HEADS, (1,))

        CHUNK = range(CHUNKS)
        TILE = before[:QT]

        def first(head):
            return isinstance(head, int) and head == 0

        @block.gpsimd
        def _(pool):
            pool.sem_inc(out_free, 1)

            def turn(h, turns):
                for s in range(CHUNKS):
                    for t, k in due(s, TILE, ROWS_LO, turns):
                        pool.wait_ge(split_hi, QT * (h - k) + t + 1)
                        pool.sem_inc(pool_turn, 1)
                        k_rows = raw[:, 1, t].rearrange("p (c d) -> p c d", d=HD)
                        q_rows = raw[:, 0, t].rearrange("p (c o d) -> p c o d", o=1, d=HD).broadcast_to([P, 2, 2, HD])
                        nc.gpsimd.tensor_tensor(kin[:, t % QRING, :, 1], k_rows, kin[:, t % QRING, :, 0].bitcast(F32), ALU.subtract)
                        nc.gpsimd.tensor_tensor(qin[:, t % QRING, :, 1], q_rows, qin[:, t % QRING, :, 0].bitcast(F32), ALU.subtract).then_inc(split, 1)
                    for t, k in due(s, TILE, V_LO, turns):
                        pool.wait_ge(v_hi, QT * (h - k) + t + 1)
                        pool.sem_inc(pool_turn, 1)
                        nc.gpsimd.tensor_tensor(vv[:, t, 1], raw[:, 2, t], vv[:, t, 0].bitcast(F32), ALU.subtract).then_inc(v_lo, 1)
                    for half, k in due(s, STORE, 0, turns):
                        head = h - k
                        pool.wait_ge(out_ready, 4 * head + 2 * half + 2)
                        pool.sem_inc(pool_turn, 1)
                        cols = slice(half * SEQ // 2, (half + 1) * SEQ // 2)
                        pool.dma_start(out_v[head, :, cols], oT[:, cols]).then_inc(stored[half], 16)
                    if s == CHUNKS - 4 and 1 in turns and 0 in turns:
                        pool.wait_ge(stored[1], 16 * h)
                        pool.sem_inc(out_free, 1)
                    for g, k in due(s, CHUNK, MULT, turns):
                        head, i = h - k, tile_of[g]
                        kc = g - before[i]
                        if kc == 0:
                            pool.wait_ge(coef_ready, QT * head + i + 1)
                            pool.sem_inc(pool_turn, 1)
                        part = p[:, g % PRING, 1, 0:size(i, kc)]
                        nc.gpsimd.tensor_scalar(part, part, coef[:, i % TRING, 1, kc:kc + 1], 1.0, ALU.mult, ALU.mult).then_inc(t2_ready, 1)

            heads(pool, turn)
            for half in range(2):
                pool.wait_ge(stored[half], 16 * HEADS)

        @block.scalar
        def _(act):
            A = nc.scalar
            act.wait_ge(lam_sum, 1)
            A.activation(lam_s[:, 2:4], lam_s[:, 0:2], ACT.Exp).then_inc(setup, 1)
            act.wait_ge(consts_in, 16 * 7)
            A.activation(ident_r[:], ident[:], ACT.Copy)
            A.activation(mask[:], mask_in[:], ACT.Copy).then_inc(setup, 1)

            def turn(h, turns):
                for s in range(CHUNKS):
                    for t, k in due(s, TILE, ROWS_HI, turns):
                        head = h - k
                        if t % 4 == 0:
                            act.wait_ge(rows_in[t // 4], 48 * (head + 1))
                        if t >= QRING or not first(head):
                            act.wait_ge(m_done, 2 * (QT * head + t - QRING + 1))
                        k_rows = raw[:, 1, t].rearrange("p (c d) -> p c d", d=HD)
                        q_rows = raw[:, 0, t].rearrange("p (c o d) -> p c o d", o=1, d=HD).broadcast_to([P, 2, 2, HD])
                        A.activation(kin[:, t % QRING, :, 0], k_rows, ACT.Copy)
                        A.activation(qin[:, t % QRING, :, 0], q_rows, ACT.Copy).then_inc(split_hi, 1)
                    for g, k in due(s, CHUNK, WHI, turns):
                        head, i = h - k, tile_of[g]
                        n = size(i, g - before[i])
                        if g >= 2 or not first(head):
                            act.wait_ge(pv_done, CHUNKS * head + g - 1)
                        act.wait_ge(wt_done, CHUNKS * head + g + 1)
                        A.activation(wT[:, g % 2, 0, 0:n], WT[g % 2][:, 0:n], ACT.Copy).then_inc(wt_hi, 1)
                    for i, k in due(s, last_of, OUT, turns):
                        head = h - k
                        act.wait_ge(pv_done, CHUNKS * head + last_of[i] + 1)
                        if i or not first(head):
                            act.wait_ge(o_ready, QT * head + i)
                        A.activation(ob[:], O[:, P:2 * P], ACT.Copy).then_inc(ob_ready, 1)
                    for i, k in due(s, last_of, SUM, turns):
                        if NK[i] > 1:
                            act.wait_ge(dm_ready, RESCALED[QT] * (h - k) + RESCALED[i] + 1)
                            A.activation(al[:, :, 0:NK[i]], dm[:, :, 0:NK[i]], ACT.Exp, scale=QSCALE).then_inc(al_ready, 1)
                    for g, k in due(s, CHUNK, 0, turns):
                        i = tile_of[g]
                        kc = g - before[i]
                        n = size(i, kc)
                        act.wait_ge(nm_ready, CHUNKS * h + g + 1)
                        if g >= PRING or not first(h):
                            act.wait_ge(w_ready, CHUNKS * h + g - PRING + 1)
                        for c in range(2):
                            A.activation(p[:, g % PRING, c, 0:n], S[g % 2][:, c, 0:n], ACT.Exp, bias=nm[:, i % TRING, c, kc:kc + 1],
                                         scale=QSCALE, accum_out=ls[:, i % TRING, c, kc:kc + 1]).then_inc(exp_done, 1)
                    for t, k in due(s, TILE, V_HI, turns):
                        head = h - k
                        if not first(head):
                            act.wait_ge(pv_done, CHUNKS * (head - 1) + before[QT - 1] + 1 if t < 4 else CHUNKS * head + 1)
                        A.activation(vv[:, t, 0], raw[:, 2, t], ACT.Copy).then_inc(v_hi, 1)
                    for t, k in due(s, TILE, TURN_K, turns):
                        act.wait_ge(m_done, 2 * (QT * (h - k) + t) + 1)
                        A.activation(kT[:, :, t * P:t * P + P], M[:, 0:2 * P].rearrange("p (c t) -> p c t", c=2), ACT.Copy)
                        A.activation(qT[:, t % QRING, 0:2], M[:, 2 * P:4 * P].rearrange("p (a t) -> p a t", a=2), ACT.Copy).then_inc(k_free, 1)
                    for i, k in due(s, last_of, SQUARE, turns):
                        act.wait_ge(o_ready, QT * (h - k) + i + 1)
                        if i or not first(h - k):
                            act.wait_ge(osq_ready, QT * (h - k) + i)
                        A.activation(junk[:], o[:, i], ACT.Square, accum_out=oss[:, i:i + 1]).then_inc(osq_ready, 1)
                    for half, k in due(s, ROOT, 0, turns):
                        part = slice(8 * half, 8 * half + 8)
                        act.wait_ge(osq_ready, QT * (h - k) + 8 * half + 8)
                        A.activation(ors[:, part], oss[:, part], ACT.Sqrt, bias=eps[:], scale=1.0 / P).then_inc(std_ready, 1)

            heads(act, turn)

        @block.vector
        def _(dve):
            V = nc.vector
            V.memset(eps[:], EPS_SUBLN)
            link = Chain(dve, dve_chain)
            dve.wait_ge(consts_in, 16 * 7)
            link(V.tensor_tensor(lam_t[:], lam_in[:, 0:4:2], lam_in[:, 1:4:2], ALU.mult))
            V.reduce_sum(lam_s[:, 0:2], lam_t[:], axis=AX).then_inc(lam_sum, 1)
            dve.wait_ge(setup, 1)
            link(V.tensor_tensor(nlam[:], lam_s[:, 3:4], lam_s[:, 2:3], ALU.subtract))
            link(V.tensor_scalar(nlam[:], nlam[:], -LAM_INIT, None, ALU.add))
            link(V.tensor_scalar(gain[:], gain[:], 1.0 - LAM_INIT, None, ALU.mult))
            links0 = link.n
            LINKS = CHUNKS + 5 * RESCALED[QT] + QT - RESCALED[QT] + 2
            LATE = 5

            def turn(h, turns):
                before_turn = links0 + (0 if 1 not in turns else LINKS * h - LATE)
                link = Chain(dve, dve_chain, before_turn)
                for s in range(CHUNKS):
                    for g, k in due(s, CHUNK, 0, turns):
                        i = tile_of[g]
                        kc = g - before[i]
                        n = size(i, kc)
                        dve.wait_ge(s_done, CHUNKS * h + g + 1)
                        link(V.reduce_max(m[:, i % TRING, :, kc], S[g % 2][:, :, 0:n], axis=AX))
                        V.tensor_scalar(nm[:, i % TRING, :, kc], m[:, i % TRING, :, kc], -QSCALE, None, ALU.mult).then_inc(nm_ready, 1)
                    for g, k in due(s, CHUNK, ADD, turns):
                        head, i = h - k, tile_of[g]
                        kc = g - before[i]
                        n = size(i, kc)
                        dve.wait_ge(t2_ready, CHUNKS * head + g + 1)
                        if g >= 2 or not first(head):
                            dve.wait_ge(wt_hi, CHUNKS * head + g - 1)
                        V.scalar_tensor_tensor(w[:, g % 2, 0:n], p[:, g % PRING, 0, 0:n], coef[:, i % TRING, 0, kc:kc + 1],
                                               p[:, g % PRING, 1, 0:n], ALU.mult, ALU.add).then_inc(w_ready, 1)
                    for g, k in due(s, CHUNK, WHI, turns):
                        n = size(tile_of[g], g - before[tile_of[g]])
                        dve.wait_ge(wt_hi, CHUNKS * (h - k) + g + 1)
                        V.tensor_tensor(wT[:, g % 2, 1, 0:n], WT[g % 2][:, 0:n], wT[:, g % 2, 0, 0:n].bitcast(F32), ALU.subtract).then_inc(wt_lo, 1)
                    for i, k in due(s, last_of, OUT, turns):
                        dve.wait_ge(ob_ready, QT * (h - k) + i + 1)
                        V.tensor_tensor(o[:, i], O[:, 0:P], ob[:], ALU.add).then_inc(o_ready, 1)
                    for b, k in due(s, TURN_O, 1, turns):
                        head = h - k
                        dve.wait_ge(o_turned, 4 * head + b + 1)
                        if b == 0 and not first(head):
                            dve.wait_ge(stored[0], 16 * head)
                        if b == 2:
                            dve.wait_ge(out_free, h)
                        V.tensor_scalar(oT[:, b * 512:b * 512 + 512], M[:], gain[:], None, ALU.mult).then_inc(out_ready, 1)
                    for t, k in due(s, TILE, TURN_Q, turns):
                        dve.wait_ge(m_done, 2 * (QT * (h - k) + t) + 2)
                        V.tensor_copy(qT[:, t % QRING, 2:4].rearrange("p a t -> p (a t)"), M[:, 0:2 * P]).then_inc(q_free, 1)
                    for i, k in due(s, last_of, SUM, turns):
                        b, n, head = i % TRING, NK[i], h - k
                        dve.wait_ge(exp_done, SCORES * head + 2 * before[i + 1])
                        if n > 1:
                            dve.wait_ge(al_ready, RESCALED[QT] * head + RESCALED[i] + 1)
                            link(V.tensor_tensor(la[:, :, 0:n], ls[:, b, :, 0:n], al[:, :, 0:n], ALU.mult))
                            link(V.reduce_sum(rl[:], la[:, :, 0:n], axis=AX))
                            link(V.reciprocal(rl[:], rl[:]))
                            link(V.tensor_tensor(rl[:, 1:2], rl[:, 1:2], nlam[:], ALU.mult))
                            V.tensor_tensor(coef[:, b, :, 0:n], al[:, :, 0:n], rl[:].rearrange("p (c o) -> p c o", o=1).broadcast_to([P, 2, n]),
                                            ALU.mult).then_inc(coef_ready, 1)
                        else:
                            link(V.reciprocal(coef[:, b, :, 0:1], ls[:, b, :, 0:1]))
                            V.tensor_tensor(coef[:, b, 1, 0:1], coef[:, b, 1, 0:1], nlam[:], ALU.mult).then_inc(coef_ready, 1)
                    for i, k in due(s, last_of, 0, turns):
                        b, n = i % TRING, NK[i]
                        if n > 1:
                            link(V.reduce_max(top[:], m[:, b, :, 0:n], axis=AX))
                            V.tensor_tensor(dm[:, :, 0:n], m[:, b, :, 0:n], top[:].rearrange("p (c o) -> p c o", o=1).broadcast_to([P, 2, n]),
                                            ALU.subtract).then_inc(dm_ready, 1)
                    for half, k in due(s, SCALE, 0, turns):
                        part = slice(8 * half, 8 * half + 8)
                        dve.wait_ge(std_ready, 2 * (h - k) + half + 1)
                        link(V.reciprocal(ors[:, part], ors[:, part]))
                        V.tensor_tensor(o[:, part], o[:, part], ors[:, part].rearrange("p (t o) -> p t o", o=1).broadcast_to([P, 8, P]), ALU.mult).then_inc(on_ready, 1)
                wanted = LINKS if 1 in turns and 0 in turns else LINKS - LATE if 0 in turns else LATE if 1 in turns else 0
                assert link.n == wanted, (link.n, wanted)

            heads(dve, turn)

        @block.tensor
        def _(pe):
            pe.wait_ge(setup, 2)

            def turn(h, turns):
                used = (q_free, QT * h) if 1 in turns else None
                for s in range(CHUNKS):
                    for j, k in due(s, CHUNK, SCORE, turns):
                        head, i = h - k, tile_of[j]
                        kc = j - before[i]
                        n = size(i, kc)
                        if kc == 0:
                            pe.wait_ge(q_free, QT * head + i + 1)
                        if j >= 2 or not first(head):
                            pe.wait_ge(exp_done, SCORES * head + 2 * (j - 1))
                        diagonal = kc == NK[i] - 1
                        for c in range(2):
                            for a in range(2):
                                ins = nc.tensor.matmul(S[j % 2][:, c, 0:n], qT[:, i % QRING, 2 * c + a], kT[:, c, kc * 512:kc * 512 + n],
                                                       start=a == 0, stop=a == 1 and not diagonal)
                            if diagonal:
                                ins = nc.tensor.matmul(S[j % 2][:, c, n - P:n], ident_r[:], mask[:], start=False, stop=True)
                        ins.then_inc(s_done, 1)
                    for t, k in due(s, TILE, TURN_Q, turns):
                        pe.wait_ge(k_free, QT * (h - k) + t + 1)
                        for a in range(2):
                            ins = nc.tensor.transpose(M[:, a * P:a * P + P], qin[:, t % QRING, 1, a].bitcast(F32).rearrange("p a d -> p (a d)"), ident[:])
                        ins.then_inc(m_done, 1)
                        used = (q_free, QT * (h - k) + t + 1)
                    for g, k in due(s, CHUNK, ADD, turns):
                        head, i = h - k, tile_of[g]
                        pe.wait_ge(w_ready, CHUNKS * head + g + 1)
                        if g >= 2 or not first(head):
                            pe.wait_ge(wt_lo, CHUNKS * head + g - 1)
                        for t in range(size(i, g - before[i]) // P):
                            ins = nc.tensor.transpose(WT[g % 2][:, t * P:t * P + P], w[:, g % 2, t * P:t * P + P], ident[:])
                        ins.then_inc(wt_done, 1)
                    for g, k in due(s, CHUNK, VAL, turns):
                        head, i = h - k, tile_of[g]
                        kc = g - before[i]
                        pe.wait_ge(wt_lo, CHUNKS * head + g + 1)
                        if kc == NK[i] - 1:
                            pe.wait_ge(v_lo, QT * head + i + 1)
                        if kc == 0 and (i or not first(head)):
                            pe.wait_ge(o_ready, QT * head + i)
                        for t in range(size(i, kc) // P):
                            x = kc * 4 + t
                            nc.tensor.matmul(O[:, 0:2 * P], wT[:, g % 2, 0, t * P:t * P + P], vv[:, x].rearrange("p a e -> p (a e)"),
                                             start=x == 0, stop=False)
                            ins = nc.tensor.matmul(O[:, 0:P], wT[:, g % 2, 1, t * P:t * P + P], vv[:, x, 0], start=False, stop=x == i)
                        ins.then_inc(pv_done, 1)
                    for t, k in due(s, TILE, TURN_K, turns):
                        pe.wait_ge(split, QT * (h - k) + t + 1)
                        if used:
                            pe.wait_ge(*used)
                        for c in range(2):
                            nc.tensor.transpose(M[:, c * P:c * P + P], kin[:, t % QRING, c].bitcast(F32).rearrange("p a d -> p (a d)"), ident[:])
                        for a in range(2):
                            ins = nc.tensor.transpose(M[:, (2 + a) * P:(3 + a) * P], qin[:, t % QRING, 0, a].bitcast(F32).rearrange("p a d -> p (a d)"), ident[:])
                        ins.then_inc(m_done, 1)
                    for b, k in due(s, TURN_O, 0, turns):
                        if b % 2 == 0:
                            pe.wait_ge(on_ready, 2 * (h - k) + b // 2 + 1)
                        pe.wait_ge(*used)
                        for t in range(4):
                            ins = nc.tensor.transpose(M[:, t * P:t * P + P], o[:, 4 * b + t], ident[:])
                        ins.then_inc(o_turned, 1)
                        used = (out_ready, 4 * (h - k) + b + 1)

            heads(pe, turn)


def attend_sample(nc, io, sems, table, kp, k_in):
    ctx = ExitStack()
    sb = lambda name, shape, dt=F32: ctx.enter_context(nc.sbuf_tensor(name, shape, dt))
    sem = lambda name: sems.enter_context(nc.semaphore(name))
    W = HEADS * P
    R = NS * COMP
    RH = NS * HEADS
    CONSTS = 10 + NS
    with ctx:
        vp = sb("d_v", [P, NS, PAGES, W])
        qb = sb("d_q", [P, NS, W])
        prod = sb("d_prod", [P, 2, PAGES, W])
        sc = sb("d_scores", [P, PAGES, R])
        ident = sb("d_ident", [P, P])
        sel = sb("d_sel", [R, 2])
        lam_in = sb("d_lam_in", [P, 4, HD])
        lam_t = sb("d_lam_t", [P, 2, HD])
        lam_s = sb("d_lam_s", [P, 4])
        nlam = sb("d_nlam", [P, 1])
        gain = sb("d_gain", [P, 1])
        eps = sb("d_eps", [P, 1])
        q64 = sb("d_q64", [R, HD])
        k64 = sb("d_k64", [R, HD])
        v32 = sb("d_v32", [RH, P])
        own = sb("d_own", [R, 1])
        pp = sb("d_p", [R, PAGES * PAGE])
        st = sb("d_st", [R, 8])
        cp = sb("d_cp", [P, PAGES * R])
        wz = sb("d_wz", [P, NS, PAGES, RH])
        pair = sb("d_pair", [R, RH])
        head = sb("d_head", [RH, HEADS])
        wo = sb("d_wo", [RH, 1])
        mine = sb("d_mine", [RH, HEADS, P])
        o = sb("d_o", [RH, P])
        osq = sb("d_osq", [RH, P])
        ss = sb("d_ss", [RH, 1])
        ors = sb("d_ors", [RH, 1])
        res = sb("d_res", [P, HEADS, NS])
        ST = ctx.enter_context(nc.psum_tensor("d_ST", [P, 512], F32))
        PT = ctx.enter_context(nc.psum_tensor("d_PT", [P, 512], F32))
        OT = ctx.enter_context(nc.psum_tensor("d_OT", [P, 512], F32))
        WB = ctx.enter_context(nc.psum_tensor("d_WB", [P, 512], F32))
        RT = ctx.enter_context(nc.psum_tensor("d_RT", [P, 512], F32))
        consts_in = sem("d_consts_in")
        v_in = [sem(f"d_v_in{b}") for b in range(NS // 2)]
        prod_ready = sem("d_products")
        prod_used = sem("d_products_summed")
        chain = sem("d_dve_chain")
        to_act = sem("d_to_act")
        from_act = sem("d_from_act")
        to_pe = sem("d_to_pe")
        from_pe = sem("d_from_pe")
        res_ready = sem("d_res_ready")
        stored = sem("d_stored")
        rows = [io["q"][SEQ:SEQ + NS], io["k_sample"].rearrange("l b s h e -> (l b s) (h e)"),
                io["v_sample"].rearrange("l b s h e -> (l b s) (h e)")]
        cv = io["cache_v"].rearrange("l n t h e -> (l n) t (h e)")
        block = ctx.enter_context(nc.Block())

        @block.sync
        def _(sp):
            for b in range(NS):
                sp.dma_start(qb[:, b], rows[0][b:b + 1].broadcast_to([P, W])).then_inc(consts_in, 16)
            load_pages(sp, table, cv, vp, range(0, NS, 2), v_in)
            sp.wait_ge(res_ready, 1)
            for h in range(HEADS):
                sp.dma_start(io["mixT"][LRU + h * P:LRU + h * P + P, SEQ:SEQ + NS], res[:, h]).then_inc(stored, 16)
            sp.wait_ge(stored, 16 * HEADS)

        @block.gpsimd
        def _(pool):
            pool.wait_ge(consts_in, 16 * CONSTS)
            for b in range(1, NS, 2):
                pool.wait_ge(k_in[b // 2], 2 * 16 * PAGES)
                if b >= 3:
                    pool.wait_ge(prod_used, b // 2)
                nc.gpsimd.tensor_tensor(prod[:, b % 2], kp[:, b], qb[:, b:b + 1].broadcast_to([P, PAGES, W]), ALU.mult).then_inc(prod_ready, 1)

        @block.scalar
        def _(act):
            A = nc.scalar
            act.dma_start(ident[:], io["ident"]).then_inc(consts_in, 16)
            act.dma_start(sel[:], io["sel"]).then_inc(consts_in, 16)
            for n, name in enumerate(("lambda_q1", "lambda_k1", "lambda_q2", "lambda_k2")):
                act.dma_start(lam_in[:, n], io[name].broadcast_to([P, HD])).then_inc(consts_in, 16)
            act.dma_start(gain[:], io["subln_g"].rearrange("l (e o) -> (l e) o", o=1)).then_inc(consts_in, 16)
            act.dma_start(q64[:], rows[0].rearrange("b (c d) -> (b c) d", d=HD)).then_inc(consts_in, 16)
            act.dma_start(k64[:], rows[1].rearrange("b (c d) -> (b c) d", d=HD)).then_inc(consts_in, 16)
            act.dma_start(v32[:], rows[2].rearrange("b (h e) -> (b h) e", e=P)).then_inc(consts_in, 16)
            load_pages(act, table, cv, vp, range(1, NS, 2), v_in)
            act.wait_ge(to_act, 1)
            A.activation(lam_s[:, 2:4], lam_s[:, 0:2], ACT.Exp).then_inc(from_act, 1)
            act.wait_ge(to_act, 2)
            A.activation(pp[:], ST[0:R], ACT.Exp, bias=st[:, 1:2], scale=QSCALE, accum_out=st[:, 2:3])
            A.activation(st[:, 3:4], own[:], ACT.Exp, bias=st[:, 1:2], scale=QSCALE).then_inc(from_act, 1)
            act.wait_ge(from_pe, 2)
            A.activation(cp[:], PT[:, 0:PAGES * R], ACT.Copy).then_inc(from_act, 1)
            act.wait_ge(to_act, 3)
            A.activation(ors[:], ss[:], ACT.Sqrt, bias=eps[0:RH], scale=1.0 / P).then_inc(from_act, 1)

        @block.vector
        def _(dve):
            V = nc.vector
            link = Chain(dve, chain)
            V.memset(wz[:], 0.0)
            link(V.memset(eps[:], EPS_SUBLN))
            dve.wait_ge(consts_in, 16 * CONSTS)
            link(V.tensor_tensor(lam_t[:], lam_in[:, 0:4:2], lam_in[:, 1:4:2], ALU.mult))
            V.reduce_sum(lam_s[:, 0:2], lam_t[:], axis=AX).then_inc(to_act, 1)
            for b in range(NS):
                if b % 2 == 0:
                    dve.wait_ge(k_in[b // 2], 2 * 16 * PAGES)
                    link(V.tensor_tensor(prod[:, b % 2], kp[:, b], qb[:, b:b + 1].broadcast_to([P, PAGES, W]), ALU.mult))
                else:
                    dve.wait_ge(prod_ready, b // 2 + 1)
                ins = V.reduce_sum(sc[:, :, b * COMP:(b + 1) * COMP], prod[:, b % 2].rearrange("p n (c d) -> p n c d", d=HD), axis=AX)
                if b % 2 == 0:
                    link(ins)
                elif b < NS - 2:
                    ins.then_inc(prod_used, 1)
            ins.then_inc(to_pe, 1)
            dve.wait_ge(from_act, 1)
            link(V.tensor_tensor(nlam[:], lam_s[:, 3:4], lam_s[:, 2:3], ALU.subtract))
            link(V.tensor_scalar(nlam[:], nlam[:], -LAM_INIT, None, ALU.add))
            link(V.tensor_scalar(gain[:], gain[:], 1.0 - LAM_INIT, None, ALU.mult))
            V.reduce_sum(pair[:], ident[0:R, 0:R].rearrange("p (r c) -> p r c", c=2), axis=AX)
            V.reduce_sum(head[:], ident[0:RH, 0:RH].rearrange("p (b h) -> p h b", h=HEADS), axis=AX)
            link(V.scalar_tensor_tensor(st[:, 5:6], sel[:, 1:2], nlam[0:R], sel[:, 0:1], ALU.mult, ALU.add))
            link(V.tensor_tensor(q64[:], q64[:], k64[:], ALU.mult))
            link(V.reduce_sum(own[:], q64[:], axis=AX))
            dve.wait_ge(from_pe, 1)
            link(V.reduce_max(st[:, 0:1], ST[0:R], axis=AX))
            link(V.tensor_tensor(st[:, 0:1], st[:, 0:1], own[:], ALU.max))
            V.tensor_scalar(st[:, 1:2], st[:, 0:1], -QSCALE, None, ALU.mult).then_inc(to_act, 1)
            dve.wait_ge(from_act, 2)
            link(V.tensor_tensor(st[:, 4:5], st[:, 2:3], st[:, 3:4], ALU.add))
            link(V.reciprocal(st[:, 4:5], st[:, 4:5]))
            link(V.tensor_tensor(st[:, 4:5], st[:, 4:5], st[:, 5:6], ALU.mult))
            V.tensor_scalar(pp[:], pp[:], st[:, 4:5], None, ALU.mult)
            V.tensor_tensor(st[:, 6:7], st[:, 3:4], st[:, 4:5], ALU.mult).then_inc(to_pe, 1)
            dve.wait_ge(from_act, 3)
            c4 = cp[:].rearrange("p (n r c) -> p n r c", n=PAGES, c=2)
            for b in range(NS):
                r = slice(b * HEADS, (b + 1) * HEADS)
                ins = V.tensor_tensor(wz[:, b, :, r], c4[:, :, r, 0], c4[:, :, r, 1], ALU.add)
            ins.then_inc(to_pe, 1)
            dve.wait_ge(from_pe, 2)
            link(V.tensor_copy(wo[:], WB[0:RH, 0:1]))
            dve.wait_ge(from_pe, 3)
            link(V.tensor_tensor(mine[:], OT[0:RH].rearrange("p (h e) -> p h e", h=HEADS),
                                 head[:].rearrange("p (h o) -> p h o", o=1).broadcast_to([RH, HEADS, P]), ALU.mult))
            link(V.reduce_sum(o[:], mine[:].rearrange("p h e -> p e h"), axis=AX))
            link(V.scalar_tensor_tensor(o[:], v32[:], wo[:], o[:], ALU.mult, ALU.add))
            link(V.tensor_tensor(osq[:], o[:], o[:], ALU.mult))
            V.reduce_sum(ss[:], osq[:], axis=AX).then_inc(to_act, 1)
            dve.wait_ge(from_act, 4)
            link(V.reciprocal(ors[:], ors[:]))
            V.tensor_scalar(o[:], o[:], ors[:], None, ALU.mult).then_inc(to_pe, 1)
            dve.wait_ge(from_pe, 4)
            V.tensor_scalar(res[:].rearrange("p h b -> p b h"), RT[:, 0:RH].rearrange("p (b h) -> p b h", h=HEADS), gain[:], None, ALU.mult).then_inc(res_ready, 1)

        @block.tensor
        def _(pe):
            T = nc.tensor
            pe.wait_ge(consts_in, 16 * CONSTS)
            pe.wait_ge(to_pe, 1)
            for n in range(PAGES):
                ins = T.transpose(ST[0:R, n * PAGE:(n + 1) * PAGE], sc[:, n], ident[:])
            ins.then_inc(from_pe, 1)
            pe.wait_ge(to_pe, 2)
            for n in range(PAGES):
                T.transpose(PT[:, n * R:(n + 1) * R], pp[:, n * PAGE:(n + 1) * PAGE], ident[0:R, 0:R])
            T.matmul(WB[0:RH, 0:1], pair[:], st[:, 6:7], start=True, stop=True).then_inc(from_pe, 1)
            pe.wait_ge(to_pe, 3)
            for b in range(NS):
                pe.wait_ge(v_in[b // 2], 2 * 16 * PAGES)
                for n in range(PAGES):
                    ins = T.matmul(OT[0:RH], wz[:, b, n], vp[:, b, n], start=b == 0 and n == 0, stop=b == NS - 1 and n == PAGES - 1)
            ins.then_inc(from_pe, 1)
            pe.wait_ge(to_pe, 4)
            T.transpose(RT[:, 0:RH], o[:], ident[0:RH, 0:RH]).then_inc(from_pe, 1)


def mix_and_feed(nc, io, sems, pool_turn):
    ctx = ExitStack()
    sem = lambda name: sems.enter_context(nc.semaphore(name))
    CH, RING, RAW, AHEAD = 42, 3, 2, 2
    UP0, DOWN0, PROJ, GATE0 = 4, 26, 37, 38
    MIXED = DOWN0 + 5
    HALVES = (slice(0, KD // 2), slice(KD // 2, KD))
    FJOBS = FB
    with ctx:
        base = nc.sbuf_base
        base += -base % 64
        top = [base]

        def sb(name, shape, dt=F32, at=None):
            n = int(np.prod(shape[1:])) * (2 if dt == mybir.dt.bfloat16 else 4)
            if at is None:
                at, top[0] = top[0], top[0] + n + -n % 32
            return nc.alloc_sbuf_tensor_at(name, shape, dt, offset=at)

        w = sb("c_w", [P, RING, 2, 2048], F32R)
        raw = sb("c_raw", [P, RAW, 2048])
        h_at = top[0]
        hT = sb("c_hT", [P, 2, KD, WIDE], F32R)
        f_at = top[0]
        fT = sb("c_fT", [P, FB, 2, WIDE], F32R)
        x2T = sb("c_x2T", [P, 2, KD, WIDE], F32R, at=f_at)
        hn = sb("c_hn", [P, 2, D], at=f_at)
        at = f_at + 2 * KD * WIDE * 4
        mix = sb("c_mix", [P, KD, WIDE], at=at)
        at += KD * WIDE * 4
        x1 = sb("c_x1", [P, TILES + 1, D], at=at)
        x2 = sb("c_x2", [P, TILES + 1, D], at=at)
        at += (TILES + 1) * D * 4
        mo = sb("c_mo", [P, TILES + 1, D], at=at)
        pr = sb("c_pr", [P, TILES + 1, D], at=at)
        assert at + (TILES + 1) * D * 4 <= top[0]
        fo = sb("c_fo", [P, TILES + 1, D], at=h_at)
        pT = sb("c_pT", [P, 2, 2, WIDE], F32R)
        xr = sb("c_xr", [P, 2, D])
        gains = sb("c_gains", [P, 2, D])
        act1 = sb("c_act1", [P, 2, WIDE])
        junk_at = top[0]
        junk = sb("c_junk", [P, D], mybir.dt.bfloat16)
        fs = sb("c_fs", [P, 2, P], at=junk_at)
        pin = sb("c_pin", [P, 2, PLE])
        ident = sb("c_ident", [P, P])
        eps = sb("c_eps", [P, 1])
        ss = sb("c_ss", [P, 4, TILES + 1])
        rs = sb("c_rs", [P, 4, TILES + 1])
        assert top[0] <= nc.sbuf_usable_end, (top[0], nc.sbuf_usable_end)
        banks = [ctx.enter_context(nc.psum_tensor(f"c_bank{n}", [P, 512], F32)) for n in range(8)]
        ACC = banks[0:5]
        TB = banks[5:7]
        PB = banks[7]
        SPB = (TB[0], PB)
        consts_in = sem("c_consts_in")
        ready0 = sem("c_eps_written")
        raw_in = [sem(f"c_raw_in{n}") for n in range(RAW)]
        w_hi = sem("c_w_hi")
        w_ready = sem("c_w_ready")
        w_used = sem("c_w_used")
        mix_in = [sem(f"c_mix_in{n}") for n in range(2)]
        mix_hi = sem("c_mix_hi")
        mix_ready = sem("c_mix_ready")
        xr_in = [sem(f"c_xr_in{n}") for n in range(2)]
        gain_in = [sem(f"c_gain_in{n}") for n in range(2)]
        p_in = [sem(f"c_p_in{n}") for n in range(2)]
        acc_done = sem("c_acc_done")
        acc_free = sem("c_acc_free")
        std = [sem(f"c_std{n}") for n in range(4)]
        act_chain = sem("c_act_chain")
        dve_chain = sem("c_dve_chain")
        mo_ready = sem("c_mo_ready")
        x1_ready = sem("c_x1_ready")
        x1_out = sem("c_x1_out")
        hn_ready = sem("c_hn_ready")
        tp_done = sem("c_transposed")
        t_hi = sem("c_T_hi")
        t_lo = sem("c_T_lo")
        pair_done = sem("c_gate_up_done")
        silu_done = sem("c_silu")
        f_ready = sem("c_f")
        f_hi = sem("c_f_hi")
        f_lo = sem("c_f_lo")
        spair_done = sem("c_sample_gate_up_done")
        ssilu_done = sem("c_sample_silu")
        sf_ready = sem("c_sample_f")
        sft_done = sem("c_sample_f_transposed")
        fo_ready = sem("c_fo_ready")
        x2_ready = sem("c_x2_ready")
        pt_done = sem("c_p_transposed")
        pt_hi = sem("c_pT_hi")
        pt_lo = sem("c_pT_lo")
        proj_done = sem("c_proj_done")
        proj_free = sem("c_proj_free")
        sig_ready = sem("c_sigmoid")
        v_ready = sem("c_v_ready")
        y_ready = sem("c_y_ready")
        y_out = sem("c_y_out")

        rows = lambda name: io[name][0].rearrange("(k p) n -> p k n", p=P)
        wo, wg, wu, wd, wp, wpg = (rows(n) for n in ("w_out", "ffn_w_gate", "ffn_w_up", "ffn_w_down", "ple_w_proj", "ple_w_gate"))

        def chunk(c):
            if c < UP0:
                return [(wo[:, c % 2 * 4:c % 2 * 4 + 4, c // 2 * 512:c // 2 * 512 + 512], lambda v: v.rearrange("p (k n) -> p k n", n=512))]
            if c < DOWN0:
                b = c - UP0
                return [(s[:, :, b * P:b * P + P], lambda v, n=n: v[:, n * 1024:n * 1024 + 1024].rearrange("p (k n) -> p k n", n=P)) for n, s in enumerate((wg, wu))]
            if c < MIXED:
                return [(wd[:, 4 * (c - DOWN0):4 * (c - DOWN0) + 4, 0:512], lambda v: v.rearrange("p (k n) -> p k n", n=512))]
            if c == MIXED:
                return [(wd[:, 20:22, n * 512:n * 512 + 512], lambda v, n=n: v[:, n * 1024:n * 1024 + 1024].rearrange("p (k n) -> p k n", n=512)) for n in range(2)]
            if c < PROJ:
                b = 4 * (c - MIXED - 1)
                return [(wd[:, b:b + 4, 512:1024], lambda v: v.rearrange("p (k n) -> p k n", n=512))]
            if c == PROJ:
                return [(wp, lambda v: v.rearrange("p (k n) -> p k n", n=1024))]
            g = c - GATE0
            return [(wpg[:, g % 2 * 4:g % 2 * 4 + 4, g // 2 * 512:g // 2 * 512 + 512], lambda v: v.rearrange("p (k n) -> p k n", n=512))]

        DMAS = [len(chunk(c)) for c in range(CH)]

        def arrived(i, c):
            return 16 * (sum(DMAS[c % RAW::RAW]) * i + sum(DMAS[c % RAW:c + 1:RAW]))

        ACCS = 6 * TILES

        def acc_job(i, last, phase, d, t):
            n = TILES + 1 if last else TILES
            return ACCS * i + n * (2 * phase + d) + t + 1

        x_v = io["x_prompt"].rearrange("b (g t p) d -> (b g) t p d", g=GROUPS, p=P)
        y_v = io["y_prompt"].rearrange("b (g t p) d -> (b g) t p d", g=GROUPS, p=P)
        x1_v = io["x1"][0:SEQ].rearrange("(g t p) d -> g t p d", g=GROUPS, p=P)
        p_v = io["p_prompt"].rearrange("l b (g t p) e -> (l b g) t p e", g=GROUPS, p=P)
        mix_v = io["mixT"].rearrange("(k p) t -> p k t", p=P)

        def tile_of(view, sample, i, t):
            return sample if t == TILES else view[i, t]

        x_s = io["x_sample"].rearrange("b s d -> (b s) d")
        y_s = io["y_sample"].rearrange("b s d -> (b s) d")
        p_s = io["p_sample"].rearrange("l b s e -> (l b s) e")
        x1_s = io["x1"][SEQ:SEQ + NS]
        GAINS = ("norm_post_mix", "norm_pre_ffn", "norm_post_ffn", "ple_norm")
        PRJ = (PB, banks[4])
        T_PER = 4 * TILES

        def chunk_used(eng, i, c, last):
            if c < 0:
                if isinstance(i, int) and i == 0:
                    return
                i, c, last = i - 1, c + CH, False
            if c in ENDS:
                phase, d = ENDS[c]
                eng.wait_ge(acc_done, acc_job(i, last, phase, d, TILES if last else TILES - 1))
            elif UP0 <= c < DOWN0:
                eng.wait_ge(pair_done, 2 * FJOBS * i + 2 * (c - UP0) + 2)
                if last:
                    eng.wait_ge(spair_done, c - UP0 + 1)
            elif c == PROJ:
                eng.wait_ge(proj_done, 2 * TILES * i + 2 * (TILES + 1 if last else TILES))
            else:
                eng.wait_ge(w_used, len(PLAIN) * i + PLAIN.index(c) + 1)

        ENDS = {1: (0, 0), 3: (0, 1), PROJ - 1: (1, 1), GATE0 + 1: (2, 0), GATE0 + 3: (2, 1)}
        PLAIN = [c for c in range(CH) if c not in ENDS and not UP0 <= c < DOWN0 and c != PROJ]

        block = ctx.enter_context(nc.Block())

        @block.sync
        def _(sp):
            def load(c):
                for src, place in chunk(c):
                    sp.dma_start(place(raw[:, c % RAW]), src).then_inc(raw_in[c % RAW], 16)

            for half in range(2):
                load(half)
                sp.dma_start(mix[:, HALVES[half], 0:GROUP], mix_v[:, HALVES[half], 0:GROUP]).then_inc(mix_in[half], 16)
            sp.dma_start(ident[:], io["ident"]).then_inc(consts_in, 16)

            def group(i, last):
                for c in range(AHEAD, CH):
                    sp.wait_ge(w_ready, CH * i + c - RAW + 1)
                    load(c)
                if not last:
                    sp.wait_ge(acc_done, acc_job(i, last, 1, 1, TILES - 1))
                    for half in range(2):
                        sp.dma_start(mix[:, HALVES[half], 0:GROUP], mix_v[:, HALVES[half], bass.ts(i + 1, GROUP)]).then_inc(mix_in[half], 16)
                    for c in range(AHEAD):
                        sp.wait_ge(w_ready, CH * i + CH + c - RAW + 1)
                        load(c)

            group(0, False)
            with sp.Fori(1, GROUPS - 1) as i:
                group(i, False)
            sp.wait_ge(mix_in[0], 16 * GROUPS)
            sp.dma_start(mix[:, :, GROUP:], mix_v[:, :, SEQ:]).then_inc(mix_in[0], 16)
            group(GROUPS - 1, True)

        @block.gpsimd
        def _(pool):
            def load(dst, src, arrived):
                pool.sem_inc(pool_turn, 1)
                pool.dma_start(dst, src).then_inc(arrived, 16)

            def load_gain(n):
                load(gains[:, n % 2], io[GAINS[n]].broadcast_to([P, D]), gain_in[n % 2])

            def group(i, last):
                tiles = group_tiles(last)

                def load_rows(t, n, view, sample):
                    load(xr[0:n, t % 2], tile_of(view, sample, i, t), xr_in[t % 2])

                wait_if_any(pool, y_ready, TILES * i)
                for n in range(2):
                    load_gain(n)
                for t, _, n in tiles[0:2]:
                    load_rows(t, n, x_v, x_s)
                for t, _, n in tiles:
                    pool.wait_ge(x1_ready, TILES * i + t + 1)
                    load(tile_of(x1_v, x1_s, i, t), x1[0:n, t], x1_out)
                    if t + 2 < len(tiles):
                        load_rows(t + 2, tiles[t + 2][2], x_v, x_s)
                pool.wait_ge(hn_ready, TILES * i + len(tiles))
                for n in range(2, 4):
                    load_gain(n)
                pool.wait_ge(x1_out, 16 * (TILES * i + len(tiles)))
                for t, _, n in tiles[0:2]:
                    load_rows(t, n, x1_v, x1_s)
                for t, _, n in tiles:
                    if t >= 2:
                        pool.wait_ge(pt_done, TILES * i + t - 1)
                    load(pin[0:n, t % 2], tile_of(p_v, p_s, i, t), p_in[t % 2])
                for t, _, n in tiles[2:]:
                    pool.wait_ge(x2_ready, TILES * i + t - 1)
                    load_rows(t, n, x1_v, x1_s)
                for t, _, n in tiles:
                    pool.wait_ge(y_ready, TILES * i + t + 1)
                    load(tile_of(y_v, y_s, i, t), x2[0:n, t], y_out)

            group(0, False)
            with pool.Fori(1, GROUPS - 1) as i:
                group(i, False)
            group(GROUPS - 1, True)
            pool.wait_ge(y_out, 16 * (TILES * GROUPS + 1))
            pool.wait_ge(x1_out, 16 * (TILES * GROUPS + 1))

        @block.scalar
        def _(act):
            A = nc.scalar
            NORMS = 4 * TILES

            def split(i, c, last):
                act.wait_ge(raw_in[c % RAW], arrived(i, c))
                chunk_used(act, i, c - RING, last)
                A.activation(w[:, c % RING, 0], raw[:, c % RAW], ACT.Copy).then_inc(w_hi, 1)

            def norm(i, link, k, t, n, ready, src):
                act.wait_ge(ready, TILES * i + t + 1)
                link(A.activation(junk[0:n], src[0:n, t], ACT.Square, accum_out=ss[0:n, k, t:t + 1]))
                A.activation(rs[0:n, k, t:t + 1], ss[0:n, k, t:t + 1], ACT.Sqrt, bias=eps[0:n], scale=1.0 / D).then_inc(std[k], 1)

            def hi_halves(i, last, phase, t, col, n, dst):
                for half in range(2):
                    act.wait_ge(tp_done, T_PER * i + 2 * len(group_tiles(last)) * phase + 2 * t + half + 1)
                    A.activation(dst[:, 0, 4 * half:4 * half + 4, col:col + n], TB[half][:, 0:4 * n].rearrange("p (k t) -> p k t", k=4), ACT.Copy).then_inc(t_hi, 1)

            act.wait_ge(ready0, 1)

            def mix_split(n, half):
                act.wait_ge(mix_in[half], 16 * n)
                A.activation(hT[:, 0, HALVES[half], 0:GROUP], mix[:, HALVES[half], 0:GROUP], ACT.Copy).then_inc(mix_hi, 1)

            for half in range(2):
                act.wait_ge(raw_in[half], 16)
                A.activation(w[:, half, 0], raw[:, half], ACT.Copy).then_inc(w_hi, 1)
                mix_split(1, half)

            def group(i, last):
                tiles = group_tiles(last)
                link = Chain(act, act_chain, NORMS * i)
                if last:
                    act.wait_ge(mix_in[0], 16 * (GROUPS + 1))
                    A.activation(hT[:, 0, :, GROUP:], mix[:, :, GROUP:], ACT.Copy).then_inc(mix_hi, 1)
                for c in range(CH):
                    if c + AHEAD < CH:
                        split(i, c + AHEAD, last)
                    elif not last:
                        split(i + 1, c + AHEAD - CH, False)
                    if c == 3:
                        for s in range(len(tiles) + 3):
                            if s < len(tiles):
                                norm(i, link, 0, *tiles[s][::2], mo_ready, mo)
                            if s >= 3:
                                hi_halves(i, last, 0, *tiles[s - 3], hT)
                            if 1 <= s <= len(tiles):
                                norm(i, link, 1, *tiles[s - 1][::2], x1_ready, x1)
                    if UP0 <= c < DOWN0:
                        b = c - UP0
                        act.wait_ge(pair_done, 2 * FJOBS * i + 2 * b + 1)
                        wait_if_any(act, f_lo, FJOBS * i + max(b - 1, 0))
                        A.activation(act1[:, b % 2, 0:GROUP], ACC[b % 2 * 2][:], ACT.Silu).then_inc(silu_done, 1)
                        if last:
                            act.wait_ge(spair_done, b + 1)
                            if b >= 2:
                                act.wait_ge(sft_done, b - 1)
                            A.activation(fs[0:NS, b % 2], SPB[b % 2][0:NS, 0:P], ACT.Silu).then_inc(ssilu_done, 1)
                        act.wait_ge(f_ready, FJOBS * i + b + 1)
                        if b == 0:
                            act.wait_ge(x1_out, 16 * (TILES * i + len(tiles)))
                        A.activation(fT[:, b, 0, 0:GROUP], act1[:, b % 2, 0:GROUP], ACT.Copy).then_inc(f_hi, 1)
                    if last and c == DOWN0:
                        act.wait_ge(sft_done, FB)
                        A.activation(fT[:, :, 0, GROUP:], TB[1][:, 0:FB * NS].rearrange("p (b t) -> p b t", b=FB), ACT.Copy).then_inc(f_hi, 1)
                    if not last and c == GATE0 + 2:
                        act.wait_ge(x2_ready, TILES * (i + 1))
                        for half in range(2):
                            mix_split(i + 2, half)
                    if c == MIXED + 1:
                        for t, col, n in tiles:
                            act.wait_ge(pt_done, TILES * i + t + 1)
                            A.activation(pT[:, 0, :, col:col + n], PB[:, 0:2 * n].rearrange("p (k t) -> p k t", k=2), ACT.Copy).then_inc(pt_hi, 1)
                    if c == PROJ:
                        for s in range(len(tiles) + 3):
                            if s < len(tiles):
                                norm(i, link, 2, *tiles[s][::2], fo_ready, fo)
                                t, _, n = tiles[s]
                                for d in range(2):
                                    act.wait_ge(proj_done, 2 * TILES * i + 2 * t + d + 1)
                                    A.activation(pr[0:n, t, d * 512:d * 512 + 512], PRJ[d][0:n], ACT.Copy).then_inc(proj_free, 1)
                            if s >= 3:
                                hi_halves(i, last, 1, *tiles[s - 3], x2T)
                    if c in (GATE0 + 1, GATE0 + 3):
                        d = (c - GATE0) // 2
                        for t, _, n in tiles:
                            act.wait_ge(acc_done, acc_job(i, last, 2, d, t))
                            wait_if_any(act, v_ready, 2 * TILES * i + max(len(tiles) * d + t - 1, 0))
                            A.activation(act1[0:n, (len(tiles) * d + t) % 2, 0:512], ACC[t][0:n], ACT.Sigmoid).then_inc(sig_ready, 1)
                for t, _, n in tiles:
                    act.wait_ge(v_ready, 2 * TILES * i + len(tiles) + t + 1)
                    link(A.activation(junk[0:n], pr[0:n, t], ACT.Square, accum_out=ss[0:n, 3, t:t + 1]))
                    A.activation(rs[0:n, 3, t:t + 1], ss[0:n, 3, t:t + 1], ACT.Sqrt, bias=eps[0:n], scale=1.0 / D).then_inc(std[3], 1)

            group(0, False)
            with act.Fori(1, GROUPS - 1) as i:
                group(i, False)
            group(GROUPS - 1, True)

        @block.vector
        def _(dve):
            V = nc.vector
            V.memset(eps[:], EPS).then_inc(ready0, 1)

            def split_lo(n, c):
                dve.wait_ge(w_hi, n)
                V.tensor_tensor(w[:, c % RING, 1], raw[:, c % RAW], w[:, c % RING, 0].bitcast(F32), ALU.subtract).then_inc(w_ready, 1)

            def mix_lo(n, rows, cols):
                dve.wait_ge(mix_hi, n)
                V.tensor_tensor(hT[:, 1, rows, cols], mix[:, rows, cols], hT[:, 0, rows, cols].bitcast(F32), ALU.subtract).then_inc(mix_ready, 1)

            for half in range(2):
                split_lo(half + 1, half)
                mix_lo(half + 1, HALVES[half], slice(0, GROUP))

            def group(i, last, link):
                tiles = group_tiles(last)
                if last:
                    mix_lo(2 * GROUPS + 1, slice(0, KD), slice(GROUP, WIDE))

                def copies(phase, d, dst):
                    for t, _, n in tiles:
                        dve.wait_ge(acc_done, acc_job(i, last, phase, d, t))
                        V.tensor_copy(dst[0:n, t, d * 512:d * 512 + 512], ACC[t][0:n]).then_inc(acc_free, 1)

                def scaled(k, t, n, src, dst):
                    dve.wait_ge(std[k], TILES * i + t + 1)
                    link(V.reciprocal(rs[0:n, k, t:t + 1], rs[0:n, k, t:t + 1]))
                    if t == 0:
                        dve.wait_ge(gain_in[k % 2], 16 * (2 * i + k // 2 + 1))
                    return V.scalar_tensor_tensor(dst, src, rs[0:n, k, t:t + 1], gains[0:n, k % 2], ALU.mult, ALU.mult)

                def lo_halves(phase, t, col, n, dst):
                    for half in range(2):
                        dve.wait_ge(t_hi, T_PER * i + 2 * len(tiles) * phase + 2 * t + half + 1)
                        to = dst[:, :, 4 * half:4 * half + 4, col:col + n]
                        V.tensor_tensor(to[:, 1], TB[half][:, 0:4 * n].rearrange("p (k t) -> p k t", k=4), to[:, 0].bitcast(F32), ALU.subtract).then_inc(t_lo, 1)

                for c in range(CH):
                    if c + AHEAD < CH or not last:
                        split_lo(CH * i + c + AHEAD + 1, (c + AHEAD) % CH)
                    if c == 1:
                        wait_if_any(dve, y_ready, TILES * i)
                        copies(0, 0, mo)
                    if c == 3:
                        for s in range(len(tiles) + 3):
                            if s < len(tiles):
                                t, _, n = tiles[s]
                                dve.wait_ge(acc_done, acc_job(i, last, 0, 1, t))
                                link(V.tensor_copy(mo[0:n, t, 512:], ACC[t][0:n]))
                                V.nop().then_inc(mo_ready, 1)
                            if 1 <= s <= len(tiles):
                                t, _, n = tiles[s - 1]
                                if t == 0:
                                    wait_if_any(dve, y_out, 16 * TILES * i)
                                link(scaled(0, t, n, mo[0:n, t], mo[0:n, t]))
                                dve.wait_ge(xr_in[t % 2], XR * i + 16 * (t // 2 + 1))
                                V.tensor_tensor(x1[0:n, t], mo[0:n, t], xr[0:n, t % 2], ALU.add).then_inc(x1_ready, 1)
                            if s >= 3:
                                t, col, n = tiles[s - 3]
                                lo_halves(0, t, col, n, hT)
                            if 2 <= s < len(tiles) + 2:
                                t, col, n = tiles[s - 2]
                                if t >= 2:
                                    dve.wait_ge(tp_done, T_PER * i + 2 * (t - 1))
                                scaled(1, t, n, x1[0:n, t], hn[0:n, t % 2]).then_inc(hn_ready, 1)
                    if UP0 <= c < DOWN0:
                        b = c - UP0
                        dve.wait_ge(pair_done, 2 * FJOBS * i + 2 * b + 2)
                        dve.wait_ge(silu_done, FJOBS * i + b + 1)
                        V.tensor_tensor(act1[:, b % 2, 0:GROUP], act1[:, b % 2, 0:GROUP], ACC[b % 2 * 2 + 1][:], ALU.mult).then_inc(f_ready, 1)
                        if last:
                            dve.wait_ge(ssilu_done, b + 1)
                            V.tensor_tensor(fs[0:NS, b % 2], fs[0:NS, b % 2], SPB[b % 2][0:NS, P:2 * P], ALU.mult).then_inc(sf_ready, 1)
                        dve.wait_ge(f_hi, FJOBS * i + b + 1)
                        V.tensor_tensor(fT[:, b, 1, 0:GROUP], act1[:, b % 2, 0:GROUP], fT[:, b, 0, 0:GROUP].bitcast(F32), ALU.subtract).then_inc(f_lo, 1)
                    if last and c == DOWN0:
                        dve.wait_ge(f_hi, FJOBS * GROUPS + 1)
                        V.tensor_tensor(fT[:, :, 1, GROUP:], TB[1][:, 0:FB * NS].rearrange("p (b t) -> p b t", b=FB),
                                        fT[:, :, 0, GROUP:].bitcast(F32), ALU.subtract).then_inc(f_lo, 1)
                    if not last and c == GATE0 + 2:
                        for half in range(2):
                            mix_lo(2 * (i + 1) + half + 1, HALVES[half], slice(0, GROUP))
                    if c == MIXED:
                        for t, _, n in tiles:
                            dve.wait_ge(acc_done, acc_job(i, last, 1, 0, t))
                            V.tensor_copy(fo[0:n, t, 0:512], ACC[t][0:n]).then_inc(acc_free, 1)
                    if c == MIXED + 1:
                        for t, col, n in tiles:
                            dve.wait_ge(pt_hi, TILES * i + t + 1)
                            V.tensor_tensor(pT[:, 1, :, col:col + n], PB[:, 0:2 * n].rearrange("p (k t) -> p k t", k=2),
                                            pT[:, 0, :, col:col + n].bitcast(F32), ALU.subtract).then_inc(pt_lo, 1)
                    if c == PROJ - 1:
                        for t, _, n in tiles:
                            dve.wait_ge(acc_done, acc_job(i, last, 1, 1, t))
                            link(V.tensor_copy(fo[0:n, t, 512:], ACC[t][0:n]))
                            V.nop().then_inc(fo_ready, 1)
                    if c == PROJ:
                        for s in range(len(tiles) + 3):
                            if s < len(tiles):
                                t, _, n = tiles[s]
                                link(scaled(2, t, n, fo[0:n, t], fo[0:n, t]))
                                if t < 2:
                                    dve.wait_ge(xr_in[t % 2], XR * i + 16 * (len(tiles[t::2]) + 1))
                                else:
                                    dve.wait_ge(xr_in[t % 2], XR * i + 16 * (len(tiles[t % 2::2]) + t // 2 + 1))
                                V.tensor_tensor(x2[0:n, t], fo[0:n, t], xr[0:n, t % 2], ALU.add).then_inc(x2_ready, 1)
                            if s >= 3:
                                t, col, n = tiles[s - 3]
                                lo_halves(1, t, col, n, x2T)
                    if c in (GATE0 + 1, GATE0 + 3):
                        d = (c - GATE0) // 2
                        for t, _, n in tiles:
                            j = len(tiles) * d + t
                            dve.wait_ge(sig_ready, 2 * TILES * i + j + 1)
                            if d == 0:
                                dve.wait_ge(proj_free, 2 * TILES * i + 2 * t + 2)
                            half = pr[0:n, t, d * 512:d * 512 + 512]
                            V.tensor_tensor(half, half, act1[0:n, j % 2, 0:512], ALU.mult).then_inc(v_ready, 1)
                for t, _, n in tiles:
                    link(scaled(3, t, n, pr[0:n, t], pr[0:n, t]))
                    V.tensor_tensor(x2[0:n, t], pr[0:n, t], x2[0:n, t], ALU.add).then_inc(y_ready, 1)

            XR = 64
            LINKS = 9 * TILES
            group(0, False, Chain(dve, dve_chain))
            with dve.Fori(1, GROUPS - 1) as i:
                link = Chain(dve, dve_chain, LINKS * i)
                group(i, False, link)
                assert link.n == LINKS, (link.n, LINKS)
            group(GROUPS - 1, True, Chain(dve, dve_chain, LINKS * (GROUPS - 1)))

        @block.tensor
        def _(pe):
            pe.wait_ge(consts_in, 16)

            def products(out, blocks, lhs, rhs, first=True, end=True):
                for k in range(blocks):
                    for n, (a, b) in enumerate(PRODUCTS):
                        ins = nc.tensor.matmul(out, lhs(k, a), rhs(k, b), start=first and k == 0 and n == 0,
                                               stop=end and k == blocks - 1 and n == 2)
                return ins

            def group(i, last):
                tiles = group_tiles(last)
                per = len(tiles)

                def transposes(phase, t, n, ready, src, slot):
                    pe.wait_ge(ready, TILES * i + t + 1)
                    for half in range(2):
                        wait_if_any(pe, t_lo, T_PER * i + max(2 * per * phase + 2 * t + half - 1, 0))
                        for k in range(4):
                            kk = 4 * half + k
                            ins = nc.tensor.transpose(TB[half][:, k * n:k * n + n], src[0:n, slot, kk * P:kk * P + P], ident[0:n, 0:n])
                        ins.then_inc(tp_done, 1)

                def accumulate(phase, d, blocks, lhs, rhs, first, end, plain):
                    for t, col, n in tiles:
                        if t == TILES and first and phase == 0 and d == 0:
                            pe.wait_ge(mix_ready, 2 * GROUPS + 1)
                        if t == TILES and first and phase == 1 and d == 0:
                            sample_transpose(FB - 1)
                            pe.wait_ge(f_lo, FJOBS * GROUPS + 1)
                        if first and (t < TILES or phase or d):
                            wait_if_any(pe, acc_free_of(phase, d, t)[0], acc_free_of(phase, d, t)[1])
                        if first and phase == 2 and d == 0:
                            pe.wait_ge(t_lo, T_PER * i + 2 * per + 2 * t + 2)
                        ins = products(ACC[t][0:n], blocks, lambda k, a: lhs(k, a)[:, col:col + n], rhs, first, end)
                        if end:
                            ins.then_inc(acc_done, 1)
                        if first and phase == 2 and d == 0 and t + 2 < per:
                            transposes(1, t + 2, tiles[t + 2][2], x2_ready, x2, t + 2)
                    if not end and plain:
                        ins.then_inc(w_used, 1)

                def acc_free_of(phase, d, t):
                    if phase == 0 and d == 0:
                        return sig_ready, 2 * TILES * i
                    if phase == 0:
                        return acc_free, 2 * TILES * i + t + 1
                    if phase == 1 and d == 0:
                        return (f_ready, FJOBS * i + FB - 1 + t // 2) if t < 4 else (mo_ready, TILES * i + per)
                    if phase == 1:
                        return acc_free, 2 * TILES * i + per + t + 1
                    if d == 0:
                        return (fo_ready, TILES * i + t + 1) if t < 4 else (proj_free, 2 * TILES * i + 2 * per)
                    return sig_ready, 2 * TILES * i + t + 1

                def weights_of(b):
                    return w[:, (UP0 + b) % RING].rearrange("p a (g k n) -> p a g k n", g=2, n=P)

                def gate_up(b, cols):
                    wb = weights_of(b)
                    for g in range(2):
                        yield products(ACC[b % 2 * 2 + g][:, cols], KD, lambda k, a: wb[:, a, g, k], lambda k, r: hT[:, r, k, cols])

                def sample_transpose(b):
                    pe.wait_ge(sf_ready, b + 1)
                    nc.tensor.transpose(TB[1][:, b * NS:b * NS + NS], fs[0:NS, b % 2], ident[0:NS, 0:NS]).then_inc(sft_done, 1)

                for c in range(CH):
                    pe.wait_ge(w_ready, CH * i + c + 1)
                    wv = w[:, c % RING].rearrange("p a (k n) -> p a k n", n=512)
                    if c < UP0:
                        kh = 4 * (c % 2)
                        if c < 2:
                            pe.wait_ge(mix_ready, 2 * i + c + 1)
                        accumulate(0, c // 2, 4, lambda k, a: hT[:, a, kh + k], lambda k, b: wv[:, b, k], c % 2 == 0, c % 2 == 1, True)
                    if c == UP0 - 1:
                        for t, _, n in tiles:
                            transposes(0, t, n, hn_ready, hn, t % 2)
                            if t in (1, 2):
                                b = t - 1
                                pe.wait_ge(w_ready, CH * i + UP0 + b + 1)
                                pe.wait_ge(t_lo, T_PER * i + 4)
                                pe.wait_ge(mo_ready, TILES * i + per)
                                list(gate_up(b, slice(0, 2 * P)))
                        pe.wait_ge(t_lo, T_PER * i + 2 * per)
                    if UP0 <= c < DOWN0:
                        b = c - UP0
                        if b >= 2:
                            pe.wait_ge(f_ready, FJOBS * i + b - 1)
                        for ins in gate_up(b, slice(0 if b >= 2 else 2 * P, GROUP)):
                            ins.then_inc(pair_done, 1)
                        wb = weights_of(b)
                        if last:
                            if b >= 2:
                                pe.wait_ge(sf_ready, b - 1)
                            elif b == 1:
                                wait_if_any(pe, proj_free, 2 * TILES * i)
                            products(SPB[b % 2][0:NS, 0:2 * P], KD, lambda k, r: hT[:, r, k, GROUP:],
                                     lambda k, a: wb[:, a, :, k]).then_inc(spair_done, 1)
                            if b:
                                sample_transpose(b - 1)
                    if DOWN0 <= c < MIXED:
                        pe.wait_ge(f_lo, FJOBS * i + 4 * (c - DOWN0) + 4)
                    if c == MIXED:
                        pe.wait_ge(f_lo, FJOBS * (i + 1))
                    if DOWN0 <= c < MIXED:
                        kb = 4 * (c - DOWN0)
                        accumulate(1, 0, 4, lambda k, a: fT[:, kb + k, a], lambda k, b: wv[:, b, k], c == DOWN0, False, True)
                    if c == MIXED:
                        accumulate(1, 0, 2, lambda k, a: fT[:, 20 + k, a], lambda k, b: wv[:, b, k], False, True, False)
                        accumulate(1, 1, 2, lambda k, a: fT[:, 20 + k, a], lambda k, b: wv[:, b, 2 + k], True, False, True)
                    if MIXED < c < PROJ:
                        kb = 4 * (c - MIXED - 1)
                        accumulate(1, 1, 4, lambda k, a: fT[:, kb + k, a], lambda k, b: wv[:, b, k], False, c == PROJ - 1, True)
                    if c == MIXED + 1:
                        for t, _, n in tiles:
                            pe.wait_ge(p_in[t % 2], 16 * (2 * i + t // 2 + 1))
                            wait_if_any(pe, pt_lo, TILES * i + t)
                            wait_if_any(pe, proj_free, 2 * TILES * i)
                            for k in range(2):
                                ins = nc.tensor.transpose(PB[:, k * n:k * n + n], pin[0:n, t % 2, k * P:k * P + P], ident[0:n, 0:n])
                            ins.then_inc(pt_done, 1)
                    if c == PROJ:
                        pe.wait_ge(pt_lo, TILES * i + per)
                        if last:
                            pe.wait_ge(fo_ready, TILES * i + per)
                        wq = w[:, c % RING].rearrange("p a (k d n) -> p a k d n", k=2, d=2)
                        for t, col, n in tiles:
                            for d in range(2):
                                wait_if_any(pe, proj_free, 2 * TILES * i + max(2 * t + d - 1, 0))
                                products(PRJ[d][0:n], 2, lambda k, a: pT[:, a, k, col:col + n], lambda k, b: wq[:, b, k, d]).then_inc(proj_done, 1)
                        for t, _, n in tiles[0:2]:
                            transposes(1, t, n, x2_ready, x2, t)
                    if c >= GATE0:
                        g = c - GATE0
                        kh = 4 * (g % 2)
                        accumulate(2, g // 2, 4, lambda k, a: x2T[:, a, kh + k], lambda k, b: wv[:, b, k], g % 2 == 0, g % 2 == 1, True)

            group(0, False)
            with pe.Fori(1, GROUPS - 1) as i:
                group(i, False)
            group(GROUPS - 1, True)


def build(nc, io):
    with ExitStack() as sems:
        pool_turn = sems.enter_context(nc.semaphore("pool_turn"))
        project(nc, io, sems, pool_turn)
        with nc.sbuf_tensor("page_table", [1, NS * PAGES], I32) as table, \
                nc.sbuf_tensor("k_pages", [P, NS, PAGES, HEADS * P], F32) as k_pages:
            k_in = [sems.enter_context(nc.semaphore(f"k_pages_in{b}")) for b in range(NS // 2)]
            attend_prompt(nc, io, sems, pool_turn, table, k_pages, k_in)
            attend_sample(nc, io, sems, table, k_pages, k_in)
        mix_and_feed(nc, io, sems, pool_turn)


_INS = ["x_prompt", "x_sample", "cache_k", "cache_v", "state_conv", "state_h", "page_table", "p_prompt", "p_sample",
        "norm_pre_mix", "w_in", "conv_w", "conv_b", "lru_w_a", "lru_b_a", "lru_w_x", "lru_b_x", "lru_L",
        "lambda_q1", "lambda_k1", "lambda_q2", "lambda_k2", "subln_g", "w_out", "norm_post_mix",
        "norm_pre_ffn", "ffn_w_gate", "ffn_w_up", "ffn_w_down", "norm_post_ffn",
        "ple_w_gate", "ple_w_proj", "ple_norm"]
_OUTS = [("y_prompt", (1, SEQ, D)), ("y_sample", (NS, 1, D)),
         ("k_prompt", (1, 1, SEQ, HEADS, P)), ("v_prompt", (1, 1, SEQ, HEADS, P)),
         ("conv_prompt", (1, 1, TAPS - 1, LRU)), ("h_prompt", (1, 1, LRU)),
         ("k_sample", (1, NS, 1, HEADS, P)), ("v_sample", (1, NS, 1, HEADS, P)),
         ("conv_sample", (1, NS, TAPS - 1, LRU)), ("h_sample", (1, NS, LRU))]
_SCRATCH = [("q", (SEQ + NS, LRU)), ("mixT", (D, SEQ + NS)), ("x1", (SEQ + NS, D))]


def _constants():
    inv = np.float32(500000.0) ** (-np.arange(0, ROT, 2, dtype=np.float32) / np.float32(ROT))
    positions = np.concatenate([np.arange(SEQ), np.full(NS, PAGES * PAGE)]).astype(np.float32)
    angle = positions[:, None] * inv[None, :]
    key, query = np.arange(P)[None, :], np.arange(P)[:, None]
    return {
        "rope": np.stack([np.cos(angle), np.sin(angle)], 1).astype(np.float32),
        "ident": np.eye(P, dtype=np.float32),
        "mask": np.where(key > query, np.float32(-1e30), np.float32(0.0)).astype(np.float32),
        "sel": np.tile(np.eye(2, dtype=np.float32), (NS * HEADS, 1)),
    }


def kernel(**inputs):
    import concourse.bacc as _bacc
    from concourse.bass_utils import run_bass_kernel_spmd as _run

    nc = _bacc.Bacc("TRN2", target_bir_lowering=False, num_devices=1, dynamic_dma_scratch_size=4096)
    arrays, io = {}, {}
    for name, a in [(n, inputs[n]) for n in _INS] + list(_constants().items()):
        a = np.ascontiguousarray(a)
        arrays[f"in_{name}"] = a
        io[name] = nc.dram_tensor(f"in_{name}", a.shape, mybir.dt.from_np(a.dtype), kind="ExternalInput").ap()
    for name, shape in _OUTS:
        io[name] = nc.dram_tensor(f"out_{name}", shape, F32, kind="ExternalOutput").ap()
    for name, shape in _SCRATCH:
        io[name] = nc.dram_tensor(f"scratch_{name}", shape, F32, kind="Internal").ap()
    build(nc, io)
    r = _run(nc, [arrays], core_ids=[0])
    return tuple(r.results[0][f"out_{name}"] for name, _ in _OUTS)
```
